# Optimizing a Trainium2 kernel written in Bass

```python
import math
import jax
import jax.numpy as jnp
from jax import lax
import numpy as np

D_MODEL = 1024
BATCH = 1
SEQ = 128
DEPTH = 2
DEC_BATCH = 1
DEC_SEQ = 1024
PAST_LEN = 128

GRID_W = 64
CHUNK = 64
Q_BLOCK = 128
CONV_W = 3
EPS = 1e-6
GDN_HEADS = 4
GDN_DK = 128
GDN_DV = 128
GDN_WIDTH = GDN_HEADS * GDN_DV
N_HEADS = 8
KV_HEADS = 2
HEAD_DIM = 64
GROUP = N_HEADS // KV_HEADS
ATTN_WIDTH = N_HEADS * HEAD_DIM
KV_WIDTH = KV_HEADS * HEAD_DIM
ATTN_SCALE = HEAD_DIM ** -0.5
ROT_AXIS = HEAD_DIM // 2
ROPE_BASE = 10000.0
SSM_HEADS = 16
SSM_HEAD_DIM = 64
D_INNER = SSM_HEADS * SSM_HEAD_DIM
SSM_GROUPS = 2
SSM_STATE = 128
SSM_XBC = D_INNER + 2 * SSM_GROUPS * SSM_STATE
IN_SPLITS = (3 * GDN_WIDTH, GDN_WIDTH, 2 * GDN_HEADS, 2 * GDN_HEADS,
             ATTN_WIDTH, KV_WIDTH, KV_WIDTH, ATTN_WIDTH,
             SSM_XBC, D_INNER, 2 * SSM_HEADS,
             3 * D_MODEL)
IN_WIDTH = sum(IN_SPLITS)

kernel_name = 'hybrid_gdn_gqa_ssd_prefix_dit_step'

def split_cols(a, widths):
    out, start = [], 0
    for w in widths:
        out.append(a[..., start:start + w])
        start += w
    return out

def rev(a):
    return jnp.flip(a, axis=1)

def rms_norm(x, w):
    xf = x.astype(jnp.float32)
    y = xf * lax.rsqrt(jnp.mean(xf * xf, axis=-1, keepdims=True) + EPS)
    return (y * w.astype(jnp.float32)).astype(x.dtype)

def l2_normalize(x):
    xf = x.astype(jnp.float32)
    return (xf * lax.rsqrt(jnp.sum(xf * xf, axis=-1, keepdims=True) + EPS)).astype(x.dtype)

def centred_dwconv(x, w):
    ch = x.shape[-1]
    return lax.conv_general_dilated(
        x, w[:, None, :].astype(x.dtype), window_strides=(1,),
        padding=[(CONV_W // 2, CONV_W // 2)],
        dimension_numbers=('NWC', 'WIO', 'NWC'), feature_group_count=ch)

def axial_rope(x):
    t = x.shape[1]
    rows = t // GRID_W
    row = jnp.repeat(jnp.arange(rows), GRID_W)
    col = jnp.tile(jnp.arange(GRID_W), rows)
    freqs = ROPE_BASE ** (-jnp.arange(ROT_AXIS // 2, dtype=jnp.float32) / (ROT_AXIS // 2))

    def rotate(xa, pos):
        ang = pos.astype(jnp.float32)[:, None] * freqs
        cos = jnp.cos(ang)[None, :, None, :]
        sin = jnp.sin(ang)[None, :, None, :]
        x1, x2 = jnp.split(xa.astype(jnp.float32), 2, axis=-1)
        return jnp.concatenate([x1 * cos - x2 * sin, x2 * cos + x1 * sin], axis=-1)

    out = jnp.concatenate([rotate(x[..., :ROT_AXIS], row), rotate(x[..., ROT_AXIS:], col)], axis=-1)
    return out.astype(x.dtype)

def blocked_attention(q, k, v):
    b, t = q.shape[:2]
    nb = t // Q_BLOCK
    qb = jnp.moveaxis(q.reshape(b, nb, Q_BLOCK, KV_HEADS, GROUP, HEAD_DIM), 1, 0)

    def attend(q_blk):
        s = jnp.einsum('bqkgd,bskd->bkgqs', q_blk, k).astype(jnp.float32) * ATTN_SCALE
        p = jax.nn.softmax(s, axis=-1).astype(v.dtype)
        return jnp.einsum('bkgqs,bskd->bqkgd', p, v)

    o = lax.map(attend, qb)
    return jnp.moveaxis(o, 0, 1).reshape(b, t, ATTN_WIDTH)

def gdn_scan(q, k, v, g, beta, s0):
    out_dtype = v.dtype
    q, k, v, g, beta = (a.astype(jnp.float32) for a in (q, k, v, g, beta))
    b, t, h, dk = k.shape
    dv = v.shape[-1]
    n = t // CHUNK

    def blocks(a):
        a = a.reshape(b, n, CHUNK, h, *a.shape[3:])
        return jnp.moveaxis(a, (1, 2), (0, 3))

    qc, kc, vc, gc, bc = (blocks(a) for a in (q, k, v, g, beta))
    gcum = jnp.cumsum(gc, axis=-1)
    lower = jnp.tril(jnp.ones((CHUNK, CHUNK), dtype=bool))
    strict = jnp.tril(jnp.ones((CHUNK, CHUNK), dtype=bool), -1)
    decay = jnp.exp(jnp.where(lower, gcum[..., :, None] - gcum[..., None, :], -jnp.inf))
    kb = kc * bc[..., None]
    a_mat = jnp.where(strict, jnp.einsum('nbhid,nbhjd->nbhij', kb, kc) * decay, 0.0) \
        + jnp.eye(CHUNK, dtype=jnp.float32)
    rhs = jnp.concatenate([vc * bc[..., None], kb * jnp.exp(gcum)[..., None]], axis=-1)
    sol = lax.linalg.triangular_solve(a_mat, rhs, left_side=True, lower=True)
    u, w = sol[..., :dv], sol[..., dv:]
    intra = jnp.einsum('nbhid,nbhjd->nbhij', qc, kc) * decay
    q_dec = qc * jnp.exp(gcum)[..., None]
    k_dec = kc * jnp.exp(gcum[..., -1:] - gcum)[..., None]
    g_last = jnp.exp(gcum[..., -1])

    def step(S, xs):
        q_i, k_i, u_i, w_i, a_i, gl = xs
        v_new = u_i - jnp.einsum('bhcd,bhde->bhce', w_i, S)
        o = jnp.einsum('bhcd,bhde->bhce', q_i, S) + jnp.einsum('bhij,bhje->bhie', a_i, v_new)
        S = S * gl[..., None, None] + jnp.einsum('bhcd,bhce->bhde', k_i, v_new)
        return S, o

    s_fin, o = lax.scan(step, s0.astype(jnp.float32), (q_dec, k_dec, u, w, intra, g_last))
    o = jnp.moveaxis(o, (0, 3), (1, 2)).reshape(b, t, h, dv)
    return o.astype(out_dtype), s_fin

def ssd_scan(x, a, bm, cm, s0):
    out_dtype = x.dtype
    x, a, bm, cm = (z.astype(jnp.float32) for z in (x, a, bm, cm))
    b, t, h, p = x.shape
    g = bm.shape[2]
    r = h // g
    nc = t // CHUNK
    xc = x.reshape(b, nc, CHUNK, g, r, p)
    bc = bm.reshape(b, nc, CHUNK, g, SSM_STATE)
    cc = cm.reshape(b, nc, CHUNK, g, SSM_STATE)
    ac = jnp.moveaxis(a.reshape(b, nc, CHUNK, g, r), 2, -1)
    acum = jnp.cumsum(ac, axis=-1)
    lower = jnp.tril(jnp.ones((CHUNK, CHUNK), dtype=bool))
    lmat = jnp.exp(jnp.where(lower, acum[..., :, None] - acum[..., None, :], -jnp.inf))
    cb = jnp.einsum('bclgn,bcsgn->bcgls', cc, bc)
    y_diag = jnp.einsum('bcgls,bcgrls,bcsgrp->bclgrp', cb, lmat, xc)
    dstate = jnp.exp(acum[..., -1:] - acum)
    states = jnp.einsum('bclgn,bcgrl,bclgrp->bcgrpn', bc, dstate, xc)
    decay_in = jnp.exp(acum)
    chunk_decay = jnp.exp(acum[..., -1])

    def step(S, xs):
        c_i, st_i, din_i, cd_i = xs
        y_off = jnp.einsum('blgn,bgrpn,bgrl->blgrp', c_i, S, din_i)
        S = S * cd_i[..., None, None] + st_i
        return S, y_off

    xs = tuple(jnp.moveaxis(z, 1, 0) for z in (cc, states, decay_in, chunk_decay))
    s_fin, y_off = lax.scan(step, s0.astype(jnp.float32).reshape(b, g, r, p, SSM_STATE), xs)
    y = y_diag + jnp.moveaxis(y_off, 0, 1)
    return y.reshape(b, t, h, p).astype(out_dtype), s_fin.reshape(b, h, p, SSM_STATE)

def modulation(cond, w_mod, b_mod):
    m = jnp.einsum('...d,de->...e', jax.nn.silu(cond), w_mod) + b_mod
    return split_cols(m, (D_MODEL, D_MODEL, D_MODEL))

def mixer(h, lp, ctx):
    b, t, _ = h.shape
    proj = jnp.einsum('btd,de->bte', h, lp['w_in'])
    (a_qkv, a_z, a_beta, a_alpha, b_q, b_k, b_v, b_z,
     c_xbc, c_z, c_dt, gates) = split_cols(proj, IN_SPLITS)

    a_qkv = jax.nn.silu(centred_dwconv(a_qkv, lp['gdn_conv_w']))
    a_q, a_k, a_v = split_cols(a_qkv, (GDN_WIDTH, GDN_WIDTH, GDN_WIDTH))
    a_q = l2_normalize(a_q.reshape(b, t, GDN_HEADS, GDN_DK)) * (GDN_DK ** -0.5)
    a_k = l2_normalize(a_k.reshape(b, t, GDN_HEADS, GDN_DK))
    a_v = a_v.reshape(b, t, GDN_HEADS, GDN_DV)
    beta = jax.nn.sigmoid(a_beta.reshape(b, t, 2, GDN_HEADS))
    log_decay = -jnp.exp(lp['gdn_a_log']) * jax.nn.softplus(
        a_alpha.reshape(b, t, 2, GDN_HEADS) + lp['gdn_dt_bias'])
    s_gdn0 = jnp.zeros((b, 2, GDN_HEADS, GDN_DK, GDN_DV), jnp.float32) if ctx is None else ctx[2]
    o_f, sg_f = gdn_scan(a_q, a_k, a_v, log_decay[:, :, 0], beta[:, :, 0], s_gdn0[:, 0])
    o_b, sg_b = gdn_scan(rev(a_q), rev(a_k), rev(a_v), rev(log_decay[:, :, 1]),
                         rev(beta[:, :, 1]), s_gdn0[:, 1])
    o_a = rms_norm(o_f + rev(o_b), lp['gdn_norm_w']) * jax.nn.silu(a_z.reshape(b, t, GDN_HEADS, GDN_DV))
    branch_a = jnp.einsum('bte,ed->btd', o_a.reshape(b, t, GDN_WIDTH), lp['w_branch_a'])

    q = rms_norm(b_q.reshape(b, t, N_HEADS, HEAD_DIM), lp['attn_q_norm'])
    k = rms_norm(b_k.reshape(b, t, KV_HEADS, HEAD_DIM), lp['attn_k_norm'])
    v = b_v.reshape(b, t, KV_HEADS, HEAD_DIM)
    if ctx is None:
        keys, vals = k, v
    else:
        q = axial_rope(q)
        keys = jnp.concatenate([axial_rope(k), ctx[0].astype(k.dtype)], axis=1)
        vals = jnp.concatenate([v, ctx[1].astype(v.dtype)], axis=1)
    o_att = blocked_attention(q, keys, vals) * jax.nn.silu(b_z)
    branch_b = jnp.einsum('bte,ed->btd', o_att, lp['w_branch_b'])

    xbc = jax.nn.silu(centred_dwconv(c_xbc, lp['ssm_conv_w']) + lp['ssm_conv_b'])
    c_x, c_b, c_c = split_cols(xbc, (D_INNER, SSM_GROUPS * SSM_STATE, SSM_GROUPS * SSM_STATE))
    c_x = c_x.reshape(b, t, SSM_HEADS, SSM_HEAD_DIM)
    c_b = c_b.reshape(b, t, SSM_GROUPS, SSM_STATE)
    c_c = c_c.reshape(b, t, SSM_GROUPS, SSM_STATE)
    dt = jax.nn.softplus(c_dt.reshape(b, t, 2, SSM_HEADS) + lp['ssm_dt_bias'])
    da = dt * (-jnp.exp(lp['ssm_a_log']))
    s_ssm0 = jnp.zeros((b, 2, SSM_HEADS, SSM_HEAD_DIM, SSM_STATE), jnp.float32) if ctx is None else ctx[3]
    y_f, ss_f = ssd_scan(c_x * dt[:, :, 0, :, None], da[:, :, 0], c_b, c_c, s_ssm0[:, 0])
    y_b, ss_b = ssd_scan(rev(c_x * dt[:, :, 1, :, None]), rev(da[:, :, 1]), rev(c_b), rev(c_c), s_ssm0[:, 1])
    y = y_f + rev(y_b) + lp['ssm_d'][:, None] * c_x
    y = rms_norm(y.reshape(b, t, D_INNER) * jax.nn.silu(c_z), lp['ssm_norm_w'])
    branch_c = jnp.einsum('bte,ed->btd', y, lp['w_branch_c'])

    g_a, g_b, g_c = split_cols(gates, (D_MODEL, D_MODEL, D_MODEL))
    merged = jax.nn.sigmoid(g_a) * branch_a + jax.nn.sigmoid(g_b) * branch_b + jax.nn.sigmoid(g_c) * branch_c
    out = jnp.einsum('btd,de->bte', merged, lp['w_out'])
    ctx_out = None
    if ctx is None:
        ctx_out = (k, v, jnp.stack([sg_f, sg_b], axis=1), jnp.stack([ss_f, ss_b], axis=1))
    return out, ctx_out

def setup_inputs(seed: int = 0) -> dict:
    key = jax.random.key(seed)
    ks = iter(jax.random.split(key, 40))
    nrm = lambda shape, s: jax.random.normal(next(ks), shape, jnp.float32) * s

    def a_log(shape):
        return jnp.log(jax.random.uniform(next(ks), shape, jnp.float32, 1.0, 16.0))

    def dt_bias(shape):
        dt = jnp.exp(jax.random.uniform(next(ks), shape, jnp.float32, math.log(1e-3), math.log(1e-1)))
        return dt + jnp.log(-jnp.expm1(-dt))

    return {
        'x_prompt': nrm((BATCH, SEQ, D_MODEL), 1.0),
        'x_sample': nrm((DEC_BATCH, DEC_SEQ, D_MODEL), 1.0),
        'cache_k': nrm((DEC_BATCH, DEPTH, PAST_LEN, KV_HEADS, HEAD_DIM), 1.0),
        'cache_v': nrm((DEC_BATCH, DEPTH, PAST_LEN, KV_HEADS, HEAD_DIM), 1.0),
        'state_gdn': nrm((DEC_BATCH, DEPTH, 2, GDN_HEADS, GDN_DK, GDN_DV), 0.3),
        'state_ssm': nrm((DEC_BATCH, DEPTH, 2, SSM_HEADS, SSM_HEAD_DIM, SSM_STATE), 0.1),
        'c': nrm((DEC_BATCH, D_MODEL), 1.0),
        'c_ctx': nrm((D_MODEL,), 1.0),
        'norm_w': 1.0 + nrm((DEPTH, D_MODEL), 0.02),
        'w_mod': nrm((DEPTH, D_MODEL, 3 * D_MODEL), 0.5 * D_MODEL ** -0.5),
        'b_mod': nrm((DEPTH, 3 * D_MODEL), 0.02),
        'w_in': nrm((DEPTH, D_MODEL, IN_WIDTH), D_MODEL ** -0.5),
        'gdn_conv_w': nrm((DEPTH, CONV_W, 3 * GDN_WIDTH), CONV_W ** -0.5),
        'gdn_a_log': a_log((DEPTH, 2, GDN_HEADS)),
        'gdn_dt_bias': dt_bias((DEPTH, 2, GDN_HEADS)),
        'gdn_norm_w': 1.0 + nrm((DEPTH, GDN_DV), 0.02),
        'attn_q_norm': 1.0 + nrm((DEPTH, HEAD_DIM), 0.02),
        'attn_k_norm': 1.0 + nrm((DEPTH, HEAD_DIM), 0.02),
        'ssm_conv_w': nrm((DEPTH, CONV_W, SSM_XBC), CONV_W ** -0.5),
        'ssm_conv_b': nrm((DEPTH, SSM_XBC), 0.02),
        'ssm_a_log': a_log((DEPTH, 2, SSM_HEADS)),
        'ssm_dt_bias': dt_bias((DEPTH, 2, SSM_HEADS)),
        'ssm_d': 1.0 + nrm((DEPTH, SSM_HEADS), 0.1),
        'ssm_norm_w': 1.0 + nrm((DEPTH, D_INNER), 0.02),
        'w_branch_a': nrm((DEPTH, GDN_WIDTH, D_MODEL), GDN_WIDTH ** -0.5),
        'w_branch_b': nrm((DEPTH, ATTN_WIDTH, D_MODEL), ATTN_WIDTH ** -0.5),
        'w_branch_c': nrm((DEPTH, D_INNER, D_MODEL), D_INNER ** -0.5),
        'w_out': nrm((DEPTH, D_MODEL, D_MODEL), D_MODEL ** -0.5),
        'final_norm_w': 1.0 + nrm((D_MODEL,), 0.02),
    }

def reference(x_prompt, x_sample, cache_k, cache_v, state_gdn, state_ssm, c, c_ctx,
              norm_w, w_mod, b_mod, w_in, gdn_conv_w, gdn_a_log, gdn_dt_bias, gdn_norm_w,
              attn_q_norm, attn_k_norm, ssm_conv_w, ssm_conv_b, ssm_a_log, ssm_dt_bias,
              ssm_d, ssm_norm_w, w_branch_a, w_branch_b, w_branch_c, w_out, final_norm_w):
    xp = x_prompt
    xs = x_sample
    new_k, new_v, new_gdn, new_ssm = [], [], [], []
    for l in range(DEPTH):
        lp = {
            'w_in': w_in[l], 'gdn_conv_w': gdn_conv_w[l], 'gdn_a_log': gdn_a_log[l],
            'gdn_dt_bias': gdn_dt_bias[l], 'gdn_norm_w': gdn_norm_w[l],
            'attn_q_norm': attn_q_norm[l], 'attn_k_norm': attn_k_norm[l],
            'ssm_conv_w': ssm_conv_w[l], 'ssm_conv_b': ssm_conv_b[l], 'ssm_a_log': ssm_a_log[l],
            'ssm_dt_bias': ssm_dt_bias[l], 'ssm_d': ssm_d[l], 'ssm_norm_w': ssm_norm_w[l],
            'w_branch_a': w_branch_a[l], 'w_branch_b': w_branch_b[l], 'w_branch_c': w_branch_c[l],
            'w_out': w_out[l],
        }
        shift, scale, gate = modulation(c_ctx, w_mod[l], b_mod[l])
        h = rms_norm(xp, norm_w[l]) * (1.0 + scale) + shift
        out, (k_c, v_c, s_g, s_s) = mixer(h, lp, None)
        xp = xp + gate * out
        new_k.append(k_c)
        new_v.append(v_c)
        new_gdn.append(s_g)
        new_ssm.append(s_s)
        shift, scale, gate = modulation(c, w_mod[l], b_mod[l])
        h = rms_norm(xs, norm_w[l]) * (1.0 + scale[:, None, :]) + shift[:, None, :]
        out, _ = mixer(h, lp, (cache_k[:, l], cache_v[:, l], state_gdn[:, l], state_ssm[:, l]))
        xs = xs + gate[:, None, :] * out
    y_prompt = rms_norm(xp, final_norm_w)
    y_sample = rms_norm(xs, final_norm_w)
    new_cache_k = jnp.stack(new_k, axis=1)
    new_cache_v = jnp.stack(new_v, axis=1)
    new_state_gdn = jnp.stack(new_gdn, axis=1)
    new_state_ssm = jnp.stack(new_ssm, axis=1)
    return (y_prompt, y_sample, new_cache_k, new_cache_v, new_state_gdn, new_state_ssm)


_drawn_inputs = setup_inputs


def setup_inputs(seed=0):
    import zlib

    import numpy as np

    out = dict(_drawn_inputs(seed))
    spreads = {}
    factors = {'cache_k': 8.0,
     'cache_v': 8.0,
     'state_gdn': 2.907,
     'state_ssm': 3.209,
     'gdn_norm_w': 8.0,
     'attn_q_norm': 8.0,
     'attn_k_norm': 2.909,
     'ssm_d': 4.317,
     'ssm_norm_w': 8.0,
     'final_norm_w': 2.73}
    for name, (base, spread) in spreads.items():
        noise = np.random.default_rng([zlib.crc32(name.encode()), seed]).standard_normal(out[name].shape)
        drawn = base * np.exp(spread * noise) if base else spread * noise
        out[name] = jnp.asarray(drawn.astype(out[name].dtype))
    for name, factor in factors.items():
        out[name] = (out[name] * factor).astype(out[name].dtype)
    return out
```

```python
from contextlib import ExitStack

import numpy as np

import concourse.bass as bass
from concourse import mybir

ALU = mybir.AluOpType
ACT = mybir.ActivationFunctionType
F32 = mybir.dt.float32
F32R = mybir.dt.float32r
AX_X = mybir.AxisListType.X

P = 128
DEPTH = 2
D_MODEL = 1024
KT = D_MODEL // P
SAMPLE = 1024
PROMPT = 128
T = SAMPLE + PROMPT
NT = T // P
NS = SAMPLE // P
EPS = 1e-6
GH, GD = 4, 128
AH, KVH, AD = 8, 2, 64
SH, SP_, SG, SN = 16, 64, 2, 128
PAST = 128
IN_WIDTH = 9008
GW = 256
CHUNKS = ((0, 512), (512, 1024), (1024, 1152))

PROJ_RUNS = (
    ("conv_gdn", 3, 0, 0),
    ("silu", 1, 1536, 12),
    ("plain", 1, 2064, 16),
    ("kv_small", 1, 2576, 20),
    ("silu", 1, 2832, 22),
    ("conv_ssm", 3, 3344, 26),
    ("silu", 2, 4880, 38),
    ("tanh", 6, 5936, 46),
)
BETA_COL, DT_COL = 2048, 5904
NB_PROJ = 70
B_GDN, B_ZA, B_ATT, B_ZB, B_XBC, B_ZC, B_GATE = 0, 12, 16, 22, 26, 38, 46
G_PROJ, G_SSM, G_GDN, G_ATT, G_OUT, NG = 0, 36, 40, 44, 48, 52

V_NORM, V_BMOD, V_GCONV, V_SCONV, V_SBIAS, V_SNORM, V_GNORM, NV = 0, 8, 32, 68, 104, 116, 124, 125

LEVELS = (1, 2, 4, 8, 16, 32, 64)
C_ID, C_TRI, C_STRICT, C_ONE, C_LV = 0, 1, 3, 5, 6
NC_ = 6 + 2 * len(LEVELS)
NPH = 16


def constants():
    i = np.arange(P)
    t = np.zeros((P, NC_, P), np.float32)
    t[:, C_ID] = np.eye(P)
    t[:, C_TRI] = i[:, None] <= i[None, :]
    t[:, C_TRI + 1] = i[:, None] >= i[None, :]
    t[:, C_STRICT] = i[:, None] > i[None, :]
    t[:, C_STRICT + 1] = i[:, None] < i[None, :]
    t[:, C_ONE] = 1.0
    for n, b in enumerate(LEVELS):
        r, c = i[:, None] // b, i[None, :] // b
        t[:, C_LV + n] = -1.0 * ((r % 2 == 1) & (c == r - 1))
        t[:, C_LV + len(LEVELS) + n] = t[:, C_LV + n].T
    rot = AD // 2
    freqs = 10000.0 ** (-np.arange(rot // 2, dtype=np.float32) / (rot // 2))
    pos = np.arange(SAMPLE)
    cs = np.zeros((T, 2, 2, 2, rot // 2), np.float32)
    cs[:, 0] = 1.0
    for axis, x in enumerate((pos // 64, pos % 64)):
        ang = x.astype(np.float32)[:, None] * freqs.astype(np.float32)
        cs[:SAMPLE, 0, axis, 0] = cs[:SAMPLE, 0, axis, 1] = np.cos(ang)
        cs[:SAMPLE, 1, axis, 0] = -np.sin(ang)
        cs[:SAMPLE, 1, axis, 1] = np.sin(ang)
    cs = cs.reshape(NT, P, 2 * AD).transpose(1, 0, 2)
    return t.reshape(P, NC_ * P), np.ascontiguousarray(cs).reshape(P, NT * 2 * AD)


def over(ap, n):
    return ap.unsqueeze(2).broadcast_to([ap.shape[0], ap.shape[1], n])


def again(ap, n):
    return ap.unsqueeze(1).broadcast_to([ap.shape[0], n, ap.shape[1]])


def backbone_kernel(nc, A, O, table, rope_table):
    with ExitStack() as ctx:
        sem_of = {}

        def sem(name):
            if name not in sem_of:
                sem_of[name] = ctx.enter_context(nc.semaphore(name))
            return sem_of[name]

        def dram(name, shape):
            return nc.dram_tensor(name, shape, F32, kind="Internal").ap()

        x_d = dram("x_d", [KT, P, T])
        proj_d = dram("proj_d", [NB_PROJ, P, T])
        ssm_tok_d = dram("ssm_tok_d", [NT, P, 1280])
        gdn_tile_d = dram("gdn_tile_d", [NT, P, 6, 512])

        base = 16512
        top = [base]

        def fixed(name, shape, dt=F32):
            size = int(np.prod(shape[1:])) * 4
            t = nc.alloc_sbuf_tensor_at(name, shape, dt, offset=top[0])
            top[0] += (size + 31) // 32 * 32
            return t

        def region(size):
            start = top[0]
            top[0] += size
            return [start, start, start + size]

        def place(r, name, shape, dt=F32):
            size = (int(np.prod(shape[1:])) * 4 + 31) // 32 * 32
            assert r[1] + size <= r[2], (name, r, size)
            t = nc.alloc_sbuf_tensor_at(name, shape, dt, offset=r[1])
            r[1] += size
            return t

        def fresh(r):
            return [r[0], r[0], r[2]]

        cst = fixed("cst", [P, NC_, P])
        rope = fixed("rope", [P, NT, 2, AD])
        cond = fixed("cond", [P, 24])
        vec = fixed("vec", [P, NV])
        half_vec = fixed("half_vec", [P, NV])
        mod = fixed("mod", [P, 24, 2])
        gain = fixed("gain", [P, KT, 2])
        half_gate = fixed("half_gate", [P, KT, 2])
        rows = fixed("rows", [P, 96])
        coef = fixed("coef", [P, 2, 20])
        qk_gain = fixed("qk_gain", [P, 10, AD])
        beta = fixed("beta", [P, NT, 2, GH])
        dt_ = fixed("dt_", [P, NT, 2, SH])
        logd = fixed("logd", [P, NT, 2, 20])
        cum = fixed("cum", [P, 2, NT, 20])
        tot = fixed("tot", [P, 2, NT, 20])
        e_cum = fixed("e_cum", [P, 2, NT, 20])
        e_tot = fixed("e_tot", [P, 2, NT, 20])
        e_rest = fixed("e_rest", [P, 2, NT, 20])
        neg_be = fixed("neg_be", [P, 2, NT, GH])
        dt_rest = fixed("dt_rest", [P, 2, NT, SH])
        stat = fixed("stat", [P, 32])
        minus_half = fixed("minus_half", [P, 16])
        r_tok = fixed("r_tok", [P, NT])

        ACTV = region(2 * KT * T * 4)
        MRG = region(KT * T * 4)
        WT = region(6 * KT * GW * 4)
        EV = region(229344 - top[0])
        a = fresh(ACTV)
        h_hi = place(a, "h_hi", [P, KT, T], F32R)
        h_lo = place(a, "h_lo", [P, KT, T], F32R)
        a = fresh(ACTV)
        b_hi = place(a, "b_hi", [P, KT, T], F32R)
        b_lo = place(a, "b_lo", [P, KT, T], F32R)
        a = fresh(WT)
        w_raw = [place(a, f"w_raw{n}", [P, KT, GW]) for n in range(2)]
        w_hi = [place(a, f"w_hi{n}", [P, KT, GW], F32R) for n in range(2)]
        w_lo = [place(a, f"w_lo{n}", [P, KT, GW], F32R) for n in range(2)]
        a = fresh(MRG)
        merged = place(a, "merged", [P, KT, T])
        a = fresh(MRG)
        x_sb = place(a, "x_sb", [P, KT, T])
        a = fresh(MRG)
        CW = T + 4
        conv_in = [place(a, f"conv_in{n}", [P, CW]) for n in range(2)]
        conv_out = [place(a, f"conv_out{n}", [P, CW]) for n in range(2)]
        leave = [place(a, f"leave{n}", [P, CW]) for n in range(2)]
        a = fresh(EV)
        row_bc = place(a, "row_bc", [P, T])
        wide = [place(a, f"wide{n}", [P, T]) for n in range(2)]
        at_tmp = list(a)
        tmp = place(a, "tmp", [P, T])

        a = fresh(ACTV)
        xin = [place(a, f"xin{n}", [P, 12, P]) for n in range(2)]
        xt = [place(a, f"xt{n}", [P, 1280]) for n in range(2)]
        after = place(a, "after", [P, SH, P])
        before = place(a, "before", [P, SH, P])
        e_ssm = place(a, "e_ssm", [P, SH, P])
        w_f = place(a, "w_f", [P, SH, P])
        a2 = fresh(WT)
        w_b = place(a2, "w_b", [P, SH, P])
        x_dt = [place(a2, f"x_dt{n}", [P, SH, SP_]) for n in range(2)]
        d_x = place(a2, "d_x", [P, SH, SP_])
        cb = [place(a2, f"cb{n}", [P, SG, P]) for n in range(2)]
        a = fresh(MRG)
        y_acc = place(a, "y_acc", [P, NT, D_MODEL])
        a = fresh(ACTV)
        xs = [[place(a, f"xs{d}{n}", [P, 1280]) for n in range(2)] for d in range(2)]
        c_t = [[place(a, f"c_t{d}{n}", [P, SG, P]) for n in range(2)] for d in range(2)]
        s_ssm = [place(a, f"s_ssm{d}", [P, D_MODEL]) for d in range(2)]
        s_kept = [place(a, f"s_kept{d}", [P, D_MODEL]) for d in range(2)]
        x_in = [place(a, f"x_in{d}", [P, SH, SP_]) for d in range(2)]
        y_tmp = [place(a, f"y_tmp{d}", [P, D_MODEL]) for d in range(2)]
        s_io = [place(a, f"s_io{d}", [P, 8, P]) for d in range(2)]
        a = fresh(WT)
        y_st = [place(a, f"y_st{n}", [P, D_MODEL]) for n in range(2)]
        z_c = [place(a, f"z_c{n}", [P, KT, P]) for n in range(2)]
        yz = place(a, "yz", [P, KT, P])
        yzw = place(a, "yzw", [P, KT, P])
        y_sq = place(a, "y_sq", [P, KT, P])
        a = fresh(ACTV)
        gin = [place(a, f"gin{n}", [P, 12, P]) for n in range(2)]
        g_sq = place(a, "g_sq", [P, 8, GD])
        q_n = place(a, "q_n", [P, GH, GD])
        g_out = [place(a, f"g_out{n}", [P, 6, 512]) for n in range(2)]
        a = fresh(WT)
        g_t = [[place(a, f"g_t{d}{n}", [P, 6, 512]) for n in range(2)] for d in range(2)]
        a = fresh(ACTV)
        gd = []
        for d in range(2):
            g = {"col": place(a, f"col{d}", [P, 8, P])}
            for n in ("E", "Q0", "Q", "A0", "A", "T", "X", "Y", "VB", "R0", "R", "V", "KD", "SK", "S", "O"):
                g[n] = place(a, f"g_{n}{d}", [P, GH, GD])
            gd.append(g)
        a = fresh(EV)
        o_acc = place(a, "o_acc", [P, NT, 512])
        a = fresh(WT)
        o_st = [place(a, f"o_st{n}", [P, GH, GD]) for n in range(2)]
        z_a = [place(a, f"z_a{n}", [P, GH, P]) for n in range(2)]
        o_sq = place(a, "o_sq", [P, GH, GD])
        o_z = place(a, "o_z", [P, GH, P])
        a = fresh(WT)
        q_stack = place(a, "q_stack", [P, NT, AH, P], F32R)
        q_now = place(a, "q_now", [P, AH, P], F32R)
        o_att = place(a, "o_att", [P, AH, AD])
        z_b = place(a, "z_b", [P, 4, P])
        o_bz = place(a, "o_bz", [P, 4, P])
        half = ACTV[0] + 4 * T * 4
        a = [half, half, half + 4 * T * 4]
        k_hi = place(a, "k_hi", [P, KVH, 10 * P], F32R)
        v_all = place(a, "v_all", [P, 10, P])
        half = ACTV[0] + 12 * T * 4
        a = [half, half, half + 4 * T * 4]
        k_lo = place(a, "k_lo", [P, KVH, 10 * P], F32R)
        a = fresh(EV)
        ain = [place(a, f"ain{n}", [P, 6, P]) for n in range(2)]
        a_sq = place(a, "a_sq", [P, 10, AD])
        qk = place(a, "qk", [P, 10, AD])
        qk_c = place(a, "qk_c", [P, 10, AD])
        q_hl = place(a, "q_hl", [P, AH, P], F32R)
        k_hh = place(a, "k_hh", [P, KVH, P], F32R)
        k_ll = place(a, "k_ll", [P, KVH, P], F32R)
        a = fresh(EV)
        prob = [place(a, f"prob{n}", [P, T]) for n in range(2)]
        prob_t = [place(a, f"prob_t{n}", [P, 9, P]) for n in range(2)]
        a = fresh(WT)
        x_tok = [place(a, f"x_tok{n}", [P, D_MODEL]) for n in range(2)]
        x_blk = [place(a, f"x_blk{n}", [P, KT, P]) for n in range(2)]
        f_gain = place(a, "f_gain", [P, D_MODEL])
        rows_wide = place(a, "rows_wide", [P, D_MODEL])
        rows_in = place(a, "rows_in", [P, P])
        a = fresh(EV)
        vec_in = place(a, "vec_in", [P, P])
        dec = {}
        a = fresh(ACTV)
        for n in ("pre", "neg", "low", "e_abs", "e_low", "u", "s", "s2", "poly", "soft"):
            dec[n] = place(a, f"dec_{n}", [P, NT, 48])
        r_diag = place(at_tmp, "r_diag", [P, NT, P])
        rest = place(a, "rest", [P, 2, NT, 20])

        PSUM = ctx.enter_context(nc.psum_tensor("PSUM", [P, 4096], F32))

        def bank(n, width=512, at=0):
            return PSUM[:, 512 * n + at:512 * n + at + width]

        def acc(b):
            return PSUM[:, 1536 * b:1536 * b + T]

        ident = cst[:, C_ID]
        ones = cst[:, C_ONE]
        block = ctx.enter_context(nc.Block())
        phase_done = sem("phase_done")

        waits_held = sem("waits_held")

        cst_in = sem("cst_in")
        first_t = sem("first_t")
        first_c = sem("first_c")
        cond_t = sem("cond_t")
        cond_th = sem("cond_th")
        vec_loaded = sem("vec_loaded")
        vec_t = sem("vec_t")
        coef_e = sem("coef_e")
        mod_used = sem("mod_used")
        x_in_sb = sem("x_in_sb")
        n_sq = sem("n_sq")
        n_mm = sem("n_mm")
        n_ms = sem("n_ms")
        n_r = sem("n_r")
        n_diag = sem("n_diag")
        n_bc = sem("n_bc")
        n_row = sem("n_row")
        n_t = sem("n_t")
        n_h = sem("n_h")
        dt_loaded = sem("dt_loaded")
        decay_prod = sem("decay_prod")
        decay_term = sem("decay_term")
        decay_exp = sem("decay_exp")
        sp_prod = sem("sp_prod")
        sp_fwd = sem("sp_fwd")
        sp_bwd = sem("sp_bwd")
        sp_e = sem("sp_e")
        sp_yd = sem("sp_yd")
        states_out = sem("states_out")
        y_copied = sem("y_copied")
        y_ss_read = sem("y_ss_read")
        transposed = sem("transposed")
        squared = sem("squared")
        sums_made = sem("sums_made")
        inv_rms = sem("inv_rms")
        scaled = sem("scaled")
        gated = sem("gated")
        hi_made = sem("hi_made")
        lo_made = sem("lo_made")
        out_ready = sem("out_ready")
        tile_stored = sem("tile_stored")
        gp_c = sem("gp_c")
        gp_k = sem("gp_k")
        gp_tt = sem("gp_tt")
        o_zero = sem("o_zero")
        a_v = sem("a_v")
        a_split = sem("a_split")
        a_st = sem("a_st")
        a_k = sem("a_k")
        a_q = sem("a_q")
        a_sin = sem("a_sin")
        qk_done = sem("qk_done")
        past_in = sem("past_in")
        kv_out = sem("kv_out")
        q_set = sem("q_set")
        at_s = sem("at_s")
        at_m = sem("at_m")
        at_e = sem("at_e")
        at_v = sem("at_v")
        o_norm = sem("o_norm")
        o_tr = sem("o_tr")
        zb_in = sem("zb_in")
        m_hi = sem("m_hi")
        m_lo = sem("m_lo")
        x_new = sem("x_new")
        f_in = sem("f_in")
        f_tr = sem("f_tr")
        f_sq = sem("f_sq")
        f_ms = sem("f_ms")
        f_r = sem("f_r")
        f_y = sem("f_y")
        tok_in = [sem(f"tok_in{i}") for i in range(2)]
        first_out = [sem(f"first_out{i}") for i in range(2)]
        f_out = [sem(f"f_out{i}") for i in range(2)]
        mod_in = [sem(f"mod_in{i}") for i in range(2)]
        w_loaded = [sem(f"w_loaded{i}") for i in range(2)]
        w_ready = [sem(f"w_ready{i}") for i in range(2)]
        acc_ready = [sem(f"acc_ready{i}") for i in range(2)]
        acc_free = [sem(f"acc_free{i}") for i in range(2)]
        conv_mid = [sem(f"conv_mid{i}") for i in range(2)]
        th_ready = [sem(f"th_ready{i}") for i in range(2)]
        leave_free = [sem(f"leave_free{i}") for i in range(2)]
        leave_ready = [sem(f"leave_ready{i}") for i in range(2)]
        leave_out = [sem(f"leave_out{i}") for i in range(2)]
        wide_free = [sem(f"wide_free{i}") for i in range(2)]
        wide_in = [sem(f"wide_in{i}") for i in range(2)]
        x_out = [sem(f"x_out{i}") for i in range(2)]
        tile_in = [sem(f"tile_in{i}") for i in range(2)]
        state_in = [sem(f"state_in{i}") for i in range(2)]
        ssm_s_t = [sem(f"ssm_s_t{i}") for i in range(2)]
        state = [sem(f"state{i}") for i in range(2)]
        ssm_s_out = [sem(f"ssm_s_out{i}") for i in range(2)]
        ssm_prod = [sem(f"ssm_prod{i}") for i in range(2)]
        ssm_side = [sem(f"ssm_side{i}") for i in range(2)]
        g_term = [sem(f"g_term{i}") for i in range(2)]
        g_row = [sem(f"g_row{i}") for i in range(2)]
        g_e = [sem(f"g_e{i}") for i in range(2)]
        g_x = [sem(f"g_x{i}") for i in range(2)]
        g_level = [sem(f"g_level{i}") for i in range(2)]
        g_tm = [sem(f"g_tm{i}") for i in range(2)]
        g_from_s = [sem(f"g_from_s{i}") for i in range(2)]
        g_side = [sem(f"g_side{i}") for i in range(2)]
        g_from_v = [sem(f"g_from_v{i}") for i in range(2)]
        g_v = [sem(f"g_v{i}") for i in range(2)]
        g_vc = [sem(f"g_vc{i}") for i in range(2)]
        g_step = [sem(f"g_step{i}") for i in range(2)]
        at_t = [sem(f"at_t{i}") for i in range(3)]
        at_c = [sem(f"at_c{i}") for i in range(3)]
        scan_in = [[sem(f"scan_in{d}{i}") for i in range(2)] for d in range(2)]

        def barrier(e, l, k):
            e.sem_inc(waits_held, 1)
            e.drain().then_inc(phase_done, 1)
            e.wait_ge(phase_done, l * 5 * NPH + 5 * (k + 2))
            e.sem_inc(waits_held, 1)

        def first_barrier(e):
            e.drain().then_inc(phase_done, 1)
            e.wait_ge(phase_done, 5)

        def tiles(e, body):
            with e.Fori(0, NT // 2) as i:
                for p in range(2):
                    body(i * 2 + p, p, i)
            body(NT - 1, 0, NT // 2)

        def cols(t):
            return slice(t * P, t * P + P) if isinstance(t, int) else bass.ds(t * P, P)

        def one(c):
            return slice(c, c + 1) if isinstance(c, int) else bass.ds(c, 1)

        def nth(l, t, k, of):
            return (l * of + k) * NT + t

        def loaded(l, p, i, k):
            return ((l * 5 + k) * (5 - p) + i + 1) * 16

        def scan_loaded(l, p, count):
            return (l * 3 * (5 - p) + count) * 16

        def split_count(l, m):
            return l * (NG // 2) + m

        def load_group(sp, l, p, m, src):
            sp.wait_ge(w_ready[p], split_count(l, m) + 1)
            sp.dma_start(w_raw[p][:, 0:src.shape[1], 0:src.shape[2]], src).then_inc(w_loaded[p], 16)

        def split_group(dve, l, n, p, m, kt):
            dve.wait_ge(w_loaded[p], 16 * split_count(l, m) + 16)
            dve.wait_ge(acc_ready[1], l * NG + n + 1)
            dve.tensor_copy(w_hi[p][:, 0:kt], w_raw[p][:, 0:kt])
            dve.drain()
            dve.tensor_tensor(w_lo[p][:, 0:kt], w_raw[p][:, 0:kt], w_hi[p][:, 0:kt].bitcast(F32),
                              ALU.subtract).then_inc(w_ready[p], 1)

        def multiply_group(pe, l, n, p, m, kt, x_hi, x_lo):
            pe.wait_ge(w_ready[p], split_count(l, m) + 2)
            for b in range(2):
                pe.wait_ge(acc_free[b], l * NG + n + 1)
                for lo, hi in CHUNKS:
                    dst = PSUM[:, 1536 * b + lo:1536 * b + hi]
                    for k in range(kt):
                        wh = w_hi[p][:, k, b * P:b * P + P]
                        wl = w_lo[p][:, k, b * P:b * P + P]
                        pe.matmul(dst, wh, x_hi[:, k, lo:hi], start=(k == 0), stop=False)
                        pe.matmul(dst, wh, x_lo[:, k, lo:hi], start=False, stop=False)
                        last = pe.matmul(dst, wl, x_hi[:, k, lo:hi], start=False, stop=(k == kt - 1))
                last.then_inc(acc_ready[b], 1)

        def acc_done(l, n, b):
            return l * NG + n + 1 + (2 if b else 0)

        def groups(e, base, count, body):
            with e.Fori(0, count // 2) as i:
                for p in range(2):
                    body(i * 2 + (base + p), p, i + base // 2, i * 2 + p)

        @block.sync
        def _(sp):
            sp.dma_start(cst[:], table.rearrange("p (c n) -> p c n", n=P)).then_inc(cst_in, 16)
            sp.dma_start(rope[:], rope_table.rearrange("p (t a d) -> p t a d", t=NT, a=2)).then_inc(cst_in, 16)
            sp.dma_start(rows_in[0:8], A["c"].rearrange("b (k p) -> (b k) p", p=P)).then_inc(cst_in, 16)
            sp.dma_start(rows_in[8:16], A["c_ctx"].rearrange("(k p) -> k p", p=P)).then_inc(cst_in, 16)
            sp.dma_start(rows_in[16:24], A["final_norm_w"].rearrange("(k p) -> k p", p=P)).then_inc(cst_in, 16)
            xsm = A["x_sample"].rearrange("b t d -> (b t) d")
            for t in range(NT):
                if t >= 2:
                    sp.wait_ge(first_t, t - 1)
                src = xsm[t * P:(t + 1) * P] if t < NS else A["x_prompt"].rearrange("b t d -> (b t) d")
                sp.dma_start(x_tok[t % 2][:], src).then_inc(tok_in[t % 2], 16)
            first_barrier(sp)

            with sp.Fori(0, DEPTH) as l:
                for at, name in ((V_NORM, "norm_w"), (V_BMOD, "b_mod"), (V_SBIAS, "ssm_conv_b"),
                                 (V_SNORM, "ssm_norm_w"), (V_GNORM, "gdn_norm_w")):
                    src = A[name][l].rearrange("(k p) -> k p", p=P)
                    sp.dma_start(vec_in[at:at + src.shape[0]], src).then_inc(vec_loaded, 16)
                for at, name in ((V_GCONV, "gdn_conv_w"), (V_SCONV, "ssm_conv_w")):
                    sp.dma_start(vec_in[at:at + 36], A[name][l].rearrange("w (k p) -> (w k) p", p=P)).then_inc(vec_loaded, 16)
                for at, name in ((0, "gdn_a_log"), (8, "ssm_a_log"), (40, "gdn_dt_bias"), (48, "ssm_dt_bias")):
                    src = A[name][l].rearrange("d h -> (d h)")
                    sp.dma_start(rows[:, at:at + src.shape[0]], src.partition_broadcast(P)).then_inc(vec_loaded, 16)
                sp.dma_start(rows[:, 80:96], A["ssm_d"][l].partition_broadcast(P)).then_inc(vec_loaded, 16)
                for at, name, heads in ((0, "attn_q_norm", AH), (AH, "attn_k_norm", KVH)):
                    for h in range(heads):
                        sp.dma_start(qk_gain[:, at + h], A[name][l].partition_broadcast(P)).then_inc(vec_loaded, 16)
                wm = A["w_mod"][l].rearrange("(k p) n -> p k n", p=P)
                for g in range(12):
                    if g >= 2:
                        sp.wait_ge(mod_used, l * 12 + g - 1)
                    sp.dma_start(w_raw[g % 2][:], wm[:, :, g * GW:(g + 1) * GW]).then_inc(mod_in[g % 2], 16)
                barrier(sp, l, 0)

                for k in range(KT):
                    sp.dma_start(x_sb[:, k], x_d[k]).then_inc(x_in_sb, 16)
                barrier(sp, l, 1)

                win = A["w_in"][l].rearrange("(k p) n -> p k n", p=P)
                base = G_PROJ
                for kind, pairs, col, _ in PROJ_RUNS:
                    if kind == "kv_small":
                        load_group(sp, l, 0, base // 2, win[:, :, col:col + GW])
                        load_group(sp, l, 1, base // 2, win[:, :, BETA_COL:BETA_COL + 16])
                        sp.dma_start(w_raw[1][:, :, P:P + 32], win[:, :, DT_COL:DT_COL + 32]).then_inc(dt_loaded, 16)
                    else:
                        groups(sp, base, 2 * pairs, lambda n, p, m, j: load_group(
                            sp, l, p, m, win[:, :, bass.ds(j * GW + col, GW)]))
                    base += 2 * pairs
                barrier(sp, l, 2)
                barrier(sp, l, 3)

                def xin_load(t, p):
                    sp.dma_start(xin[p][:], proj_d[B_XBC:B_XBC + 12, :, cols(t)].rearrange("k p t -> p k t")).then_inc(tile_in[p], 16)

                def xt_store(t, p):
                    sp.wait_ge(out_ready, nth(l, t, 0, 2) + 1)
                    sp.dma_start(ssm_tok_d[t], xt[p][:]).then_inc(tile_stored, 16)
                    sp.wait_ge(tile_stored, nth(l, t, 0, 2) * 16 + 16)
                    sp.sem_inc(waits_held, 1)
                xin_load(0, 0)
                xin_load(1, 1)
                with sp.Fori(0, 3) as i:
                    for p in range(2):
                        xt_store(i * 2 + p, p)
                        xin_load(i * 2 + (p + 2), p)
                xt_store(6, 0)
                xin_load(8, 0)
                xt_store(7, 1)
                xt_store(8, 0)
                barrier(sp, l, 4)

                def scan_tile(i, d):
                    if isinstance(i, int) and i == NS:
                        return NS
                    return i if d == 0 else (NS - 1) - i

                def ssm_loads(i, p):
                    for d in range(2):
                        t = scan_tile(i, d)
                        sp.dma_start(xs[d][p][:], ssm_tok_d[t]).then_inc(scan_in[d][p], 16)
                        sp.dma_start(c_t[d][p][:], proj_d[B_XBC + 10:B_XBC + 12, :, cols(t)].rearrange("k p t -> p k t")).then_inc(scan_in[d][p], 16)
                for d in range(2):
                    sp.dma_start(s_io[d][:], A["state_ssm"][0, l, d].rearrange("(b h) p n -> (h p) b n", h=2)).then_inc(state_in[d], 16)
                ssm_loads(0, 0)
                ssm_loads(1, 1)
                with sp.Fori(0, 3) as i:
                    for p in range(2):
                        for d in range(2):
                            sp.wait_ge(state[d], i * 2 + (l * 22 + p + 2))
                        ssm_loads(i * 2 + (p + 2), p)
                for d in range(2):
                    sp.wait_ge(state[d], l * 22 + 8)
                ssm_loads(NS, 0)
                for d in range(2):
                    sp.wait_ge(ssm_s_out[d], l + 1)
                    sp.dma_start(O["state_ssm"][0, l, d].rearrange("(b h) p n -> (h p) b n", h=2), s_io[d][:]).then_inc(states_out, 16)
                sp.wait_ge(states_out, l * 64 + 32)
                barrier(sp, l, 5)

                def z_loads(buf, blk, n_blk, k):
                    def load(t, p):
                        sp.dma_start(buf[p][:], proj_d[blk:blk + n_blk, :, cols(t)].rearrange("k p t -> p k t")).then_inc(tile_in[p], 16)
                    load(0, 0)
                    load(1, 1)
                    with sp.Fori(0, 3) as i:
                        for p in range(2):
                            sp.wait_ge(lo_made, nth(l, i * 2, k, 3) + (p + 1))
                            load(i * 2 + (p + 2), p)
                    sp.wait_ge(lo_made, nth(l, 7, k, 3))
                    load(8, 0)
                z_loads(z_c, B_ZC, KT, 0)
                barrier(sp, l, 6)

                def branch(base, name, kt, gate):
                    w = A[name][l].rearrange("(k p) n -> p k n", p=P)

                    def body(n, p, m, j):
                        load_group(sp, l, p, m, w[:, :, bass.ds(j * GW, GW)])
                        for b in range(2):
                            sp.wait_ge(wide_free[b], l * 16 + (j + (base - G_SSM + 1)))
                            sp.dma_start(wide[b][:], proj_d[j * 2 + (gate + b)] if gate is not None else x_d[j * 2 + b]).then_inc(wide_in[b], 16)
                    groups(sp, base, 4, body)
                branch(G_SSM, "w_branch_c", 8, B_GATE + 16)
                barrier(sp, l, 7)

                def gin_load(t, p):
                    sp.dma_start(gin[p][:], proj_d[B_GDN:B_GDN + 12, :, cols(t)].rearrange("k p t -> p k t")).then_inc(tile_in[p], 16)

                def g_store(t, p):
                    sp.wait_ge(out_ready, nth(l, t, 1, 2) + 1)
                    sp.dma_start(gdn_tile_d[t], g_out[p][:]).then_inc(tile_stored, 16)
                    sp.wait_ge(tile_stored, nth(l, t, 1, 2) * 16 + 16)
                    sp.sem_inc(waits_held, 1)
                gin_load(0, 0)
                gin_load(1, 1)
                with sp.Fori(0, 3) as i:
                    for p in range(2):
                        g_store(i * 2 + p, p)
                        gin_load(i * 2 + (p + 2), p)
                g_store(6, 0)
                gin_load(8, 0)
                g_store(7, 1)
                g_store(8, 0)
                barrier(sp, l, 8)

                def gdn_loads(i, p):
                    for d in range(2):
                        sp.dma_start(g_t[d][p][:], gdn_tile_d[scan_tile(i, d)]).then_inc(scan_in[d][p], 16)
                for d in range(2):
                    sp.dma_start(gd[d]["S"][:], A["state_gdn"][0, l, d].rearrange("h k v -> k h v")).then_inc(state_in[d], 16)
                gdn_loads(0, 0)
                gdn_loads(1, 1)
                with sp.Fori(0, 3) as i:
                    for p in range(2):
                        for d in range(2):
                            sp.wait_ge(g_step[d], i * 2 + (l * NT + p + 1))
                        gdn_loads(i * 2 + (p + 2), p)
                for d in range(2):
                    sp.wait_ge(g_step[d], l * NT + 7)
                gdn_loads(NS, 0)
                for d in range(2):
                    sp.wait_ge(g_step[d], l * NT + 9)
                    sp.dma_start(O["state_gdn"][0, l, d].rearrange("h k v -> k h v"), gd[d]["S"][:]).then_inc(states_out, 16)
                sp.wait_ge(states_out, l * 64 + 64)
                barrier(sp, l, 9)

                z_loads(z_a, B_ZA, 4, 1)
                barrier(sp, l, 10)
                branch(G_GDN, "w_branch_a", 4, B_GATE)
                barrier(sp, l, 11)

                def ain_load(t, p):
                    sp.dma_start(ain[p][:], proj_d[B_ATT:B_ATT + 6, :, cols(t)].rearrange("k p t -> p k t")).then_inc(tile_in[p], 16)
                ain_load(0, 0)
                ain_load(1, 1)
                with sp.Fori(0, 3) as i:
                    for p in range(2):
                        sp.wait_ge(transposed, nth(l, i * 2, 4, 5) + (p + 1))
                        ain_load(i * 2 + (p + 2), p)
                sp.wait_ge(transposed, nth(l, 7, 4, 5))
                ain_load(8, 0)
                sp.wait_ge(transposed, nth(l, 8, 4, 5))
                sp.dma_start(ain[1][:, 0], A["cache_k"][0, l].rearrange("t g d -> t (g d)")).then_inc(past_in, 16)
                sp.dma_start(v_all[:, NT], A["cache_v"][0, l].rearrange("t g d -> t (g d)")).then_inc(past_in, 16)
                sp.wait_ge(qk_done, l * NT + 9)
                sp.dma_start(O["cache_k"][0, l].rearrange("t g d -> t (g d)"), qk[:, AH:10].rearrange("p h d -> p (h d)")).then_inc(kv_out, 16)
                sp.dma_start(O["cache_v"][0, l].rearrange("t g d -> t (g d)"), v_all[:, NS]).then_inc(kv_out, 16)
                sp.wait_ge(kv_out, l * 32 + 32)
                barrier(sp, l, 12)

                def zb_load(t):
                    sp.dma_start(z_b[:], proj_d[B_ZB:B_ZB + 4, :, cols(t)].rearrange("k p t -> p k t")).then_inc(zb_in, 16)
                zb_load(0)
                with sp.Fori(0, NS) as t:
                    sp.wait_ge(lo_made, nth(l, t, 2, 3) + 1)
                    zb_load(t + 1)
                barrier(sp, l, 13)
                branch(G_ATT, "w_branch_b", 4, B_GATE + 8)
                barrier(sp, l, 14)
                branch(G_OUT, "w_out", 8, None)
                barrier(sp, l, 15)

            sp.dma_start(f_gain[:], A["final_norm_w"].partition_broadcast(P)).then_inc(f_in, 16)
            for t in range(NT + 2):
                if t < NT:
                    if t >= 2:
                        sp.wait_ge(f_tr, t - 1)
                    sp.dma_start(x_blk[t % 2][:], x_d[:, :, cols(t)].rearrange("k p t -> p k t")).then_inc(tok_in[t % 2], 16)
                if t >= 2:
                    sp.wait_ge(f_y, t - 1)
                    u = t - 2
                    dst = O["y_sample"].rearrange("b t d -> (b t) d")[u * P:(u + 1) * P] if u < NS else O["y_prompt"].rearrange("b t d -> (b t) d")
                    sp.dma_start(dst, x_tok[u % 2][:]).then_inc(f_out[u % 2], 16)
            sp.wait_ge(f_out[0], 80)
            sp.wait_ge(f_out[1], 64)

        @block.tensor
        def _(pe):
            pe.sem_inc(acc_ready[1], 2)

            pe.wait_ge(cst_in, 80)
            pe.transpose(bank(7, 24), rows_in[0:24], ident[0:24, 0:24]).then_inc(cond_t, 1)
            for t in range(NT):
                pe.wait_ge(tok_in[t % 2], 16 * (t // 2) + 16)
                if t >= 2:
                    pe.wait_ge(first_c, t - 1)
                for k in range(KT):
                    last = pe.transpose(bank(2 * (t % 2), P, k * P), x_tok[t % 2][:, k * P:(k + 1) * P], ident)
                last.then_inc(first_t, 1)
            first_barrier(pe)

            def sums_to_rows(u):
                pe.wait_ge(n_diag, u + 1)
                for t in range(NT):
                    last = pe.matmul(PSUM[:, 1536 + t * P:1536 + (t + 1) * P], ones, r_diag[:, t], start=True, stop=True)
                last.then_inc(n_bc, 1)

            with pe.Fori(0, DEPTH) as l:
                pe.wait_ge(vec_loaded, l * (22 * 16) + 22 * 16)
                pe.transpose(bank(0, NV), vec_in[0:NV], ident[0:NV, 0:NV]).then_inc(vec_t, 1)
                for g in range(12):
                    pe.wait_ge(mod_in[g % 2], l * 96 + 16 * (g // 2) + 16)
                    for b in range(2):
                        for k in range(KT):
                            last = pe.matmul(bank(1, 2, 2 * (2 * g + b)), w_raw[g % 2][:, k, b * P:(b + 1) * P],
                                             cond[:, k:16:8], start=(k == 0), stop=(k == KT - 1))
                    last.then_inc(mod_used, 1)
                barrier(pe, l, 0)

                for k in range(KT):
                    pe.wait_ge(n_sq, l * KT + k + 1)
                    for t in range(NT):
                        last = pe.matmul(bank(0, 1, t), wide[k % 2][:, t * P:(t + 1) * P], ones[:, 0:1],
                                         start=(k == 0 and t == 0), stop=(k == KT - 1 and t == NT - 1),
                                         skip_group_check=True)
                    last.then_inc(n_mm, 1)
                sums_to_rows(l * 2)
                barrier(pe, l, 1)

                base = G_PROJ
                for kind, pairs, col, _ in PROJ_RUNS:
                    groups(pe, base, 2 * pairs, lambda n, p, m, j: multiply_group(pe, l, n, p, m, KT, h_hi, h_lo))
                    base += 2 * pairs
                barrier(pe, l, 2)

                for t in range(NT):
                    pe.transpose(bank(0, 16, t * 48), wide[0][0:16, t * P:(t + 1) * P], ident[0:16, 0:16])
                    last = pe.transpose(bank(0, 32, t * 48 + 16), wide[1][0:32, t * P:(t + 1) * P], ident[0:32, 0:32])
                last.then_inc(decay_prod, 1)
                pe.wait_ge(decay_term, l * 3 + 2)
                for d in range(2):
                    pe.matmul(bank(1 + d, 180), cst[:, C_TRI + d], logd[:, :, d], start=True, stop=True)
                    last = pe.matmul(bank(3 + d, 180), ones, logd[:, :, d], start=True, stop=True)
                last.then_inc(decay_prod, 1)
                barrier(pe, l, 3)

                def ssm_prep(t, p, i):
                    n = l * NT + t
                    pe.wait_ge(tile_in[p], loaded(l, p, i, 0))
                    for k in range(10):
                        pe.transpose(PSUM[:, k * P:(k + 1) * P], xin[p][:, k], ident)
                    for g in range(SG):
                        last = pe.matmul(bank(7, P, g * P), xin[p][:, 8 + g], xin[p][:, 10 + g], start=True, stop=True)
                    last.then_inc(transposed, 1)
                    pe.wait_ge(sp_fwd, n * 3 + 1)
                    pe.wait_ge(sp_bwd, n * 2 + 1)
                    for h in range(SH):
                        dst = PSUM[:, 1536 + h * P:1536 + (h + 1) * P]
                        pe.matmul(dst, after[:, h], cst[:, C_TRI], start=True, stop=False)
                        last = pe.matmul(dst, before[:, h], cst[:, C_TRI + 1], start=False, stop=True)
                    last.then_inc(sp_prod, 1)
                    pe.wait_ge(sp_fwd, n * 3 + 3)
                    pe.wait_ge(sp_bwd, n * 2 + 2)
                    for h in range(SH):
                        dst = PSUM[:, h * SP_:(h + 1) * SP_]
                        pe.matmul(dst, w_f[:, h], x_dt[0][:, h], start=True, stop=False)
                        last = pe.matmul(dst, w_b[:, h], x_dt[1][:, h], start=False, stop=True)
                    last.then_inc(sp_prod, 1)
                    pe.wait_ge(sp_yd, n + 1)
                tiles(pe, ssm_prep)
                barrier(pe, l, 4)

                for d in range(2):
                    pe.wait_ge(state_in[d], l * 32 + 16)
                    for b in range(8):
                        last = pe.transpose(PSUM[:, d * 2048 + b * P:d * 2048 + (b + 1) * P], s_io[d][:, b], ident)
                    last.then_inc(ssm_s_t[d], 1)

                def ssm_step(t, p, i):
                    for d in range(2):
                        before_ = l * 22 + (10 if isinstance(t, int) else t + 1)
                        pe.wait_ge(scan_in[d][p], scan_loaded(l, p, 2 * i + 2))
                        pe.wait_ge(state[d], before_)
                        for g in range(SG):
                            last = pe.matmul(bank(4 * d + g), c_t[d][p][:, g], s_ssm[d][:, g * 512:(g + 1) * 512], start=True, stop=True)
                        last.then_inc(ssm_prod[d], 1)
                        pe.wait_ge(ssm_side[d], (l * NT + t) * 2 + 1)
                        for g in range(SG):
                            last = pe.matmul(bank(4 * d + 2 + g), xs[d][p][:, 1024 + g * P:1024 + (g + 1) * P],
                                             x_in[d][:, 8 * g:8 * g + 8].rearrange("p h q -> p (h q)"), start=True, stop=True)
                        last.then_inc(ssm_prod[d], 1)
                tiles(pe, ssm_step)
                for d in range(2):
                    pe.wait_ge(state[d], l * 22 + 11)
                    for b in range(8):
                        last = pe.transpose(PSUM[:, d * 2048 + b * P:d * 2048 + (b + 1) * P], s_ssm[d][:, b * P:(b + 1) * P], ident)
                    last.then_inc(ssm_s_t[d], 1)
                barrier(pe, l, 5)

                def ssm_post(t, p, i):
                    n = l * NT + t
                    pe.wait_ge(y_copied, n + 1)
                    for k in range(KT):
                        last = pe.transpose(PSUM[:, k * P:(k + 1) * P], y_st[p][:, k * P:(k + 1) * P], ident)
                    last.then_inc(transposed, 1)
                    pe.wait_ge(squared, nth(l, t, 0, 4) + 1)
                    for k in range(KT):
                        last = pe.matmul(bank(2, 1), y_sq[:, k], ones[:, 0:1], start=(k == 0), stop=(k == KT - 1))
                    last.then_inc(sums_made, 1)
                    pe.wait_ge(y_ss_read, n + 1)
                tiles(pe, ssm_post)
                sums_to_rows(l * 2 + 1)
                barrier(pe, l, 6)
                groups(pe, G_SSM, 4, lambda n, p, m, j: multiply_group(pe, l, n, p, m, 8, b_hi, b_lo))
                barrier(pe, l, 7)

                def gdn_prep(t, p, i):
                    n = l * NT + t
                    pe.wait_ge(tile_in[p], loaded(l, p, i, 2))
                    for k in range(12):
                        last = pe.transpose(PSUM[:, k * P:(k + 1) * P], gin[p][:, k], ident)
                    last.then_inc(transposed, 1)
                    pe.wait_ge(scaled, nth(l, t, 1, 4) + 1)
                    for h in range(GH):
                        pe.transpose(bank(3, P, h * P), q_n[:, h], ident)
                        last = pe.transpose(bank(4, P, h * P), g_out[p][:, 2, h * P:(h + 1) * P], ident)
                    last.then_inc(gp_tt, 1)
                    pe.wait_ge(gp_c, n + 1)
                    for h in range(GH):
                        hh = slice(h * P, (h + 1) * P)
                        pe.matmul(bank(5)[:, hh], g_out[p][:, 0, hh], g_out[p][:, 0, hh], start=True, stop=True)
                        last = pe.matmul(bank(6)[:, hh], g_out[p][:, 0, hh], g_out[p][:, 1, hh], start=True, stop=True)
                    last.then_inc(gp_k, 1)
                    pe.wait_ge(out_ready, nth(l, t, 1, 2) + 1)
                tiles(pe, gdn_prep)
                barrier(pe, l, 8)

                def gdn_step(t, p, i):
                    n = l * NT + t
                    for d in range(2):
                        g, b0 = gd[d], 4 * d
                        pe.wait_ge(g_term[d], n * 4 + 1)
                        for h in range(GH):
                            pe.matmul(bank(b0 + 3, P, h * P), g["col"][:, h], cst[:, C_TRI + d], start=True, stop=True)
                            last = pe.matmul(bank(b0, P, h * P), g["col"][:, 4 + h], ident, start=True, stop=True)
                        last.then_inc(g_row[d], 1)
                    for d in range(2):
                        g, b0 = gd[d], 4 * d
                        pe.wait_ge(g_term[d], n * 4 + 3)
                        for h in range(GH):
                            last = pe.transpose(bank(b0 + 3, P, h * P), g["A"][:, h], ident)
                        last.then_inc(g_row[d], 1)
                    for d in range(2):
                        g, b0 = gd[d], 4 * d
                        pe.wait_ge(g_x[d], n * 7 + 1)
                        pe.matmul(bank(b0 + 1), ident, g["X"][:].rearrange("p h t -> p (h t)"), start=True, stop=False, skip_group_check=True)
                        pe.matmul(bank(b0 + 2), ident, g["Y"][:].rearrange("p h t -> p (h t)"), start=True, stop=False, skip_group_check=True)
                    for lev in range(1, 7):
                        for d in range(2):
                            g, b0 = gd[d], 4 * d
                            if lev > 1:
                                pe.wait_ge(g_x[d], n * 7 + lev)
                            for h in range(GH):
                                last = pe.matmul(bank(b0, P, h * P), g["A"][:, h], g["X"][:, h], start=True, stop=True)
                            last.then_inc(g_level[d], 1)
                        for d in range(2):
                            g, b0 = gd[d], 4 * d
                            pe.wait_ge(g_tm[d], n * 6 + lev)
                            for h in range(GH):
                                if lev < 6:
                                    pe.matmul(bank(b0 + 1, P, h * P), g["Y"][:, h], g["T"][:, h], start=False, stop=False, skip_group_check=True)
                                last = pe.matmul(bank(b0 + 2, P, h * P), g["T"][:, h], g["Y"][:, h], start=False, stop=(lev == 6 and h == 3), skip_group_check=True)
                            last.then_inc(g_level[d], 1)
                    for d in range(2):
                        g, b0 = gd[d], 4 * d
                        pe.wait_ge(state[d], l * 22 + 11 + (10 if isinstance(t, int) else t + 1))
                        for h in range(GH):
                            last = pe.matmul(bank(b0, P, h * P), g_t[d][p][:, 0, h * P:(h + 1) * P], g["S"][:, h], start=True, stop=True)
                        last.then_inc(g_from_s[d], 1)
                        for h in range(GH):
                            last = pe.matmul(bank(b0 + 3, P, h * P), g_t[d][p][:, 1, h * P:(h + 1) * P], g["S"][:, h], start=True, stop=True)
                        last.then_inc(g_from_s[d], 1)
                    for d in range(2):
                        g, b0 = gd[d], 4 * d
                        pe.wait_ge(g_x[d], n * 7 + 7)
                        pe.wait_ge(g_term[d], n * 4 + 4)
                        for h in range(GH):
                            last = pe.matmul(bank(b0 + 1, P, h * P), g["Y"][:, h], g["R"][:, h], start=True, stop=True)
                        last.then_inc(g_v[d], 1)
                    for d in range(2):
                        g, b0 = gd[d], 4 * d
                        pe.wait_ge(g_vc[d], n + 1)
                        pe.wait_ge(g_side[d], n * 5 + 2)
                        for h in range(GH):
                            last = pe.matmul(bank(b0, P, h * P), g["KD"][:, h], g["V"][:, h], start=True, stop=True)
                        last.then_inc(g_from_v[d], 1)
                        pe.wait_ge(g_side[d], n * 5 + 5)
                        for h in range(GH):
                            last = pe.matmul(bank(b0 + 2, P, h * P), g["Q"][:, h], g["V"][:, h], start=True, stop=True)
                        last.then_inc(g_from_v[d], 1)
                    for d in range(2):
                        pe.wait_ge(g_step[d], n + 1)
                tiles(pe, gdn_step)
                barrier(pe, l, 9)

                def gdn_post(t, p, i):
                    n = l * NT + t
                    pe.wait_ge(scaled, nth(l, t, 2, 4) + 1)
                    for h in range(GH):
                        last = pe.transpose(bank(p, P, h * P), o_st[p][:, h], ident)
                    last.then_inc(transposed, 1)
                    pe.wait_ge(lo_made, nth(l, t, 1, 3) + 1)
                tiles(pe, gdn_post)
                barrier(pe, l, 10)
                groups(pe, G_GDN, 4, lambda n, p, m, j: multiply_group(pe, l, n, p, m, 4, b_hi, b_lo))
                barrier(pe, l, 11)

                def stack(n, q):
                    pe.wait_ge(a_split, n + 1)
                    if q is not None:
                        for h in range(AH):
                            pe.transpose(bank(2, P, h * P), q_hl[:, h].bitcast(F32), ident)
                    for g in range(KVH):
                        pe.transpose(bank(4, P, g * P), k_hh[:, g].bitcast(F32), ident)
                        last = pe.transpose(bank(4, P, 256 + g * P), k_ll[:, g].bitcast(F32), ident)
                    last.then_inc(a_st, 1)
                    pe.wait_ge(a_k, n + 1)
                    if q is not None:
                        pe.wait_ge(a_q, q + 1)

                def attn_prep(t, p, i):
                    n = l * (NT + 1) + t
                    pe.wait_ge(tile_in[p], loaded(l, p, i, 4))
                    for k in range(6):
                        last = pe.transpose(PSUM[:, k * P:(k + 1) * P], ain[p][:, k], ident)
                    last.then_inc(transposed, 1)
                    stack(n, l * NT + t)
                tiles(pe, attn_prep)
                stack(l * (NT + 1) + NT, None)
                barrier(pe, l, 12)

                def attn(t, key_tiles, spans):
                    n = l * NT + t
                    pe.wait_ge(q_set, n + 1)

                    def scores(h):
                        g, s = h // 4, h % 2
                        for col, width, at in spans:
                            dst = PSUM[:, 1536 * s + at:1536 * s + at + width]
                            pe.matmul(dst, q_now[:, h], k_hi[:, g, col:col + width], start=True, stop=False)
                            last = pe.matmul(dst, q_now[:, h], k_lo[:, g, col:col + width], start=False, stop=True)
                        last.then_inc(at_s, 1)
                    nk = len(key_tiles)
                    scores(0)
                    for h in range(AH):
                        g, s = h // 4, h % 2
                        if h + 1 < AH:
                            scores(h + 1)
                        pe.wait_ge(at_e, n * AH + h + 1)
                        for j in range(nk):
                            if j == 8:
                                pe.wait_ge(at_c[0], n * AH + h + 1)
                            last = pe.transpose(bank(6 + (j // 4) % 2, P, (j % 4) * P), prob[s][:, j * P:(j + 1) * P], ident)
                            if j % 4 == 3 or j == nk - 1:
                                last.then_inc(at_t[j // 4], 1)
                        pe.wait_ge(at_c[0], n * AH + h + 1)
                        for q in range(1, (nk + 3) // 4):
                            pe.wait_ge(at_c[q], (l * NS + t) * AH + h + 1)
                        for j, kt in enumerate(key_tiles):
                            last = pe.matmul(PSUM[:, 1536 * s + 1152 + (h // 2) * AD:1536 * s + 1152 + (h // 2 + 1) * AD],
                                             prob_t[s][:, j], v_all[:, kt, g * AD:(g + 1) * AD], start=(j == 0), stop=(j == nk - 1))
                        last.then_inc(at_v, 1)
                    pe.wait_ge(o_norm, n + 1)
                    for k in range(4):
                        last = pe.transpose(bank(6, P, k * P), o_att[:, 2 * k:2 * k + 2].rearrange("p h d -> p (h d)"), ident)
                    last.then_inc(o_tr, 1)
                    pe.wait_ge(lo_made, nth(l, t, 2, 3) + 1)
                with pe.Fori(0, NS) as t:
                    attn(t, [0, 1, 2, 3, 4, 5, 6, 7, 9], [(0, 512, 0), (512, 512, 512), (NT * P, P, 1024)])
                attn(NS, [NS], [(SAMPLE, P, 0)])
                barrier(pe, l, 13)
                groups(pe, G_ATT, 4, lambda n, p, m, j: multiply_group(pe, l, n, p, m, 4, b_hi, b_lo))
                barrier(pe, l, 14)

                pe.wait_ge(m_lo, l * KT + KT)
                pe.sem_inc(waits_held, 1)
                groups(pe, G_OUT, 4, lambda n, p, m, j: multiply_group(pe, l, n, p, m, 8, b_hi, b_lo))
                barrier(pe, l, 15)

            for t in range(NT):
                pe.wait_ge(tok_in[t % 2], 16 * ((5 - t % 2) + t // 2 + 1))
                if t >= 2:
                    pe.wait_ge(f_y, t - 1)
                for k in range(KT):
                    last = pe.transpose(bank(2 * (t % 2), P, k * P), x_blk[t % 2][:, k], ident)
                last.then_inc(f_tr, 1)

        @block.scalar
        def _(act):
            act.wait_ge(cond_t, 1)
            act.activation(stat[:, 0:24], bank(7, 24), ACT.Tanh, scale=0.5).then_inc(cond_th, 1)
            for t in range(NT):
                act.wait_ge(first_t, t + 1)
                if t >= 2:
                    act.wait_ge(first_out[t % 2], 16 * (t // 2))
                act.activation(x_blk[t % 2][:], PSUM[:, 1024 * (t % 2):1024 * (t % 2) + 1024].rearrange("p (k t) -> p k t", t=P), ACT.Copy).then_inc(first_c, 1)
            first_barrier(act)

            with act.Fori(0, DEPTH) as l:
                act.wait_ge(vec_loaded, l * (22 * 16) + 22 * 16)
                act.activation(coef[:, :, 0:4], rows[:, 0:8].rearrange("p (d h) -> p d h", d=2), ACT.Exp)
                act.activation(coef[:, :, 4:20], rows[:, 8:40].rearrange("p (d h) -> p d h", d=2), ACT.Exp).then_inc(coef_e, 1)
                barrier(act, l, 0)

                act.wait_ge(x_in_sb, l * 128 + 128)
                for k in range(KT):
                    if k >= 2:
                        act.wait_ge(n_mm, l * KT + k - 1)
                    act.activation(wide[k % 2][:], x_sb[:, k], ACT.Square).then_inc(n_sq, 1)

                def rows_out(u):
                    act.wait_ge(n_bc, u + 1)
                    act.activation(row_bc[:], acc(1), ACT.Copy).then_inc(n_row, 1)
                rows_out(l * 2)
                for k in range(KT):
                    act.wait_ge(n_t, l * KT + k + 1)
                    for c, (lo, hi) in enumerate(((0, SAMPLE), (SAMPLE, T))):
                        last = act.activation(h_hi[:, k, lo:hi], wide[k % 2][:, lo:hi], ACT.Identity, bias=mod[:, k, c:c + 1])
                    last.then_inc(n_h, 1)
                barrier(act, l, 1)

                base, stored, conv, th = G_PROJ, 0, 0, 0
                for kind, pairs, col, _ in PROJ_RUNS:
                    def body(n, p, m, j, kind=kind, st=stored, cv=conv, tq=th):
                        for b in range(2):
                            act.wait_ge(acc_ready[b], acc_done(l, n, b))
                            if kind.startswith("conv"):
                                act.activation(conv_in[b][:, 1:1 + SAMPLE], acc(b)[:, 0:SAMPLE], ACT.Copy)
                                act.activation(conv_in[b][:, SAMPLE + 2:T + 2], acc(b)[:, SAMPLE:T], ACT.Copy).then_inc(acc_free[b], 1)
                                act.wait_ge(conv_mid[b], l * 12 + j + (cv + 1))
                                act.wait_ge(leave_free[b], l * 35 + j + (st + 1))
                                act.activation(leave[b][:, 0:T + 1], conv_out[b][:, 0:T + 1], ACT.Tanh).then_inc(th_ready[b], 1)
                            elif kind == "kv_small" and j == 1:
                                act.activation(wide[b][0:32], acc(b)[0:32], ACT.Copy).then_inc(acc_free[b], 1)
                            else:
                                act.wait_ge(leave_free[b], l * 35 + j + (st + 1))
                                if kind == "silu":
                                    act.activation(leave[b][:, 0:T], acc(b), ACT.Tanh, scale=0.5).then_inc(th_ready[b], 1)
                                else:
                                    f, sc = (ACT.Tanh, 0.5) if kind == "tanh" else (ACT.Copy, 1.0)
                                    act.activation(leave[b][:, 0:T], acc(b), f, scale=sc).then_inc(leave_ready[b], 1)
                                    act.drain().then_inc(acc_free[b], 1)
                    if kind == "kv_small":
                        body(base, 0, base // 2, 0)
                        body(base + 1, 1, base // 2, 1)
                    else:
                        groups(act, base, 2 * pairs, body)
                    stored += 1 if kind == "kv_small" else 2 * pairs
                    conv += 2 * pairs if kind.startswith("conv") else 0
                    th += 2 * pairs if kind.startswith("conv") or kind == "silu" else 0
                    base += 2 * pairs
                barrier(act, l, 2)

                act.wait_ge(decay_term, l * 3 + 1)
                act.activation(dec["e_abs"][:], dec["neg"][:], ACT.Exp)
                act.activation(dec["e_low"][:], dec["low"][:], ACT.Exp).then_inc(decay_exp, 1)
                act.wait_ge(decay_term, l * 3 + 3)
                act.activation(e_cum[:], cum[:], ACT.Exp)
                act.activation(e_tot[:], tot[:], ACT.Exp)
                act.activation(e_rest[:], rest[:], ACT.Exp).then_inc(decay_exp, 1)
                barrier(act, l, 3)

                def ssm_prep(t, p, i):
                    n = l * NT + t
                    act.wait_ge(transposed, nth(l, t, 0, 5) + 1)
                    act.activation(xt[p][:], PSUM[:, 0:1280], ACT.Copy).then_inc(out_ready, 1)
                    act.wait_ge(sp_prod, n * 2 + 1)
                    act.activation(e_ssm[:], PSUM[:, 1536:3584].rearrange("p (h l) -> p h l", l=P), ACT.Exp).then_inc(sp_e, 1)
                tiles(act, ssm_prep)
                barrier(act, l, 4)

                for d in range(2):
                    act.wait_ge(ssm_s_t[d], l * 2 + 1)
                    act.activation(s_ssm[d][:], PSUM[:, d * 2048:d * 2048 + 1024], ACT.Copy).then_inc(state[d], 1)
                for d in range(2):
                    act.wait_ge(ssm_s_t[d], l * 2 + 2)
                    act.activation(s_io[d][:], PSUM[:, d * 2048:d * 2048 + 1024].rearrange("p (b n) -> p b n", n=P), ACT.Copy).then_inc(ssm_s_out[d], 1)
                barrier(act, l, 5)

                def ssm_post(t, p, i):
                    n = l * NT + t
                    act.activation(y_st[p][:], y_acc[:, t], ACT.Copy).then_inc(y_copied, 1)
                    act.wait_ge(gated, nth(l, t, 0, 3) + 1)
                    act.activation(y_sq[:], yz[:], ACT.Square).then_inc(squared, 1)
                    act.wait_ge(scaled, nth(l, t, 0, 4) + 1)
                    act.activation(b_hi[:, :, cols(t)], yzw[:], ACT.Copy).then_inc(hi_made, 1)
                    act.wait_ge(lo_made, nth(l, t, 0, 3) + 1)
                tiles(act, ssm_post)
                rows_out(l * 2 + 1)
                barrier(act, l, 6)
                barrier(act, l, 7)

                def gdn_prep(t, p, i):
                    n = l * NT + t
                    act.wait_ge(transposed, nth(l, t, 2, 5) + 1)
                    act.activation(g_sq[:], PSUM[:, 0:1024].rearrange("p (h d) -> p h d", d=GD), ACT.Square).then_inc(squared, 1)
                    act.activation(g_out[p][:, 3], bank(2), ACT.Copy)
                    act.wait_ge(gp_tt, n + 1)
                    act.activation(g_out[p][:, 1], bank(3), ACT.Copy)
                    act.activation(g_out[p][:, 0], bank(4), ACT.Copy).then_inc(gp_c, 1)
                    act.wait_ge(gp_k, n + 1)
                    act.activation(g_out[p][:, 4], bank(5), ACT.Copy)
                    act.activation(g_out[p][:, 5], bank(6), ACT.Copy).then_inc(out_ready, 1)
                tiles(act, gdn_prep)
                barrier(act, l, 8)

                def flat(x):
                    return x[:].rearrange("p h t -> p (h t)")

                def gdn_step(t, p, i):
                    n = l * NT + t
                    for d in range(2):
                        act.wait_ge(g_term[d], n * 4 + 2)
                        act.activation(gd[d]["E"][:], gd[d]["E"][:], ACT.Exp).then_inc(g_e[d], 1)
                    for lev in range(1, 7):
                        for d in range(2):
                            act.wait_ge(g_level[d], n * 12 + 2 * lev)
                            if lev < 6:
                                act.activation(flat(gd[d]["X"]), bank(4 * d + 1), ACT.Copy)
                            act.activation(flat(gd[d]["Y"]), bank(4 * d + 2), ACT.Copy).then_inc(g_x[d], 1)
                    for d in range(2):
                        act.wait_ge(g_v[d], n + 1)
                        act.activation(flat(gd[d]["V"]), bank(4 * d + 1), ACT.Copy).then_inc(g_vc[d], 1)
                tiles(act, gdn_step)
                barrier(act, l, 9)

                def gdn_post(t, p, i):
                    n = l * NT + t
                    act.activation(o_sq[:], o_acc[:, t].rearrange("p (h d) -> p h d", d=GD), ACT.Square).then_inc(squared, 1)
                    act.wait_ge(gated, nth(l, t, 1, 3) + 1)
                    act.activation(b_hi[:, 0:4, cols(t)], o_z[:], ACT.Copy).then_inc(hi_made, 1)
                    act.wait_ge(lo_made, nth(l, t, 1, 3) + 1)
                tiles(act, gdn_post)
                barrier(act, l, 10)
                barrier(act, l, 11)

                def attn_prep(t, p, i):
                    n, n1 = l * NT + t, l * (NT + 1) + t
                    act.wait_ge(transposed, nth(l, t, 4, 5) + 1)
                    act.activation(a_sq[:], PSUM[:, 0:640].rearrange("p (h d) -> p h d", d=AD), ACT.Square).then_inc(squared, 1)
                    act.activation(v_all[:, t], PSUM[:, 640:768], ACT.Copy).then_inc(a_v, 1)
                    act.wait_ge(a_st, n1 + 1)
                    act.activation(q_stack[:, t], PSUM[:, 1024:2048].rearrange("p (h t) -> p h t", t=P), ACT.Copy).then_inc(a_q, 1)
                tiles(act, attn_prep)
                barrier(act, l, 12)

                def attn(t, nk):
                    n, ns = l * NT + t, l * NS + t
                    width = nk * P
                    for h in range(AH):
                        s = h % 2
                        act.wait_ge(at_m, n * AH + h + 1)
                        act.activation(prob[s][:, 0:width], PSUM[:, 1536 * s:1536 * s + width], ACT.Exp, bias=stat[:, h:h + 1],
                                       accum_out=stat[:, 8 + h:9 + h]).then_inc(at_e, 1)
                        if nk > 1:
                            act.wait_ge(at_t[1], ns * AH + h + 1)
                            act.activation(prob_t[s][:, 4:8], bank(7).rearrange("p (j t) -> p j t", t=P), ACT.Copy).then_inc(at_c[1], 1)
                    act.wait_ge(gated, nth(l, t, 2, 3) + 1)
                    act.activation(b_hi[:, 0:4, cols(t)], o_bz[:], ACT.Copy).then_inc(hi_made, 1)
                with act.Fori(0, NS) as t:
                    attn(t, 9)
                attn(NS, 1)
                barrier(act, l, 13)
                barrier(act, l, 14)

                for k in range(KT):
                    act.activation(b_hi[:, k], merged[:, k], ACT.Copy).then_inc(m_hi, 1)
                barrier(act, l, 15)

            for t in range(NT):
                act.wait_ge(f_tr, t + 1)
                if t >= 2:
                    act.wait_ge(f_y, t - 1)
                if t:
                    act.wait_ge(f_sq, t)
                act.activation(rows_wide[:], PSUM[:, 1024 * (t % 2):1024 * (t % 2) + 1024], ACT.Square,
                               accum_out=stat[:, 16 + t:17 + t]).then_inc(f_sq, 1)

        @block.gpsimd
        def _(pool):
            for b in range(2):
                pool.sem_inc(leave_free[b], 1)
                pool.sem_inc(wide_free[b], 1)
            pool.memset(minus_half[:], -0.5)
            for t in range(NT):
                pool.wait_ge(first_c, t + 1)
                pool.sem_inc(waits_held, 1)
                pool.dma_start(x_d[:, :, cols(t)].rearrange("k p t -> p k t"), x_blk[t % 2][:]).then_inc(first_out[t % 2], 16)
            pool.wait_ge(first_out[0], 80)
            pool.wait_ge(first_out[1], 64)
            first_barrier(pool)

            with pool.Fori(0, DEPTH) as l:
                barrier(pool, l, 0)
                pool.wait_ge(n_ms, l * 2 + 1)
                pool.tensor_tensor(r_tok[:], stat[:, 0:NT], minus_half[:, 0:NT], ALU.pow).then_inc(n_r, 1)
                barrier(pool, l, 1)

                base, stored = G_PROJ, 0
                for kind, pairs, col, blk in PROJ_RUNS:
                    at = SAMPLE + 1 if kind.startswith("conv") else SAMPLE

                    def body(n, p, m, j, at=at, blk=blk, st=stored):
                        for b in range(2):
                            pool.wait_ge(leave_ready[b], l * 35 + j + (st + 1))
                            pool.sem_inc(waits_held, 1)
                            pool.dma_start(proj_d[j * 2 + (blk + b), :, 0:SAMPLE], leave[b][:, 0:SAMPLE]).then_inc(leave_out[b], 16)
                            pool.dma_start(proj_d[j * 2 + (blk + b), :, SAMPLE:T], leave[b][:, at:at + PROMPT]).then_inc(leave_out[b], 16)
                            pool.wait_ge(leave_out[b], (l * 35 + j + (st + 1)) * 32)
                            pool.sem_inc(leave_free[b], 1)
                    if kind == "kv_small":
                        body(base, 0, base // 2, 0)
                    else:
                        groups(pool, base, 2 * pairs, body)
                    stored += 1 if kind == "kv_small" else 2 * pairs
                    base += 2 * pairs
                barrier(pool, l, 2)
                barrier(pool, l, 3)

                def ssm_prep(t, p, i):
                    n = l * NT + t
                    pool.wait_ge(transposed, nth(l, t, 0, 5) + 1)
                    pool.tensor_tensor(before[:], again(cst[:, C_STRICT + 1], SH), over(logd[:, t, 1, 4:20], P), ALU.mult).then_inc(sp_bwd, 1)
                    pool.wait_ge(out_ready, nth(l, t, 0, 2) + 1)
                    xh = xt[p][:, 0:D_MODEL].rearrange("p (h q) -> p h q", q=SP_)
                    pool.tensor_tensor(x_dt[1][:], xh, over(dt_[:, t, 1], SP_), ALU.mult)
                    pool.tensor_tensor(d_x[:], xh, over(rows[:, 80:96], SP_), ALU.mult)
                    pool.wait_ge(sp_e, n + 1)
                    pool.wait_ge(sp_fwd, n * 3 + 2)
                    for g in range(SG):
                        last = pool.tensor_tensor(w_b[:, 8 * g:8 * g + 8], e_ssm[:, 8 * g:8 * g + 8], again(cb[1][:, g], 8), ALU.mult)
                    last.then_inc(sp_bwd, 1)
                tiles(pool, ssm_prep)
                barrier(pool, l, 4)

                def ssm_step(t, p, i):
                    for d in range(2):
                        tt = t if isinstance(t, int) or d == 0 else (NS - 1) - t
                        pool.wait_ge(scan_in[d][p], scan_loaded(l, p, 2 * i + 2))
                        pool.sem_inc(waits_held, 1)
                        pool.wait_ge(state[d], l * 22 + (10 if isinstance(t, int) else t + 1))
                        pool.sem_inc(waits_held, 1)
                        pool.tensor_tensor(x_in[d][:], xs[d][p][:, 0:D_MODEL].rearrange("p (h q) -> p h q", q=SP_), over(dt_rest[:, d, tt], SP_), ALU.mult).then_inc(ssm_side[d], 1)
                        pool.tensor_tensor(s_kept[d][:].rearrange("p (h q) -> p h q", q=SP_), s_ssm[d][:].rearrange("p (h q) -> p h q", q=SP_), over(e_tot[:, d, tt, 4:20], SP_), ALU.mult).then_inc(ssm_side[d], 1)
                tiles(pool, ssm_step)
                barrier(pool, l, 5)

                def ssm_post(t, p, i):
                    n = l * NT + t
                    pool.wait_ge(gated, nth(l, t, 0, 3) + 1)
                    pool.tensor_tensor(yzw[:], yz[:], over(vec[:, V_SNORM:V_SNORM + 8], P), ALU.mult).then_inc(scaled, 1)
                    pool.wait_ge(lo_made, nth(l, t, 0, 3) + 1)
                tiles(pool, ssm_post)
                pool.wait_ge(n_ms, l * 2 + 2)
                pool.tensor_tensor(r_tok[:], stat[:, 0:NT], minus_half[:, 0:NT], ALU.pow).then_inc(n_r, 1)
                barrier(pool, l, 6)
                barrier(pool, l, 7)

                def gdn_prep(t, p, i):
                    pool.wait_ge(sums_made, nth(l, t, 1, 4) + 1)
                    pool.tensor_tensor(stat[:, 8:16], stat[:, 0:8], minus_half[:, 0:8], ALU.pow).then_inc(inv_rms, 1)
                tiles(pool, gdn_prep)
                barrier(pool, l, 8)

                pool.memset(o_acc[:], 0.0).then_inc(o_zero, 1)

                def gdn_step(t, p, i):
                    n = l * NT + t
                    for d in range(2):
                        tt = t if isinstance(t, int) or d == 0 else (NS - 1) - t
                        g = gd[d]
                        pool.wait_ge(scan_in[d][p], scan_loaded(l, p, 2 * (5 - p) + i + 1))
                        pool.sem_inc(waits_held, 1)
                        kind = lambda c: g_t[d][p][:, c].rearrange("p (h t) -> p h t", t=P)
                        pool.wait_ge(state[d], l * 22 + 11 + (10 if isinstance(t, int) else t + 1))
                        pool.sem_inc(waits_held, 1)
                        pool.tensor_tensor(g["VB"][:], kind(3), over(beta[:, tt, d], P), ALU.mult).then_inc(g_side[d], 1)
                        pool.tensor_tensor(g["KD"][:], kind(2), over(e_rest[:, d, tt, 0:4], P), ALU.mult).then_inc(g_side[d], 1)
                        pool.tensor_tensor(g["SK"][:], g["S"][:], over(e_tot[:, d, tt, 0:4], P), ALU.mult).then_inc(g_side[d], 1)
                    for d in range(2):
                        g = gd[d]
                        kind = lambda c: g_t[d][p][:, c].rearrange("p (h t) -> p h t", t=P)
                        pool.wait_ge(g_e[d], n + 1)
                        pool.tensor_tensor(g["A0"][:], kind(4), g["E"][:], ALU.mult).then_inc(g_side[d], 1)
                        pool.tensor_tensor(g["Q0"][:], kind(5), g["E"][:], ALU.mult)
                        pool.drain()
                        pool.tensor_tensor(g["Q"][:], g["Q0"][:], again(cst[:, C_TRI + d], GH), ALU.mult).then_inc(g_side[d], 1)
                tiles(pool, gdn_step)
                barrier(pool, l, 9)

                def gdn_post(t, p, i):
                    pool.wait_ge(sums_made, nth(l, t, 2, 4) + 1)
                    pool.tensor_tensor(stat[:, 8:12], stat[:, 0:4], minus_half[:, 0:4], ALU.pow).then_inc(inv_rms, 1)
                tiles(pool, gdn_post)
                barrier(pool, l, 10)
                barrier(pool, l, 11)

                def attn_prep(t, p, i):
                    n = l * NT + t
                    pool.wait_ge(sums_made, nth(l, t, 3, 4) + 1)
                    pool.tensor_tensor(stat[:, 16:26], stat[:, 0:10], minus_half[:, 0:10], ALU.pow).then_inc(inv_rms, 1)
                    pool.wait_ge(scaled, nth(l, t, 3, 4) + 1)
                    qk5 = qk[:].rearrange("p h (a s f) -> p h a s f", a=2, s=2)
                    t5 = a_sq[:].rearrange("p h (a s f) -> p h a s f", a=2, s=2)
                    for s in range(2):
                        sin = rope[:, t, 1].rearrange("p (a s f) -> p a s f", a=2, s=2)[:, :, s]
                        last = pool.tensor_tensor(t5[:, :, :, s], qk5[:, :, :, 1 - s], sin.unsqueeze(1).broadcast_to([P, 10, 2, 16]), ALU.mult)
                    last.then_inc(a_sin, 1)
                tiles(pool, attn_prep)
                barrier(pool, l, 12)
                barrier(pool, l, 13)
                barrier(pool, l, 14)

                for blk in range(KT):
                    b = blk % 2
                    pool.wait_ge(x_new, l * KT + blk + 1)
                    pool.sem_inc(waits_held, 1)
                    pool.dma_start(x_d[blk], wide[b][:]).then_inc(x_out[b], 16)
                    pool.wait_ge(x_out[b], l * 64 + 16 * (blk // 2) + 16)
                    pool.sem_inc(wide_free[b], 1)
                barrier(pool, l, 15)

            for t in range(NT):
                pool.wait_ge(f_ms, t + 1)
                pool.tensor_tensor(r_tok[:, t:t + 1], stat[:, 25:26], minus_half[:, 0:1], ALU.pow).then_inc(f_r, 1)

        @block.vector
        def _(dve):
            for b in range(2):
                dve.sem_inc(w_ready[b], 1)
                dve.sem_inc(acc_free[b], 1)
            dve.wait_ge(cond_th, 1)
            dve.scalar_tensor_tensor(cond[:], stat[:, 0:24], 1.0, bank(7, 24), ALU.add, ALU.mult)
            dve.drain()
            dve.tensor_scalar(cond[:], cond[:], 0.5, None, ALU.mult)
            first_barrier(dve)

            def diagonals(u):
                dve.wait_ge(n_r, u + 1)
                for t in range(NT):
                    last = dve.tensor_scalar(r_diag[:, t], ident, r_tok[:, t:t + 1], None, ALU.mult)
                last.then_inc(n_diag, 1)

            with dve.Fori(0, DEPTH) as l:
                dve.wait_ge(vec_t, l + 1)
                dve.tensor_copy(vec[:], bank(0, NV))
                dve.tensor_scalar(half_vec[:], bank(0, NV), 0.5, None, ALU.mult)
                dve.wait_ge(vec_loaded, l * (22 * 16) + 22 * 16)
                dve.tensor_scalar(qk_gain[:, 0:AH], qk_gain[:, 0:AH], AD ** -0.5, None, ALU.mult)
                dve.wait_ge(coef_e, l + 1)
                dve.tensor_scalar(coef[:], coef[:], -1.0, None, ALU.mult)
                dve.drain()
                dve.wait_ge(mod_used, l * 12 + 12)
                dve.tensor_tensor(mod[:], bank(1, 48).rearrange("p (k c) -> p k c", c=2), over(vec[:, V_BMOD:V_BMOD + 24], 2), ALU.add)
                dve.drain()
                dve.scalar_tensor_tensor(gain[:], mod[:, 8:16], 1.0, over(vec[:, 0:KT], 2), ALU.add, ALU.mult)
                dve.tensor_scalar(half_gate[:], mod[:, 16:24], 0.5, None, ALU.mult)
                barrier(dve, l, 0)

                dve.wait_ge(n_mm, l * KT + KT)
                dve.tensor_scalar(stat[:, 0:NT], bank(0, NT), 1.0 / D_MODEL, EPS, ALU.mult, ALU.add).then_inc(n_ms, 1)
                diagonals(l * 2)
                dve.wait_ge(n_row, l * 2 + 1)

                def scale_block(k):
                    for c, (lo, hi) in enumerate(((0, SAMPLE), (SAMPLE, T))):
                        last = dve.scalar_tensor_tensor(wide[k % 2][:, lo:hi], x_sb[:, k, lo:hi], gain[:, k, c:c + 1], row_bc[:, lo:hi], ALU.mult, ALU.mult)
                    last.then_inc(n_t, 1)
                scale_block(0)
                for k in range(KT):
                    dve.drain()
                    if k + 1 < KT:
                        scale_block(k + 1)
                    dve.wait_ge(n_h, l * KT + k + 1)
                    for c, (lo, hi) in enumerate(((0, SAMPLE), (SAMPLE, T))):
                        dve.scalar_tensor_tensor(h_lo[:, k, lo:hi], wide[k % 2][:, lo:hi], mod[:, k, c:c + 1], h_hi[:, k, lo:hi].bitcast(F32), ALU.add, ALU.subtract)
                barrier(dve, l, 1)

                for b in range(2):
                    for c in (0, SAMPLE + 1, T + 2):
                        dve.memset(conv_in[b][:, c:c + 1], 0.0)
                split_group(dve, l, 0, 0, 0, KT)
                split_group(dve, l, 1, 1, 0, KT)
                base, stored, conv, th = G_PROJ, 0, 0, 0
                for kind, pairs, col, blk0 in PROJ_RUNS:
                    def body(n, p, m, j, kind=kind, st=stored, cv=conv, tq=th):
                        for b in range(2):
                            if kind.startswith("conv"):
                                v0 = V_GCONV if kind == "conv_gdn" else V_SCONV
                                tap = lambda w: half_vec[:, one(j * 2 + (v0 + 12 * w + b))]
                                bias = half_vec[:, one(j * 2 + (V_SBIAS + b))] if kind == "conv_ssm" else 0.0
                                dve.wait_ge(acc_free[b], l * NG + n + 2)
                                out = conv_out[b][:, 0:T + 1]
                                dve.tensor_scalar(out, conv_in[b][:, 1:T + 2], tap(1), bias, ALU.mult, ALU.add)
                                dve.drain()
                                dve.scalar_tensor_tensor(out, conv_in[b][:, 0:T + 1], tap(0), out, ALU.mult, ALU.add)
                                dve.drain()
                                dve.scalar_tensor_tensor(out, conv_in[b][:, 2:T + 3], tap(2), out, ALU.mult, ALU.add).then_inc(conv_mid[b], 1)
                                dve.wait_ge(th_ready[b], l * 20 + j + (tq + 1))
                                dve.scalar_tensor_tensor(leave[b][:, 0:T + 1], leave[b][:, 0:T + 1], 1.0, out, ALU.add, ALU.mult).then_inc(leave_ready[b], 1)
                            elif kind == "silu":
                                dve.wait_ge(th_ready[b], l * 20 + j + (tq + 1))
                                dve.scalar_tensor_tensor(leave[b][:, 0:T], leave[b][:, 0:T], 1.0, acc(b), ALU.add, ALU.mult).then_inc(leave_ready[b], 1)
                                dve.drain().then_inc(acc_free[b], 1)
                        if isinstance(n, int) and n + 2 == 11:
                            dve.wait_ge(dt_loaded, l * 16 + 16)
                        if not (isinstance(n, int) and n + 2 >= G_SSM):
                            split_group(dve, l, n + 2, p, m + 1, KT)
                    if pairs == 1:
                        for j in range(2):
                            body(base + j, j, base // 2, j)
                    elif kind == "tanh":
                        groups(dve, base, 2 * pairs - 2, body)
                        for j in range(2):
                            body(base + 2 * pairs - 2 + j, j, base // 2 + pairs - 1, 2 * pairs - 2 + j)
                    else:
                        groups(dve, base, 2 * pairs, body)
                    stored += 1 if kind == "kv_small" else 2 * pairs
                    conv += 2 * pairs if kind.startswith("conv") else 0
                    th += 2 * pairs if kind.startswith("conv") or kind == "silu" else 0
                    base += 2 * pairs
                barrier(dve, l, 2)

                dve.wait_ge(decay_prod, l * 2 + 1)
                D = {k: v[:] for k, v in dec.items()}
                pre_ps = bank(0, 432).rearrange("p (t c) -> p t c", c=48)
                dve.tensor_copy(D["pre"][:, :, 0:8], pre_ps[:, :, 0:8])
                dve.tensor_tensor(D["pre"][:, :, 8:48], pre_ps[:, :, 8:48], again(rows[:, 40:80], NT), ALU.add)
                dve.drain()
                dve.tensor_scalar(D["neg"], D["pre"], -1.0, None, ALU.mult)
                dve.tensor_scalar(D["low"], D["pre"], 0.0, None, ALU.min)
                dve.drain()
                dve.tensor_tensor(D["neg"], D["neg"], D["pre"], ALU.min).then_inc(decay_term, 1)
                dve.wait_ge(decay_exp, l * 2 + 1)
                dve.tensor_scalar(D["u"], D["e_abs"], 2.0, None, ALU.add)
                dve.drain()
                dve.reciprocal(D["u"], D["u"])
                dve.drain()
                dve.tensor_tensor(D["s"], D["u"], D["e_abs"], ALU.mult)
                dve.drain()
                dve.tensor_tensor(D["s2"], D["s"], D["s"], ALU.mult)
                dve.drain()
                dve.tensor_scalar(D["poly"], D["s2"], 1.0 / 17.0, None, ALU.mult)
                for c in (15, 13, 11, 9, 7, 5, 3):
                    dve.drain()
                    dve.scalar_tensor_tensor(D["poly"], D["poly"], 1.0 / c, D["s2"], ALU.add, ALU.mult)
                dve.drain()
                dve.scalar_tensor_tensor(D["poly"], D["poly"], 1.0, D["s"], ALU.add, ALU.mult)
                dve.tensor_scalar(D["u"], D["pre"], 0.0, None, ALU.max)
                dve.drain()
                dve.scalar_tensor_tensor(D["soft"], D["poly"], 2.0, D["u"], ALU.mult, ALU.add)
                dve.tensor_scalar(D["s"], D["e_abs"], 1.0, None, ALU.add)
                dve.drain()
                dve.reciprocal(D["s"], D["s"])
                dve.drain()
                dve.tensor_tensor(beta[:].rearrange("p t d h -> p t (d h)"), D["e_low"][:, :, 0:8], D["s"][:, :, 0:8], ALU.mult)
                dve.tensor_copy(dt_[:].rearrange("p t d h -> p t (d h)"), D["soft"][:, :, 16:48])
                for d in range(2):
                    dve.tensor_tensor(logd[:, :, d, 0:4], D["soft"][:, :, 8 + 4 * d:12 + 4 * d], again(coef[:, d, 0:4], NT), ALU.mult)
                    last = dve.tensor_tensor(logd[:, :, d, 4:20], D["soft"][:, :, 16 + 16 * d:32 + 16 * d], again(coef[:, d, 4:20], NT), ALU.mult)
                last.then_inc(decay_term, 1)
                dve.wait_ge(decay_prod, l * 2 + 2)
                for d in range(2):
                    dve.tensor_copy(cum[:, d].rearrange("p t h -> p (t h)"), bank(1 + d, 180))
                    dve.tensor_copy(tot[:, d].rearrange("p t h -> p (t h)"), bank(3 + d, 180))
                dve.drain()
                dve.tensor_tensor(rest[:], tot[:], cum[:], ALU.subtract).then_inc(decay_term, 1)
                dve.wait_ge(decay_exp, l * 2 + 2)
                for d in range(2):
                    dve.scalar_tensor_tensor(neg_be[:, d], beta[:, :, d], -1.0, e_cum[:, d, :, 0:4], ALU.mult, ALU.mult)
                    dve.tensor_tensor(dt_rest[:, d], dt_[:, :, d], e_rest[:, d, :, 4:20], ALU.mult)
                barrier(dve, l, 3)

                def ssm_prep(t, p, i):
                    n = l * NT + t
                    dve.wait_ge(transposed, nth(l, t, 0, 5) + 1)
                    dve.tensor_tensor(after[:], again(cst[:, C_STRICT], SH), over(logd[:, t, 0, 4:20], P), ALU.mult).then_inc(sp_fwd, 1)
                    cb_ps = bank(7, 256).rearrange("p (g l) -> p g l", l=P)
                    for d in range(2):
                        last = dve.tensor_tensor(cb[d][:], cb_ps, again(cst[:, C_TRI + d], SG), ALU.mult)
                    last.then_inc(sp_fwd, 1)
                    dve.wait_ge(out_ready, nth(l, t, 0, 2) + 1)
                    dve.tensor_tensor(x_dt[0][:], xt[p][:, 0:D_MODEL].rearrange("p (h q) -> p h q", q=SP_), over(dt_[:, t, 0], SP_), ALU.mult)
                    dve.drain()
                    dve.wait_ge(sp_e, n + 1)
                    for g in range(SG):
                        last = dve.tensor_tensor(w_f[:, 8 * g:8 * g + 8], e_ssm[:, 8 * g:8 * g + 8], again(cb[0][:, g], 8), ALU.mult)
                    last.then_inc(sp_fwd, 1)
                    dve.wait_ge(sp_prod, n * 2 + 2)
                    dve.tensor_tensor(y_acc[:, t], PSUM[:, 0:D_MODEL], d_x[:].rearrange("p h q -> p (h q)"), ALU.add).then_inc(sp_yd, 1)
                tiles(dve, ssm_prep)
                barrier(dve, l, 4)

                def ssm_step(t, p, i):
                    n = l * NT + t
                    if isinstance(t, int):
                        for d in range(2):
                            dve.memset(s_ssm[d][:], 0.0).then_inc(state[d], 1)
                    for d in range(2):
                        tt = t if isinstance(t, int) or d == 0 else (NS - 1) - t
                        dve.wait_ge(ssm_prod[d], n * 2 + 1)
                        dve.sem_inc(waits_held, 1)
                        dve.tensor_tensor(y_tmp[d][:].rearrange("p (h q) -> p h q", q=SP_), PSUM[:, 2048 * d:2048 * d + 1024].rearrange("p (h q) -> p h q", q=SP_),
                                          over(e_cum[:, d, tt, 4:20], SP_), ALU.mult)
                        dve.wait_ge(ssm_prod[d], n * 2 + 2)
                        dve.sem_inc(waits_held, 1)
                        dve.wait_ge(ssm_side[d], n * 2 + 2)
                        dve.tensor_tensor(s_ssm[d][:], s_kept[d][:], PSUM[:, 2048 * d + 1024:2048 * d + 2048], ALU.add).then_inc(state[d], 1)
                        dve.drain()
                        dve.tensor_tensor(y_acc[:, tt], y_acc[:, tt], y_tmp[d][:], ALU.add)
                tiles(dve, ssm_step)
                barrier(dve, l, 5)

                def ssm_post(t, p, i):
                    n = l * NT + t
                    dve.wait_ge(tile_in[p], loaded(l, p, i, 1))
                    dve.wait_ge(transposed, nth(l, t, 1, 5) + 1)
                    dve.tensor_tensor(yz[:], PSUM[:, 0:1024].rearrange("p (k t) -> p k t", t=P), z_c[p][:], ALU.mult).then_inc(gated, 1)
                    dve.wait_ge(sums_made, nth(l, t, 0, 4) + 1)
                    dve.tensor_copy(stat[:, one(t)], bank(2, 1)).then_inc(y_ss_read, 1)
                    dve.wait_ge(hi_made, nth(l, t, 0, 3) + 1)
                    dve.tensor_tensor(b_lo[:, :, cols(t)], yzw[:], b_hi[:, :, cols(t)].bitcast(F32), ALU.subtract).then_inc(lo_made, 1)
                tiles(dve, ssm_post)
                dve.drain()
                dve.tensor_scalar(stat[:, 0:NT], stat[:, 0:NT], 1.0 / D_MODEL, 4 * EPS, ALU.mult, ALU.add).then_inc(n_ms, 1)
                diagonals(l * 2 + 1)
                barrier(dve, l, 6)

                def branch(base, kt, merge):
                    for j in range(2):
                        split_group(dve, l, base + j, j, base // 2, kt)
                    for j in range(4):
                        n, p = base + j, j % 2
                        for b in range(2):
                            dve.drain()
                            dve.wait_ge(acc_ready[b], acc_done(l, n, b))
                            dve.wait_ge(wide_in[b], l * 256 + 16 * (n - G_SSM) + 16)
                            merge(2 * j + b, b)
                        if j < 2:
                            split_group(dve, l, n + 2, p, base // 2 + 1, kt)

                def merge_first(blk, b):
                    dve.tensor_tensor(tmp[:], acc(b), row_bc[:], ALU.mult)
                    dve.drain().then_inc(acc_free[b], 1)
                    dve.scalar_tensor_tensor(merged[:, blk], wide[b][:], 1.0, tmp[:], ALU.add, ALU.mult).then_inc(wide_free[b], 1)

                def merge_more(blk, b):
                    dve.scalar_tensor_tensor(tmp[:], wide[b][:], 1.0, acc(b), ALU.add, ALU.mult)
                    dve.drain().then_inc(acc_free[b], 1)
                    dve.tensor_tensor(merged[:, blk], merged[:, blk], tmp[:], ALU.add).then_inc(wide_free[b], 1)

                def merge_out(blk, b):
                    for c, (lo, hi) in enumerate(((0, SAMPLE), (SAMPLE, T))):
                        last = dve.scalar_tensor_tensor(wide[b][:, lo:hi], acc(b)[:, lo:hi], half_gate[:, blk, c:c + 1], wide[b][:, lo:hi], ALU.mult, ALU.add)
                    last.then_inc(x_new, 1)
                    dve.drain().then_inc(acc_free[b], 1)
                branch(G_SSM, 8, merge_first)
                barrier(dve, l, 7)

                def gdn_prep(t, p, i):
                    n = l * NT + t
                    dve.wait_ge(squared, nth(l, t, 1, 4) + 1)
                    dve.tensor_reduce(stat[:, 0:8], g_sq[:], AX_X, ALU.add)
                    dve.drain()
                    dve.tensor_scalar(stat[:, 0:4], stat[:, 0:4], EPS, float(GD), ALU.add, ALU.mult)
                    dve.tensor_scalar(stat[:, 4:8], stat[:, 4:8], EPS, None, ALU.add).then_inc(sums_made, 1)
                    dve.wait_ge(inv_rms, nth(l, t, 0, 3) + 1)
                    dve.tensor_tensor(q_n[:], bank(0).rearrange("p (h d) -> p h d", d=GD), over(stat[:, 8:12], GD), ALU.mult)
                    dve.tensor_tensor(g_out[p][:, 2].rearrange("p (h d) -> p h d", d=GD), bank(1).rearrange("p (h d) -> p h d", d=GD), over(stat[:, 12:16], GD), ALU.mult).then_inc(scaled, 1)
                tiles(dve, gdn_prep)
                barrier(dve, l, 8)

                for d in range(2):
                    dve.wait_ge(state_in[d], l * 32 + 32)
                    dve.sem_inc(waits_held, 1)
                    dve.drain().then_inc(state[d], 1)
                dve.wait_ge(o_zero, l + 1)
                dve.sem_inc(waits_held, 1)

                def heads(x):
                    return x.rearrange("p (h t) -> p h t", t=P)

                def gdn_step(t, p, i):
                    n = l * NT + t
                    tile_of = lambda d: t if isinstance(t, int) or d == 0 else (NS - 1) - t
                    if isinstance(t, int):
                        for d in range(2):
                            dve.memset(gd[d]["S"][:], 0.0).then_inc(state[d], 1)
                    for d in range(2):
                        tt = tile_of(d)
                        dve.tensor_copy(gd[d]["col"][:, 0:4], over(logd[:, tt, d, 0:4], P))
                        dve.tensor_copy(gd[d]["col"][:, 4:8], over(beta[:, tt, d], P)).then_inc(g_term[d], 1)
                    for d in range(2):
                        tt = tile_of(d)
                        dve.wait_ge(g_row[d], n * 2 + 1)
                        for h in range(GH):
                            last = dve.tensor_scalar(gd[d]["E"][:, h], bank(4 * d + 3, P, h * P), cum[:, d, tt, h:h + 1], 0.0, ALU.subtract, ALU.min)
                        last.then_inc(g_term[d], 1)
                    for d in range(2):
                        dve.wait_ge(g_side[d], n * 5 + 4)
                        dve.tensor_tensor(gd[d]["A"][:], gd[d]["A0"][:], heads(bank(4 * d)), ALU.mult).then_inc(g_term[d], 1)
                    for d in range(2):
                        g = gd[d]
                        dve.drain()
                        dve.tensor_tensor(g["Y"][:], g["A"][:], again(cst[:, C_LV + 7 * (1 - d)], GH), ALU.mult)
                        dve.wait_ge(g_row[d], n * 2 + 2)
                        dve.tensor_tensor(g["X"][:], heads(bank(4 * d + 3)), again(cst[:, C_LV + 7 * d], GH), ALU.mult)
                        dve.drain()
                        dve.tensor_tensor(g["Y"][:], g["Y"][:], again(ident, GH), ALU.add)
                        dve.tensor_tensor(g["X"][:], g["X"][:], again(ident, GH), ALU.add).then_inc(g_x[d], 1)
                    for lev in range(1, 7):
                        for d in range(2):
                            dve.wait_ge(g_level[d], n * 12 + 2 * lev - 1)
                            dve.tensor_tensor(gd[d]["T"][:], heads(bank(4 * d)), again(cst[:, C_LV + 7 * d + lev], GH), ALU.mult).then_inc(g_tm[d], 1)
                    for d in range(2):
                        g, tt = gd[d], tile_of(d)
                        dve.wait_ge(g_from_s[d], n * 2 + 1)
                        dve.tensor_tensor(g["R0"][:], heads(bank(4 * d)), over(neg_be[:, d, tt], P), ALU.mult)
                        dve.drain()
                        dve.wait_ge(g_side[d], n * 5 + 1)
                        dve.tensor_tensor(g["R"][:], g["R0"][:], g["VB"][:], ALU.add).then_inc(g_term[d], 1)
                    for d in range(2):
                        g, tt = gd[d], tile_of(d)
                        dve.wait_ge(g_from_s[d], n * 2 + 2)
                        dve.tensor_tensor(g["O"][:], heads(bank(4 * d + 3)), over(e_cum[:, d, tt, 0:4], P), ALU.mult)
                        dve.drain()
                        dve.tensor_tensor(o_acc[:, tt], o_acc[:, tt], g["O"][:].rearrange("p h t -> p (h t)"), ALU.add)
                    for d in range(2):
                        g, tt = gd[d], tile_of(d)
                        dve.wait_ge(g_from_v[d], n * 2 + 1)
                        dve.wait_ge(g_side[d], n * 5 + 3)
                        dve.tensor_tensor(g["S"][:], g["SK"][:], heads(bank(4 * d)), ALU.add).then_inc(state[d], 1)
                        dve.drain()
                        dve.wait_ge(g_from_v[d], n * 2 + 2)
                        dve.tensor_tensor(o_acc[:, tt], o_acc[:, tt], bank(4 * d + 2), ALU.add).then_inc(g_step[d], 1)
                tiles(dve, gdn_step)
                barrier(dve, l, 9)

                def gdn_post(t, p, i):
                    n = l * NT + t
                    dve.wait_ge(squared, nth(l, t, 2, 4) + 1)
                    dve.tensor_reduce(stat[:, 0:4], o_sq[:], AX_X, ALU.add)
                    dve.drain()
                    dve.tensor_scalar(stat[:, 0:4], stat[:, 0:4], 1.0 / GD, EPS, ALU.mult, ALU.add).then_inc(sums_made, 1)
                    dve.wait_ge(inv_rms, nth(l, t, 1, 3) + 1)
                    dve.tensor_tensor(o_st[p][:], o_acc[:, t].rearrange("p (h d) -> p h d", d=GD), over(stat[:, 8:12], GD), ALU.mult).then_inc(scaled, 1)
                    dve.wait_ge(tile_in[p], loaded(l, p, i, 3))
                    dve.wait_ge(transposed, nth(l, t, 3, 5) + 1)
                    dve.scalar_tensor_tensor(o_z[:], heads(bank(p)), half_vec[:, V_GNORM:V_GNORM + 1], z_a[p][:], ALU.mult, ALU.mult).then_inc(gated, 1)
                    dve.wait_ge(hi_made, nth(l, t, 1, 3) + 1)
                    dve.tensor_tensor(b_lo[:, 0:4, cols(t)], o_z[:], b_hi[:, 0:4, cols(t)].bitcast(F32), ALU.subtract).then_inc(lo_made, 1)
                tiles(dve, gdn_post)
                barrier(dve, l, 10)
                branch(G_GDN, 4, merge_more)
                barrier(dve, l, 11)

                def split_k(src):
                    dve.tensor_copy(k_hh[:, :, 0:AD], src)
                    dve.tensor_copy(k_hh[:, :, AD:P], src)
                    dve.drain()
                    dve.tensor_tensor(k_ll[:, :, 0:AD], src, k_hh[:, :, 0:AD].bitcast(F32), ALU.subtract)
                    return dve.tensor_tensor(k_ll[:, :, AD:P], src, k_hh[:, :, 0:AD].bitcast(F32), ALU.subtract)

                def place_k(n, t):
                    dve.wait_ge(a_st, n + 1)
                    dve.tensor_copy(k_hi[:, :, cols(t)], bank(4)[:, 0:256].rearrange("p (g t) -> p g t", t=P))
                    dve.tensor_copy(k_lo[:, :, cols(t)], bank(4)[:, 256:512].rearrange("p (g t) -> p g t", t=P)).then_inc(a_k, 1)

                def attn_prep(t, p, i):
                    n, n1 = l * NT + t, l * (NT + 1) + t
                    ps = PSUM[:, 0:640].rearrange("p (h d) -> p h d", d=AD)
                    dve.wait_ge(squared, nth(l, t, 3, 4) + 1)
                    dve.tensor_reduce(stat[:, 0:10], a_sq[:], AX_X, ALU.add)
                    dve.drain()
                    dve.tensor_scalar(stat[:, 0:10], stat[:, 0:10], 1.0 / AD, EPS, ALU.mult, ALU.add).then_inc(sums_made, 1)
                    dve.wait_ge(inv_rms, nth(l, t, 2, 3) + 1)
                    dve.wait_ge(a_v, n + 1)
                    dve.tensor_tensor(qk[:], ps, over(stat[:, 16:26], AD), ALU.mult)
                    dve.drain()
                    dve.tensor_tensor(qk[:], qk[:], qk_gain[:], ALU.mult).then_inc(scaled, 1)
                    dve.drain()
                    dve.tensor_tensor(qk_c[:], qk[:], again(rope[:, t, 0], 10), ALU.mult)
                    dve.drain()
                    dve.wait_ge(a_sin, n + 1)
                    dve.tensor_tensor(qk[:], qk_c[:], a_sq[:], ALU.add).then_inc(qk_done, 1)
                    dve.drain()
                    dve.tensor_copy(q_hl[:, :, 0:AD], qk[:, 0:AH])
                    dve.drain()
                    dve.tensor_tensor(q_hl[:, :, AD:P], qk[:, 0:AH], q_hl[:, :, 0:AD].bitcast(F32), ALU.subtract)
                    split_k(qk[:, AH:10]).then_inc(a_split, 1)
                    place_k(n1, t)
                tiles(dve, attn_prep)
                dve.wait_ge(past_in, l * 32 + 32)
                split_k(ain[1][:, 0].rearrange("p (g d) -> p g d", d=AD)).then_inc(a_split, 1)
                place_k(l * (NT + 1) + NT, NT)
                barrier(dve, l, 12)

                def attn(t, nk):
                    n, ns = l * NT + t, l * NS + t
                    dve.tensor_copy(q_now[:], q_stack[:, t]).then_inc(q_set, 1)

                    def head_max(h):
                        dve.wait_ge(at_s, n * AH + h + 1)
                        dve.tensor_reduce(stat[:, h:h + 1], PSUM[:, 1536 * (h % 2):1536 * (h % 2) + nk * P], AX_X, ALU.max, negate=True).then_inc(at_m, 1)
                    head_max(0)
                    for h in range(AH):
                        s = h % 2
                        if h + 1 < AH:
                            head_max(h + 1)
                        dve.wait_ge(at_t[0], n * AH + h + 1)
                        w = min(nk, 4)
                        dve.tensor_copy(prob_t[s][:, 0:w], bank(6, w * P).rearrange("p (j t) -> p j t", t=P)).then_inc(at_c[0], 1)
                        if nk > 1:
                            dve.wait_ge(at_t[2], ns * AH + h + 1)
                            dve.tensor_copy(prob_t[s][:, 8], bank(6, P)).then_inc(at_c[2], 1)
                    dve.wait_ge(at_v, n * AH + AH)
                    dve.reciprocal(stat[:, 16:24], stat[:, 8:16])
                    dve.drain()
                    dve.tensor_scalar(stat[:, 16:24], stat[:, 16:24], 0.5, None, ALU.mult)
                    dve.drain()
                    for s in range(2):
                        last = dve.tensor_tensor(o_att[:, s:AH:2], PSUM[:, 1536 * s + T:1536 * s + T + 256].rearrange("p (h d) -> p h d", d=AD),
                                                 over(stat[:, 16 + s:24:2], AD), ALU.mult)
                    last.then_inc(o_norm, 1)
                    dve.wait_ge(zb_in, n * 16 + 16)
                    dve.wait_ge(o_tr, n + 1)
                    dve.tensor_tensor(o_bz[:], heads(bank(6)), z_b[:], ALU.mult).then_inc(gated, 1)
                    dve.wait_ge(hi_made, nth(l, t, 2, 3) + 1)
                    dve.tensor_tensor(b_lo[:, 0:4, cols(t)], o_bz[:], b_hi[:, 0:4, cols(t)].bitcast(F32), ALU.subtract).then_inc(lo_made, 1)
                with dve.Fori(0, NS) as t:
                    attn(t, 9)
                attn(NS, 1)
                barrier(dve, l, 13)
                branch(G_ATT, 4, merge_more)
                barrier(dve, l, 14)

                for k in range(KT):
                    dve.wait_ge(m_hi, l * KT + k + 1)
                    dve.tensor_tensor(b_lo[:, k], merged[:, k], b_hi[:, k].bitcast(F32), ALU.subtract).then_inc(m_lo, 1)
                branch(G_OUT, 8, merge_out)
                barrier(dve, l, 15)

            dve.wait_ge(f_in, 16)
            for t in range(NT):
                dve.wait_ge(f_sq, t + 1)
                dve.tensor_scalar(stat[:, 25:26], stat[:, 16 + t:17 + t], 1.0 / D_MODEL, EPS, ALU.mult, ALU.add).then_inc(f_ms, 1)
                dve.wait_ge(f_r, t + 1)
                if t >= 2:
                    dve.wait_ge(f_out[t % 2], 16 * (t // 2))
                dve.scalar_tensor_tensor(x_tok[t % 2][:], PSUM[:, 1024 * (t % 2):1024 * (t % 2) + 1024], r_tok[:, t:t + 1], f_gain[:], ALU.mult, ALU.mult).then_inc(f_y, 1)


_INS = ["x_prompt", "x_sample", "cache_k", "cache_v", "state_gdn", "state_ssm", "c", "c_ctx", "norm_w", "w_mod",
        "b_mod", "w_in", "gdn_conv_w", "gdn_a_log", "gdn_dt_bias", "gdn_norm_w", "attn_q_norm", "attn_k_norm",
        "ssm_conv_w", "ssm_conv_b", "ssm_a_log", "ssm_dt_bias", "ssm_d", "ssm_norm_w", "w_branch_a", "w_branch_b",
        "w_branch_c", "w_out", "final_norm_w"]
_OUTS = [("y_prompt", (1, PROMPT, D_MODEL)), ("y_sample", (1, SAMPLE, D_MODEL)),
         ("cache_k", (1, DEPTH, PROMPT, KVH, AD)), ("cache_v", (1, DEPTH, PROMPT, KVH, AD)),
         ("state_gdn", (1, DEPTH, 2, GH, GD, GD)), ("state_ssm", (1, DEPTH, 2, SH, SP_, SN))]


def kernel(**inputs):
    import numpy as _np
    import concourse.bacc as _bacc
    from concourse.bass_utils import run_bass_kernel_spmd as _run

    nc = _bacc.Bacc("TRN2", target_bir_lowering=False, num_devices=1)
    arrays, ins, outs = {}, {}, {}
    for name in _INS:
        arrays[f"in_{name}"] = _np.ascontiguousarray(inputs[name])
        ins[name] = nc.dram_tensor(f"in_{name}", arrays[f"in_{name}"].shape, F32, kind="ExternalInput").ap()
    tables = []
    for name, a in zip(("table", "rope_table"), constants()):
        arrays[name] = a
        tables.append(nc.dram_tensor(name, a.shape, F32, kind="ExternalInput").ap())
    for name, shape in _OUTS:
        outs[name] = nc.dram_tensor(f"out_{name}", shape, F32, kind="ExternalOutput").ap()
    backbone_kernel(nc, ins, outs, *tables)
    r = _run(nc, [arrays], core_ids=[0])
    return tuple(r.results[0][f"out_{name}"] for name, _ in _OUTS)
```

```python
from contextlib import ExitStack

import numpy as np

import concourse.bass as bass
from concourse import mybir

ALU = mybir.AluOpType
ACT = mybir.ActivationFunctionType
F32 = mybir.dt.float32
F32R = mybir.dt.float32r
AX_X = mybir.AxisListType.X

P = 128
DEPTH = 2
D_MODEL = 1024
KT = D_MODEL // P
SAMPLE = 1024
PROMPT = 128
T = SAMPLE + PROMPT
NT = T // P
NS = SAMPLE // P
EPS = 1e-6
GH, GD = 4, 128
AH, KVH, AD = 8, 2, 64
SH, SP_, SG, SN = 16, 64, 2, 128
PAST = 128
IN_WIDTH = 9008
GW = 256
THIRD = T // 3

PROJ_RUNS = (
    ("conv_gdn", 3, 0, 0),
    ("silu", 1, 1536, 12),
    ("plain", 1, 2064, 16),
    ("kv_small", 1, 2576, 20),
    ("silu", 1, 2832, 22),
    ("conv_ssm", 3, 3344, 26),
    ("silu", 2, 4880, 38),
    ("tanh", 6, 5936, 46),
)
BETA_COL, DT_COL = 2048, 5904
NB_PROJ = 70
B_GDN, B_ZA, B_ATT, B_ZB, B_XBC, B_ZC, B_GATE = 0, 12, 16, 22, 26, 38, 46
G_PROJ, G_SSM, G_GDN, G_ATT, G_OUT, NG = 0, 36, 40, 44, 48, 52

V_NORM, V_BMOD, V_GCONV, V_SCONV, V_SBIAS, V_SNORM, V_GNORM, NV = 0, 8, 32, 68, 104, 116, 124, 125

LEVELS = (1, 2, 4, 8, 16, 32, 64)
C_ID, C_TRI, C_STRICT, C_ONE, C_LV = 0, 1, 3, 5, 6
NC_ = 6 + 2 * len(LEVELS)
NPH = 15


def constants():
    i = np.arange(P)
    t = np.zeros((P, NC_, P), np.float32)
    t[:, C_ID] = np.eye(P)
    t[:, C_TRI] = i[:, None] <= i[None, :]
    t[:, C_TRI + 1] = i[:, None] >= i[None, :]
    t[:, C_STRICT] = i[:, None] > i[None, :]
    t[:, C_STRICT + 1] = i[:, None] < i[None, :]
    t[:, C_ONE] = 1.0
    for n, b in enumerate(LEVELS):
        r, c = i[:, None] // b, i[None, :] // b
        t[:, C_LV + n] = -1.0 * ((r % 2 == 1) & (c == r - 1))
        t[:, C_LV + len(LEVELS) + n] = t[:, C_LV + n].T
    rot = AD // 2
    freqs = 10000.0 ** (-np.arange(rot // 2, dtype=np.float32) / (rot // 2))
    pos = np.arange(SAMPLE)
    cs = np.zeros((T, 2, 2, 2, rot // 2), np.float32)
    cs[:, 0] = 1.0
    for axis, x in enumerate((pos // 64, pos % 64)):
        ang = x.astype(np.float32)[:, None] * freqs.astype(np.float32)
        cs[:SAMPLE, 0, axis, 0] = cs[:SAMPLE, 0, axis, 1] = np.cos(ang)
        cs[:SAMPLE, 1, axis, 0] = -np.sin(ang)
        cs[:SAMPLE, 1, axis, 1] = np.sin(ang)
    cs = cs.reshape(NT, P, 2 * AD).transpose(1, 0, 2)
    return t.reshape(P, NC_ * P), np.ascontiguousarray(cs).reshape(P, NT * 2 * AD)


def over(ap, n):
    return ap.unsqueeze(2).broadcast_to([ap.shape[0], ap.shape[1], n])


def again(ap, n):
    return ap.unsqueeze(1).broadcast_to([ap.shape[0], n, ap.shape[1]])


def backbone_kernel(nc, A, O, table, rope_table):
    with ExitStack() as ctx:
        sem_of = {}

        def sem(name):
            if name not in sem_of:
                sem_of[name] = ctx.enter_context(nc.semaphore(name))
            return sem_of[name]

        def dram(name, shape):
            return nc.dram_tensor(name, shape, F32, kind="Internal").ap()

        x_d = dram("x_d", [KT, P, T])
        proj_d = dram("proj_d", [NB_PROJ, P, T])
        ssm_tok_d = dram("ssm_tok_d", [NT, P, 1280])
        gdn_tile_d = dram("gdn_tile_d", [NT, P, 6, 512])

        base = 16512
        top = [base]

        def fixed(name, shape, dt=F32):
            size = int(np.prod(shape[1:])) * 4
            t = nc.alloc_sbuf_tensor_at(name, shape, dt, offset=top[0])
            top[0] += (size + 31) // 32 * 32
            return t

        def region(size):
            start = top[0]
            top[0] += size
            return [start, start, start + size]

        def place(r, name, shape, dt=F32):
            size = (int(np.prod(shape[1:])) * 4 + 31) // 32 * 32
            assert r[1] + size <= r[2], (name, r, size)
            t = nc.alloc_sbuf_tensor_at(name, shape, dt, offset=r[1])
            r[1] += size
            return t

        def fresh(r):
            return [r[0], r[0], r[2]]

        cst = fixed("cst", [P, NC_, P])
        rope = fixed("rope", [P, NT, 2, AD])
        cond = fixed("cond", [P, 24])
        vec = fixed("vec", [P, NV])
        half_vec = fixed("half_vec", [P, NV])
        mod = fixed("mod", [P, 24, 2])
        gain = fixed("gain", [P, KT, 2])
        half_gate = fixed("half_gate", [P, KT, 2])
        rows = fixed("rows", [P, 96])
        coef = fixed("coef", [P, 2, 20])
        qk_gain = fixed("qk_gain", [P, 10, AD])
        beta = fixed("beta", [P, NT, 2, GH])
        dt_ = fixed("dt_", [P, NT, 2, SH])
        logd = fixed("logd", [P, NT, 2, 20])
        cum = fixed("cum", [P, 2, NT, 20])
        tot = fixed("tot", [P, 2, NT, 20])
        e_cum = fixed("e_cum", [P, 2, NT, 20])
        e_tot = fixed("e_tot", [P, 2, NT, 20])
        e_rest = fixed("e_rest", [P, 2, NT, 20])
        neg_be = fixed("neg_be", [P, 2, NT, GH])
        dt_rest = fixed("dt_rest", [P, 2, NT, SH])
        stat = fixed("stat", [P, 32])
        minus_half = fixed("minus_half", [P, 16])
        r_tok = fixed("r_tok", [P, NT])

        ACTV = region(2 * KT * T * 4)
        MRG = region(KT * T * 4)
        WT = region(6 * KT * GW * 4)
        EV = region(229344 - top[0])
        a = fresh(ACTV)
        h_hi = place(a, "h_hi", [P, KT, T], F32R)
        h_lo = place(a, "h_lo", [P, KT, T], F32R)
        a = fresh(ACTV)
        b_hi = place(a, "b_hi", [P, KT, T], F32R)
        b_lo = place(a, "b_lo", [P, KT, T], F32R)
        a = fresh(WT)
        w_raw = [place(a, f"w_raw{n}", [P, KT, GW]) for n in range(2)]
        w_hi = [place(a, f"w_hi{n}", [P, KT, GW], F32R) for n in range(2)]
        w_lo = [place(a, f"w_lo{n}", [P, KT, GW], F32R) for n in range(2)]
        a = fresh(MRG)
        merged = place(a, "merged", [P, KT, T])
        a = fresh(MRG)
        x_sb = place(a, "x_sb", [P, KT, T])
        a = fresh(MRG)
        CW = T + 4
        conv_in = [place(a, f"conv_in{n}", [P, CW]) for n in range(2)]
        conv_out = [place(a, f"conv_out{n}", [P, CW]) for n in range(2)]
        leave = [place(a, f"leave{n}", [P, CW]) for n in range(2)]
        a = fresh(EV)
        row_bc = place(a, "row_bc", [P, T])
        wide = [place(a, f"wide{n}", [P, T]) for n in range(2)]
        at_tmp = list(a)
        tmp = place(a, "tmp", [P, T])
        vec_in = place(a, "vec_in", [P, P])

        a = fresh(ACTV)
        xin = [place(a, f"xin{n}", [P, 12, P]) for n in range(2)]
        xt = [place(a, f"xt{n}", [P, 1280]) for n in range(2)]
        after = place(a, "after", [P, SH, P])
        before = place(a, "before", [P, SH, P])
        e_ssm = place(a, "e_ssm", [P, SH, P])
        w_f = place(a, "w_f", [P, SH, P])
        a2 = fresh(WT)
        w_b = place(a2, "w_b", [P, SH, P])
        x_dt = [place(a2, f"x_dt{n}", [P, SH, SP_]) for n in range(2)]
        d_x = place(a2, "d_x", [P, SH, SP_])
        cb = [place(a2, f"cb{n}", [P, SG, P]) for n in range(2)]
        a = fresh(MRG)
        y_acc = place(a, "y_acc", [P, NT, D_MODEL])
        a = fresh(ACTV)
        xs = [[place(a, f"xs{d}{n}", [P, 1280]) for n in range(2)] for d in range(2)]
        c_t = [[place(a, f"c_t{d}{n}", [P, SG, P]) for n in range(2)] for d in range(2)]
        s_ssm = [place(a, f"s_ssm{d}", [P, D_MODEL]) for d in range(2)]
        s_kept = [place(a, f"s_kept{d}", [P, D_MODEL]) for d in range(2)]
        x_in = [place(a, f"x_in{d}", [P, SH, SP_]) for d in range(2)]
        y_tmp = [place(a, f"y_tmp{d}", [P, D_MODEL]) for d in range(2)]
        s_io = [place(a, f"s_io{d}", [P, 8, P]) for d in range(2)]
        a = fresh(WT)
        y_st = [place(a, f"y_st{n}", [P, D_MODEL]) for n in range(2)]
        z_c = [place(a, f"z_c{n}", [P, KT, P]) for n in range(2)]
        yz = place(a, "yz", [P, KT, P])
        yzw = place(a, "yzw", [P, KT, P])
        y_sq = place(a, "y_sq", [P, KT, P])
        a = fresh(ACTV)
        gin = [place(a, f"gin{n}", [P, 12, P]) for n in range(2)]
        g_sq = place(a, "g_sq", [P, 8, GD])
        q_n = place(a, "q_n", [P, GH, GD])
        g_out = [place(a, f"g_out{n}", [P, 6, 512]) for n in range(2)]
        a = fresh(WT)
        g_t = [[place(a, f"g_t{d}{n}", [P, 6, 512]) for n in range(2)] for d in range(2)]
        a = fresh(ACTV)
        gd = []
        for d in range(2):
            g = {"col": place(a, f"col{d}", [P, 8, P])}
            for n in ("E", "Q0", "Q", "A0", "A", "T", "X", "Y", "VB", "R0", "R", "V", "KD", "SK", "S", "O"):
                g[n] = place(a, f"g_{n}{d}", [P, GH, GD])
            gd.append(g)
        a = fresh(EV)
        o_acc = place(a, "o_acc", [P, NT, 512])
        a = fresh(WT)
        o_st = [place(a, f"o_st{n}", [P, GH, GD]) for n in range(2)]
        z_a = [place(a, f"z_a{n}", [P, GH, P]) for n in range(2)]
        o_sq = place(a, "o_sq", [P, GH, GD])
        o_z = place(a, "o_z", [P, GH, P])
        a = fresh(WT)
        q_stack = place(a, "q_stack", [P, NT, AH, P], F32R)
        q_now = [place(a, f"q_now{n}", [P, AH, P], F32R) for n in range(2)]
        o_att = place(a, "o_att", [P, AH, AD])
        half = ACTV[0] + 4 * T * 4
        a = [half, half, half + 4 * T * 4]
        k_hi = place(a, "k_hi", [P, KVH, 10 * P], F32R)
        v_all = place(a, "v_all", [P, 10, P])
        half = ACTV[0] + 12 * T * 4
        a = [half, half, half + 4 * T * 4]
        k_lo = place(a, "k_lo", [P, KVH, 10 * P], F32R)
        z_b = place(a, "z_b", [P, 4, P])
        o_bz = place(a, "o_bz", [P, 4, P])
        row_max = place(a, "row_max", [P, 2, AH])
        row_sum = place(a, "row_sum", [P, 2, AH])
        inv_sum = place(a, "inv_sum", [P, AH])
        a = fresh(EV)
        ain = [place(a, f"ain{n}", [P, 6, P]) for n in range(2)]
        a_sq = place(a, "a_sq", [P, 10, AD])
        qk = place(a, "qk", [P, 10, AD])
        qk_c = place(a, "qk_c", [P, 10, AD])
        q_hl = place(a, "q_hl", [P, AH, P], F32R)
        k_hh = place(a, "k_hh", [P, KVH, P], F32R)
        k_ll = place(a, "k_ll", [P, KVH, P], F32R)
        a = fresh(EV)
        prob = [place(a, f"prob{n}", [P, T]) for n in range(2)]
        prob_t = [place(a, f"prob_t{n}", [P, 9, P]) for n in range(2)]
        a = fresh([ACTV[2] - 12288, 0, ACTV[2]])
        mod_rows = place(a, "mod_rows", [P, 3 * D_MODEL])
        a = fresh(WT)
        w_mod = [place(a, f"w_mod{n}", [P, KT, 2 * GW]) for n in range(3)]
        a = fresh(WT)
        x_tok = [place(a, f"x_tok{n}", [P, D_MODEL]) for n in range(2)]
        x_blk = [place(a, f"x_blk{n}", [P, KT, P]) for n in range(2)]
        f_gain = place(a, "f_gain", [P, D_MODEL])
        rows_wide = place(a, "rows_wide", [P, D_MODEL])
        rows_in = place(a, "rows_in", [P, P])
        dec = {}
        a = fresh(ACTV)
        for n in ("pre", "neg", "low", "e_abs", "e_low", "u", "s", "s2", "poly", "soft"):
            dec[n] = place(a, f"dec_{n}", [P, NT, 48])
        r_diag = place(at_tmp, "r_diag", [P, NT, P])
        rest = place(a, "rest", [P, 2, NT, 20])

        PSUM = ctx.enter_context(nc.psum_tensor("PSUM", [P, 4096], F32))

        def bank(n, width=512, at=0):
            return PSUM[:, 512 * n + at:512 * n + at + width]

        def acc(b):
            return PSUM[:, 1536 * b:1536 * b + 1536].rearrange("p (c n) -> p c n", n=512)[:, :, 0:THIRD]

        def thirds(x):
            return x.rearrange("p (c n) -> p c n", n=THIRD)

        ident = cst[:, C_ID]
        ones = cst[:, C_ONE]
        block = ctx.enter_context(nc.Block())
        phase_done = sem("phase_done")

        waits_held = sem("waits_held")

        cst_in = sem("cst_in")
        first_t = sem("first_t")
        first_c = sem("first_c")
        cond_t = sem("cond_t")
        cond_th = sem("cond_th")
        vec_loaded = sem("vec_loaded")
        vec_t = sem("vec_t")
        coef_e = sem("coef_e")
        mod_used = sem("mod_used")
        mod_row = sem("mod_row")
        mod_col = sem("mod_col")
        n_add = sem("n_add")
        x_in_sb = sem("x_in_sb")
        n_sq = sem("n_sq")
        n_mm = sem("n_mm")
        n_ms = sem("n_ms")
        n_r = sem("n_r")
        n_diag = sem("n_diag")
        n_bc = sem("n_bc")
        n_row = sem("n_row")
        n_t = sem("n_t")
        n_h = sem("n_h")
        dt_loaded = sem("dt_loaded")
        decay_prod = sem("decay_prod")
        decay_term = sem("decay_term")
        decay_exp = sem("decay_exp")
        sp_prod = sem("sp_prod")
        sp_fwd = sem("sp_fwd")
        sp_bwd = sem("sp_bwd")
        sp_e = sem("sp_e")
        sp_yd = sem("sp_yd")
        sp_y = sem("sp_y")
        sp_dx = sem("sp_dx")
        states_out = sem("states_out")
        y_copied = sem("y_copied")
        y_ss_read = sem("y_ss_read")
        transposed = sem("transposed")
        squared = sem("squared")
        sums_made = sem("sums_made")
        inv_rms = sem("inv_rms")
        scaled = sem("scaled")
        gated = sem("gated")
        hi_made = sem("hi_made")
        lo_made = sem("lo_made")
        out_ready = sem("out_ready")
        tile_stored = sem("tile_stored")
        gp_c = sem("gp_c")
        gp_k = sem("gp_k")
        gp_tt = sem("gp_tt")
        o_zero = sem("o_zero")
        a_v = sem("a_v")
        a_split = sem("a_split")
        a_st = sem("a_st")
        a_k = sem("a_k")
        a_q = sem("a_q")
        a_sin = sem("a_sin")
        qk_done = sem("qk_done")
        past_in = sem("past_in")
        kv_out = sem("kv_out")
        q_set = sem("q_set")
        at_s = sem("at_s")
        at_m = sem("at_m")
        at_e = sem("at_e")
        at_v = sem("at_v")
        o_norm = sem("o_norm")
        o_tr = sem("o_tr")
        zb_in = sem("zb_in")
        m_hi = sem("m_hi")
        m_lo = sem("m_lo")
        x_new = sem("x_new")
        f_in = sem("f_in")
        f_tr = sem("f_tr")
        f_sq = sem("f_sq")
        f_ms = sem("f_ms")
        f_r = sem("f_r")
        f_y = sem("f_y")
        tok_in = [sem(f"tok_in{i}") for i in range(2)]
        first_out = [sem(f"first_out{i}") for i in range(2)]
        f_out = [sem(f"f_out{i}") for i in range(2)]
        w_loaded = [sem(f"w_loaded{i}") for i in range(2)]
        w_ready = [sem(f"w_ready{i}") for i in range(2)]
        acc_ready = [sem(f"acc_ready{i}") for i in range(2)]
        acc_free = [sem(f"acc_free{i}") for i in range(2)]
        conv_mid = [sem(f"conv_mid{i}") for i in range(2)]
        th_ready = [sem(f"th_ready{i}") for i in range(2)]
        leave_free = [sem(f"leave_free{i}") for i in range(2)]
        leave_ready = [sem(f"leave_ready{i}") for i in range(2)]
        leave_out = [sem(f"leave_out{i}") for i in range(2)]
        wide_free = [sem(f"wide_free{i}") for i in range(2)]
        wide_in = [sem(f"wide_in{i}") for i in range(2)]
        x_out = [sem(f"x_out{i}") for i in range(2)]
        tile_in = [sem(f"tile_in{i}") for i in range(2)]
        state_in = [sem(f"state_in{i}") for i in range(2)]
        ssm_s_t = [sem(f"ssm_s_t{i}") for i in range(2)]
        state = [sem(f"state{i}") for i in range(2)]
        ssm_s_out = [sem(f"ssm_s_out{i}") for i in range(2)]
        ssm_prod = [sem(f"ssm_prod{i}") for i in range(2)]
        ssm_side = [sem(f"ssm_side{i}") for i in range(2)]
        g_term = [sem(f"g_term{i}") for i in range(2)]
        g_row = [sem(f"g_row{i}") for i in range(2)]
        g_e = [sem(f"g_e{i}") for i in range(2)]
        g_x = [sem(f"g_x{i}") for i in range(2)]
        g_level = [sem(f"g_level{i}") for i in range(2)]
        g_tm = [sem(f"g_tm{i}") for i in range(2)]
        g_from_s = [sem(f"g_from_s{i}") for i in range(2)]
        g_side = [sem(f"g_side{i}") for i in range(2)]
        g_from_v = [sem(f"g_from_v{i}") for i in range(2)]
        g_v = [sem(f"g_v{i}") for i in range(2)]
        g_vc = [sem(f"g_vc{i}") for i in range(2)]
        g_step = [sem(f"g_step{i}") for i in range(2)]
        at_t = [sem(f"at_t{i}") for i in range(2)]
        at_c = [sem(f"at_c{i}") for i in range(2)]
        mod_in = [sem(f"mod_in{i}") for i in range(3)]
        scan_in = [[sem(f"scan_in{d}{i}") for i in range(2)] for d in range(2)]

        def barrier(e, l, k):
            e.sem_inc(waits_held, 1)
            e.drain().then_inc(phase_done, 1)
            e.wait_ge(phase_done, l * 5 * NPH + 5 * (k + 2))
            e.sem_inc(waits_held, 1)

        def first_barrier(e):
            e.drain().then_inc(phase_done, 1)
            e.wait_ge(phase_done, 5)

        def tiles(e, body):
            with e.Fori(0, NT // 2) as i:
                for p in range(2):
                    body(i * 2 + p, p, i)
            body(NT - 1, 0, NT // 2)

        def cols(t):
            return slice(t * P, t * P + P) if isinstance(t, int) else bass.ds(t * P, P)

        def one(c):
            return slice(c, c + 1) if isinstance(c, int) else bass.ds(c, 1)

        def nth(l, t, k, of):
            return (l * of + k) * NT + t

        def loaded(l, p, i, k):
            return ((l * 5 + k) * (5 - p) + i + 1) * 16

        def scan_loaded(l, p, count):
            return (l * 3 * (5 - p) + count) * 16

        def split_count(l, m):
            return l * (NG // 2) + m

        def load_group(sp, l, p, m, src):
            sp.wait_ge(w_ready[p], split_count(l, m) + 1)
            sp.dma_start(w_raw[p][:, 0:src.shape[1], 0:src.shape[2]], src).then_inc(w_loaded[p], 16)

        def split_group(dve, l, n, p, m, kt):
            dve.wait_ge(w_loaded[p], 16 * split_count(l, m) + 16)
            dve.wait_ge(acc_ready[1], l * NG + n + 1)
            dve.tensor_copy(w_hi[p][:, 0:kt], w_raw[p][:, 0:kt])
            dve.drain()
            dve.tensor_tensor(w_lo[p][:, 0:kt], w_raw[p][:, 0:kt], w_hi[p][:, 0:kt].bitcast(F32),
                              ALU.subtract).then_inc(w_ready[p], 1)

        def multiply_group(pe, l, n, p, m, kt, x_hi, x_lo):
            pe.wait_ge(w_ready[p], split_count(l, m) + 2)
            for b in range(2):
                pe.wait_ge(acc_free[b], l * NG + n + 1)
                for c in range(3):
                    lo, hi = c * THIRD, (c + 1) * THIRD
                    dst = bank(3 * b + c, THIRD)
                    for k in range(kt):
                        wh = w_hi[p][:, k, b * P:b * P + P]
                        wl = w_lo[p][:, k, b * P:b * P + P]
                        pe.matmul(dst, wh, x_hi[:, k, lo:hi], start=(k == 0), stop=False)
                        pe.matmul(dst, wh, x_lo[:, k, lo:hi], start=False, stop=False)
                        last = pe.matmul(dst, wl, x_hi[:, k, lo:hi], start=False, stop=(k == kt - 1))
                last.then_inc(acc_ready[b], 1)

        def acc_done(l, n, b):
            return l * NG + n + 1 + (2 if b else 0)

        def groups(e, base, count, body):
            with e.Fori(0, count // 2) as i:
                for p in range(2):
                    body(i * 2 + (base + p), p, i + base // 2, i * 2 + p)

        @block.sync
        def _(sp):
            sp.dma_start(cst[:], table.rearrange("p (c n) -> p c n", n=P)).then_inc(cst_in, 16)
            sp.dma_start(rope[:], rope_table.rearrange("p (t a d) -> p t a d", t=NT, a=2)).then_inc(cst_in, 16)
            sp.dma_start(rows_in[0:8], A["c"].rearrange("b (k p) -> (b k) p", p=P)).then_inc(cst_in, 16)
            sp.dma_start(rows_in[8:16], A["c_ctx"].rearrange("(k p) -> k p", p=P)).then_inc(cst_in, 16)
            sp.dma_start(rows_in[16:24], A["final_norm_w"].rearrange("(k p) -> k p", p=P)).then_inc(cst_in, 16)
            xsm = A["x_sample"].rearrange("b t d -> (b t) d")
            for t in range(NT):
                if t >= 2:
                    sp.wait_ge(first_t, t - 1)
                src = xsm[t * P:(t + 1) * P] if t < NS else A["x_prompt"].rearrange("b t d -> (b t) d")
                sp.dma_start(x_tok[t % 2][:], src).then_inc(tok_in[t % 2], 16)
            first_barrier(sp)

            with sp.Fori(0, DEPTH) as l:
                for k in range(KT):
                    sp.dma_start(x_sb[:, k], x_d[k]).then_inc(x_in_sb, 16)
                wm = A["w_mod"][l].rearrange("(k p) n -> p k n", p=P)
                for g in range(6):
                    if g >= 3:
                        sp.wait_ge(mod_used, l * 6 + g - 2)
                    sp.dma_start(w_mod[g % 3][:], wm[:, :, g * 2 * GW:(g + 1) * 2 * GW]).then_inc(mod_in[g % 3], 16)
                barrier(sp, l, 0)

                win = A["w_in"][l].rearrange("(k p) n -> p k n", p=P)
                base = G_PROJ
                for kind, pairs, col, _ in PROJ_RUNS:
                    if kind == "kv_small":
                        load_group(sp, l, 0, base // 2, win[:, :, col:col + GW])
                        load_group(sp, l, 1, base // 2, win[:, :, BETA_COL:BETA_COL + 16])
                        sp.dma_start(w_raw[1][:, :, P:P + 32], win[:, :, DT_COL:DT_COL + 32]).then_inc(dt_loaded, 16)
                    else:
                        groups(sp, base, 2 * pairs, lambda n, p, m, j: load_group(
                            sp, l, p, m, win[:, :, bass.ds(j * GW + col, GW)]))
                    base += 2 * pairs
                barrier(sp, l, 1)
                barrier(sp, l, 2)

                def xin_load(t, p):
                    sp.dma_start(xin[p][:], proj_d[B_XBC:B_XBC + 12, :, cols(t)].rearrange("k p t -> p k t")).then_inc(tile_in[p], 16)

                def xt_store(t, p):
                    sp.wait_ge(out_ready, nth(l, t, 0, 2) + 1)
                    sp.dma_start(ssm_tok_d[t], xt[p][:]).then_inc(tile_stored, 16)
                    sp.wait_ge(tile_stored, nth(l, t, 0, 2) * 16 + 16)
                    sp.sem_inc(waits_held, 1)
                xin_load(0, 0)
                xin_load(1, 1)
                with sp.Fori(0, 3) as i:
                    for p in range(2):
                        xt_store(i * 2 + p, p)
                        xin_load(i * 2 + (p + 2), p)
                xt_store(6, 0)
                xin_load(8, 0)
                xt_store(7, 1)
                xt_store(8, 0)
                barrier(sp, l, 3)

                def scan_tile(i, d):
                    if isinstance(i, int) and i == NS:
                        return NS
                    return i if d == 0 else (NS - 1) - i

                def ssm_loads(i, p):
                    for d in range(2):
                        t = scan_tile(i, d)
                        sp.dma_start(xs[d][p][:], ssm_tok_d[t]).then_inc(scan_in[d][p], 16)
                        sp.dma_start(c_t[d][p][:], proj_d[B_XBC + 10:B_XBC + 12, :, cols(t)].rearrange("k p t -> p k t")).then_inc(scan_in[d][p], 16)
                for d in range(2):
                    sp.dma_start(s_io[d][:], A["state_ssm"][0, l, d].rearrange("(b h) p n -> (h p) b n", h=2)).then_inc(state_in[d], 16)
                ssm_loads(0, 0)
                ssm_loads(1, 1)
                with sp.Fori(0, 3) as i:
                    for p in range(2):
                        for d in range(2):
                            sp.wait_ge(state[d], i * 2 + (l * 22 + p + 2))
                        ssm_loads(i * 2 + (p + 2), p)
                for d in range(2):
                    sp.wait_ge(state[d], l * 22 + 8)
                ssm_loads(NS, 0)
                for d in range(2):
                    sp.wait_ge(ssm_s_out[d], l + 1)
                    sp.dma_start(O["state_ssm"][0, l, d].rearrange("(b h) p n -> (h p) b n", h=2), s_io[d][:]).then_inc(states_out, 16)
                sp.wait_ge(states_out, l * 64 + 32)
                barrier(sp, l, 4)

                def z_loads(buf, blk, n_blk, k):
                    def load(t, p):
                        sp.dma_start(buf[p][:], proj_d[blk:blk + n_blk, :, cols(t)].rearrange("k p t -> p k t")).then_inc(tile_in[p], 16)
                    load(0, 0)
                    load(1, 1)
                    with sp.Fori(0, 3) as i:
                        for p in range(2):
                            sp.wait_ge(lo_made, nth(l, i * 2, k, 3) + (p + 1))
                            load(i * 2 + (p + 2), p)
                    sp.wait_ge(lo_made, nth(l, 7, k, 3))
                    load(8, 0)
                z_loads(z_c, B_ZC, KT, 0)
                barrier(sp, l, 5)

                def branch(base, name, kt, gate):
                    w = A[name][l].rearrange("(k p) n -> p k n", p=P)

                    def body(n, p, m, j):
                        load_group(sp, l, p, m, w[:, :, bass.ds(j * GW, GW)])
                        for b in range(2):
                            sp.wait_ge(wide_free[b], l * 16 + (j + (base - G_SSM + 1)))
                            sp.dma_start(wide[b][:], proj_d[j * 2 + (gate + b)] if gate is not None else x_d[j * 2 + b]).then_inc(wide_in[b], 16)
                    groups(sp, base, 4, body)
                branch(G_SSM, "w_branch_c", 8, B_GATE + 16)
                barrier(sp, l, 6)

                def gin_load(t, p):
                    sp.dma_start(gin[p][:], proj_d[B_GDN:B_GDN + 12, :, cols(t)].rearrange("k p t -> p k t")).then_inc(tile_in[p], 16)

                def g_store(t, p):
                    sp.wait_ge(out_ready, nth(l, t, 1, 2) + 1)
                    sp.dma_start(gdn_tile_d[t], g_out[p][:]).then_inc(tile_stored, 16)
                    sp.wait_ge(tile_stored, nth(l, t, 1, 2) * 16 + 16)
                    sp.sem_inc(waits_held, 1)
                gin_load(0, 0)
                gin_load(1, 1)
                with sp.Fori(0, 3) as i:
                    for p in range(2):
                        g_store(i * 2 + p, p)
                        gin_load(i * 2 + (p + 2), p)
                g_store(6, 0)
                gin_load(8, 0)
                g_store(7, 1)
                g_store(8, 0)
                barrier(sp, l, 7)

                def gdn_loads(i, p):
                    for d in range(2):
                        sp.dma_start(g_t[d][p][:], gdn_tile_d[scan_tile(i, d)]).then_inc(scan_in[d][p], 16)
                for d in range(2):
                    sp.dma_start(gd[d]["S"][:], A["state_gdn"][0, l, d].rearrange("h k v -> k h v")).then_inc(state_in[d], 16)
                gdn_loads(0, 0)
                gdn_loads(1, 1)
                with sp.Fori(0, 3) as i:
                    for p in range(2):
                        for d in range(2):
                            sp.wait_ge(g_step[d], i * 2 + (l * NT + p + 1))
                        gdn_loads(i * 2 + (p + 2), p)
                for d in range(2):
                    sp.wait_ge(g_step[d], l * NT + 7)
                gdn_loads(NS, 0)
                for d in range(2):
                    sp.wait_ge(g_step[d], l * NT + 9)
                    sp.dma_start(O["state_gdn"][0, l, d].rearrange("h k v -> k h v"), gd[d]["S"][:]).then_inc(states_out, 16)
                sp.wait_ge(states_out, l * 64 + 64)
                barrier(sp, l, 8)

                z_loads(z_a, B_ZA, 4, 1)
                barrier(sp, l, 9)
                branch(G_GDN, "w_branch_a", 4, B_GATE)
                barrier(sp, l, 10)

                def ain_load(t, p):
                    sp.dma_start(ain[p][:], proj_d[B_ATT:B_ATT + 6, :, cols(t)].rearrange("k p t -> p k t")).then_inc(tile_in[p], 16)
                ain_load(0, 0)
                ain_load(1, 1)
                with sp.Fori(0, 3) as i:
                    for p in range(2):
                        sp.wait_ge(transposed, nth(l, i * 2, 4, 5) + (p + 1))
                        ain_load(i * 2 + (p + 2), p)
                sp.wait_ge(transposed, nth(l, 7, 4, 5))
                ain_load(8, 0)
                sp.wait_ge(transposed, nth(l, 8, 4, 5))
                sp.dma_start(ain[1][:, 0], A["cache_k"][0, l].rearrange("t g d -> t (g d)")).then_inc(past_in, 16)
                sp.dma_start(v_all[:, NT], A["cache_v"][0, l].rearrange("t g d -> t (g d)")).then_inc(past_in, 16)
                sp.wait_ge(qk_done, l * NT + 9)
                sp.dma_start(O["cache_k"][0, l].rearrange("t g d -> t (g d)"), qk[:, AH:10].rearrange("p h d -> p (h d)")).then_inc(kv_out, 16)
                sp.dma_start(O["cache_v"][0, l].rearrange("t g d -> t (g d)"), v_all[:, NS]).then_inc(kv_out, 16)
                sp.wait_ge(kv_out, l * 32 + 32)
                barrier(sp, l, 11)

                def zb_load(t):
                    sp.dma_start(z_b[:], proj_d[B_ZB:B_ZB + 4, :, cols(t)].rearrange("k p t -> p k t")).then_inc(zb_in, 16)
                zb_load(0)
                with sp.Fori(0, NS) as t:
                    sp.wait_ge(lo_made, nth(l, t, 2, 3) + 1)
                    zb_load(t + 1)
                barrier(sp, l, 12)
                branch(G_ATT, "w_branch_b", 4, B_GATE + 8)
                barrier(sp, l, 13)
                branch(G_OUT, "w_out", 8, None)
                barrier(sp, l, 14)

            sp.dma_start(f_gain[:], A["final_norm_w"].partition_broadcast(P)).then_inc(f_in, 16)
            for t in range(NT + 2):
                if t < NT:
                    if t >= 2:
                        sp.wait_ge(f_tr, t - 1)
                    sp.dma_start(x_blk[t % 2][:], x_d[:, :, cols(t)].rearrange("k p t -> p k t")).then_inc(tok_in[t % 2], 16)
                if t >= 2:
                    sp.wait_ge(f_y, t - 1)
                    u = t - 2
                    dst = O["y_sample"].rearrange("b t d -> (b t) d")[u * P:(u + 1) * P] if u < NS else O["y_prompt"].rearrange("b t d -> (b t) d")
                    sp.dma_start(dst, x_tok[u % 2][:]).then_inc(f_out[u % 2], 16)
            sp.wait_ge(f_out[0], 80)
            sp.wait_ge(f_out[1], 64)

        @block.tensor
        def _(pe):
            pe.sem_inc(acc_ready[1], 2)

            pe.wait_ge(cst_in, 80)
            pe.transpose(bank(7, 24), rows_in[0:24], ident[0:24, 0:24]).then_inc(cond_t, 1)
            for t in range(NT):
                pe.wait_ge(tok_in[t % 2], 16 * (t // 2) + 16)
                if t >= 2:
                    pe.wait_ge(first_c, t - 1)
                for k in range(KT):
                    last = pe.transpose(bank(2 * (t % 2), P, k * P), x_tok[t % 2][:, k * P:(k + 1) * P], ident)
                last.then_inc(first_t, 1)
            first_barrier(pe)

            def sums_to_rows(u):
                pe.wait_ge(n_diag, u + 1)
                for t in range(NT):
                    last = pe.matmul(bank(3 + t // 3, P, (t % 3) * P), ones, r_diag[:, t], start=True, stop=True)
                last.then_inc(n_bc, 1)

            with pe.Fori(0, DEPTH) as l:
                pe.wait_ge(n_add, l * (KT - 1) + KT - 1)
                for t in range(NT):
                    last = pe.matmul(bank(2, 1, t), tmp[:, t * P:(t + 1) * P], ones[:, 0:1], start=True, stop=True)
                last.then_inc(n_mm, 1)
                pe.wait_ge(vec_loaded, l * (22 * 16) + 22 * 16)
                pe.transpose(bank(0, NV), vec_in[0:NV], ident[0:NV, 0:NV]).then_inc(vec_t, 1)
                for g in range(6):
                    if g == 2:
                        sums_to_rows(l * 2)
                    pe.wait_ge(mod_in[g % 3], l * 32 + 16 * (g // 3) + 16)
                    if g >= 2:
                        pe.wait_ge(mod_row, l * 6 + g - 1)
                    for k in range(KT):
                        last = pe.matmul(bank(6 + g % 2)[0:2], cond[:, k:16:8], w_mod[g % 3][:, k],
                                         start=(k == 0), stop=(k == KT - 1))
                    last.then_inc(mod_used, 1)
                pe.wait_ge(mod_row, l * 6 + 6)
                pe.sem_inc(waits_held, 1)
                for b in range(24):
                    last = pe.transpose(bank(1, 2, 2 * b), mod_rows[0:2, b * P:(b + 1) * P], ident[0:2, 0:2])
                last.then_inc(mod_col, 1)
                barrier(pe, l, 0)

                base = G_PROJ
                for kind, pairs, col, _ in PROJ_RUNS:
                    groups(pe, base, 2 * pairs, lambda n, p, m, j: multiply_group(pe, l, n, p, m, KT, h_hi, h_lo))
                    base += 2 * pairs
                barrier(pe, l, 1)

                for t in range(NT):
                    pe.transpose(bank(0, 16, t * 48), wide[0][0:16, t * P:(t + 1) * P], ident[0:16, 0:16])
                    last = pe.transpose(bank(0, 32, t * 48 + 16), wide[1][0:32, t * P:(t + 1) * P], ident[0:32, 0:32])
                last.then_inc(decay_prod, 1)
                pe.wait_ge(decay_term, l * 3 + 2)
                for d in range(2):
                    pe.matmul(bank(1 + d, 180), cst[:, C_TRI + d], logd[:, :, d], start=True, stop=True)
                    last = pe.matmul(bank(3 + d, 180), ones, logd[:, :, d], start=True, stop=True)
                last.then_inc(decay_prod, 1)
                barrier(pe, l, 2)

                def ssm_prep(t, p, i):
                    n = l * NT + t
                    for half in range(2):
                        pe.wait_ge(sp_fwd, n * 6 + 1 + half)
                        pe.wait_ge(sp_bwd, n * 4 + 1 + half)
                        for h in range(8 * half, 8 * half + 8):
                            dst = PSUM[:, 1536 + h * P:1536 + (h + 1) * P]
                            pe.matmul(dst, after[:, h], cst[:, C_TRI], start=True, stop=False)
                            last = pe.matmul(dst, before[:, h], cst[:, C_TRI + 1], start=False, stop=True)
                        last.then_inc(sp_prod, 1)
                    pe.wait_ge(tile_in[p], loaded(l, p, i, 0))
                    if not (isinstance(t, int) and t == 0):
                        pe.wait_ge(sp_yd, n)
                    for k in range(10):
                        pe.transpose(PSUM[:, k * P:(k + 1) * P], xin[p][:, k], ident)
                    for g in range(SG):
                        last = pe.matmul(bank(7, P, g * P), xin[p][:, 8 + g], xin[p][:, 10 + g], start=True, stop=True)
                    last.then_inc(transposed, 1)
                    pe.wait_ge(out_ready, nth(l, t, 0, 2) + 1)
                    for half in range(2):
                        pe.wait_ge(sp_fwd, n * 6 + 5 + half)
                        pe.wait_ge(sp_bwd, n * 4 + 3 + half)
                        for h in range(8 * half, 8 * half + 8):
                            dst = PSUM[:, h * SP_:(h + 1) * SP_]
                            pe.matmul(dst, w_f[:, h], x_dt[0][:, h], start=True, stop=False)
                            last = pe.matmul(dst, w_b[:, h], x_dt[1][:, h], start=False, stop=True)
                    last.then_inc(sp_y, 1)
                ssm_prep(0, 0, 0)
                ssm_prep(1, 1, 0)
                with pe.Fori(0, 3) as i:
                    for p in range(2):
                        ssm_prep(i * 2 + (p + 2), p, i + 1)
                ssm_prep(NT - 1, 0, 4)
                barrier(pe, l, 3)

                for d in range(2):
                    pe.wait_ge(state_in[d], l * 32 + 16)
                    for b in range(8):
                        last = pe.transpose(PSUM[:, d * 2048 + b * P:d * 2048 + (b + 1) * P], s_io[d][:, b], ident)
                    last.then_inc(ssm_s_t[d], 1)

                def ssm_step(t, p, i):
                    for d in range(2):
                        before_ = l * 22 + (10 if isinstance(t, int) else t + 1)
                        pe.wait_ge(scan_in[d][p], scan_loaded(l, p, 2 * i + 2))
                        pe.wait_ge(state[d], before_)
                        for g in range(SG):
                            last = pe.matmul(bank(4 * d + g), c_t[d][p][:, g], s_ssm[d][:, g * 512:(g + 1) * 512], start=True, stop=True)
                        last.then_inc(ssm_prod[d], 1)
                        pe.wait_ge(ssm_side[d], (l * NT + t) * 2 + 1)
                        for g in range(SG):
                            last = pe.matmul(bank(4 * d + 2 + g), xs[d][p][:, 1024 + g * P:1024 + (g + 1) * P],
                                             x_in[d][:, 8 * g:8 * g + 8].rearrange("p h q -> p (h q)"), start=True, stop=True)
                        last.then_inc(ssm_prod[d], 1)
                tiles(pe, ssm_step)
                for d in range(2):
                    pe.wait_ge(state[d], l * 22 + 11)
                    for b in range(8):
                        last = pe.transpose(PSUM[:, d * 2048 + b * P:d * 2048 + (b + 1) * P], s_ssm[d][:, b * P:(b + 1) * P], ident)
                    last.then_inc(ssm_s_t[d], 1)
                barrier(pe, l, 4)

                def ssm_post(t, p, i):
                    n = l * NT + t
                    pe.wait_ge(y_copied, n + 1)
                    for k in range(KT):
                        last = pe.transpose(PSUM[:, k * P:(k + 1) * P], y_st[p][:, k * P:(k + 1) * P], ident)
                    last.then_inc(transposed, 1)
                    pe.wait_ge(squared, nth(l, t, 0, 4) + 1)
                    for k in range(KT):
                        last = pe.matmul(bank(2, 1), y_sq[:, k], ones[:, 0:1], start=(k == 0), stop=(k == KT - 1))
                    last.then_inc(sums_made, 1)
                    pe.wait_ge(y_ss_read, n + 1)
                tiles(pe, ssm_post)
                sums_to_rows(l * 2 + 1)
                barrier(pe, l, 5)
                groups(pe, G_SSM, 4, lambda n, p, m, j: multiply_group(pe, l, n, p, m, 8, b_hi, b_lo))
                barrier(pe, l, 6)

                def gdn_prep(t, p, i):
                    n = l * NT + t
                    pe.wait_ge(tile_in[p], loaded(l, p, i, 2))
                    for k in range(12):
                        last = pe.transpose(PSUM[:, k * P:(k + 1) * P], gin[p][:, k], ident)
                    last.then_inc(transposed, 1)
                    pe.wait_ge(scaled, nth(l, t, 1, 4) + 1)
                    for h in range(GH):
                        pe.transpose(bank(3, P, h * P), q_n[:, h], ident)
                        last = pe.transpose(bank(4, P, h * P), g_out[p][:, 2, h * P:(h + 1) * P], ident)
                    last.then_inc(gp_tt, 1)
                    pe.wait_ge(gp_c, n + 1)
                    for h in range(GH):
                        hh = slice(h * P, (h + 1) * P)
                        pe.matmul(bank(5)[:, hh], g_out[p][:, 0, hh], g_out[p][:, 0, hh], start=True, stop=True)
                        last = pe.matmul(bank(6)[:, hh], g_out[p][:, 0, hh], g_out[p][:, 1, hh], start=True, stop=True)
                    last.then_inc(gp_k, 1)
                    pe.wait_ge(out_ready, nth(l, t, 1, 2) + 1)
                tiles(pe, gdn_prep)
                barrier(pe, l, 7)

                def gdn_step(t, p, i):
                    n = l * NT + t
                    for d in range(2):
                        g, b0 = gd[d], 4 * d
                        pe.wait_ge(g_term[d], n * 4 + 1)
                        for h in range(GH):
                            pe.matmul(bank(b0 + 3, P, h * P), g["col"][:, h], cst[:, C_TRI + d], start=True, stop=True)
                            last = pe.matmul(bank(b0, P, h * P), g["col"][:, 4 + h], ident, start=True, stop=True)
                        last.then_inc(g_row[d], 1)
                    for d in range(2):
                        g, b0 = gd[d], 4 * d
                        pe.wait_ge(g_term[d], n * 4 + 3)
                        for h in range(GH):
                            last = pe.transpose(bank(b0 + 3, P, h * P), g["A"][:, h], ident)
                        last.then_inc(g_row[d], 1)
                    for d in range(2):
                        g, b0 = gd[d], 4 * d
                        pe.wait_ge(g_x[d], n * 7 + 1)
                        pe.matmul(bank(b0 + 1), ident, g["X"][:].rearrange("p h t -> p (h t)"), start=True, stop=False, skip_group_check=True)
                        pe.matmul(bank(b0 + 2), ident, g["Y"][:].rearrange("p h t -> p (h t)"), start=True, stop=False, skip_group_check=True)
                    for lev in range(1, 7):
                        for d in range(2):
                            g, b0 = gd[d], 4 * d
                            if lev > 1:
                                pe.wait_ge(g_x[d], n * 7 + lev)
                            for h in range(GH):
                                last = pe.matmul(bank(b0, P, h * P), g["A"][:, h], g["X"][:, h], start=True, stop=True)
                            last.then_inc(g_level[d], 1)
                        for d in range(2):
                            g, b0 = gd[d], 4 * d
                            pe.wait_ge(g_tm[d], n * 6 + lev)
                            for h in range(GH):
                                if lev < 6:
                                    pe.matmul(bank(b0 + 1, P, h * P), g["Y"][:, h], g["T"][:, h], start=False, stop=False, skip_group_check=True)
                                last = pe.matmul(bank(b0 + 2, P, h * P), g["T"][:, h], g["Y"][:, h], start=False, stop=(lev == 6 and h == 3), skip_group_check=True)
                            last.then_inc(g_level[d], 1)
                    for d in range(2):
                        g, b0 = gd[d], 4 * d
                        pe.wait_ge(state[d], l * 22 + 11 + (10 if isinstance(t, int) else t + 1))
                        for h in range(GH):
                            last = pe.matmul(bank(b0, P, h * P), g_t[d][p][:, 0, h * P:(h + 1) * P], g["S"][:, h], start=True, stop=True)
                        last.then_inc(g_from_s[d], 1)
                        for h in range(GH):
                            last = pe.matmul(bank(b0 + 3, P, h * P), g_t[d][p][:, 1, h * P:(h + 1) * P], g["S"][:, h], start=True, stop=True)
                        last.then_inc(g_from_s[d], 1)
                    for d in range(2):
                        g, b0 = gd[d], 4 * d
                        pe.wait_ge(g_x[d], n * 7 + 7)
                        pe.wait_ge(g_term[d], n * 4 + 4)
                        for h in range(GH):
                            last = pe.matmul(bank(b0 + 1, P, h * P), g["Y"][:, h], g["R"][:, h], start=True, stop=True)
                        last.then_inc(g_v[d], 1)
                    for d in range(2):
                        g, b0 = gd[d], 4 * d
                        pe.wait_ge(g_vc[d], n + 1)
                        pe.wait_ge(g_side[d], n * 5 + 2)
                        for h in range(GH):
                            last = pe.matmul(bank(b0, P, h * P), g["KD"][:, h], g["V"][:, h], start=True, stop=True)
                        last.then_inc(g_from_v[d], 1)
                        pe.wait_ge(g_side[d], n * 5 + 5)
                        for h in range(GH):
                            last = pe.matmul(bank(b0 + 2, P, h * P), g["Q"][:, h], g["V"][:, h], start=True, stop=True)
                        last.then_inc(g_from_v[d], 1)
                    for d in range(2):
                        pe.wait_ge(g_step[d], n + 1)
                tiles(pe, gdn_step)
                barrier(pe, l, 8)

                def gdn_post(t, p, i):
                    n = l * NT + t
                    pe.wait_ge(scaled, nth(l, t, 2, 4) + 1)
                    for h in range(GH):
                        last = pe.transpose(bank(p, P, h * P), o_st[p][:, h], ident)
                    last.then_inc(transposed, 1)
                    pe.wait_ge(lo_made, nth(l, t, 1, 3) + 1)
                tiles(pe, gdn_post)
                barrier(pe, l, 9)
                groups(pe, G_GDN, 4, lambda n, p, m, j: multiply_group(pe, l, n, p, m, 4, b_hi, b_lo))
                barrier(pe, l, 10)

                def stack(n, q):
                    pe.wait_ge(a_split, n + 1)
                    if q is not None:
                        for h in range(AH):
                            pe.transpose(bank(2, P, h * P), q_hl[:, h].bitcast(F32), ident)
                    for g in range(KVH):
                        pe.transpose(bank(4, P, g * P), k_hh[:, g].bitcast(F32), ident)
                        last = pe.transpose(bank(4, P, 256 + g * P), k_ll[:, g].bitcast(F32), ident)
                    last.then_inc(a_st, 1)
                    pe.wait_ge(a_k, n + 1)
                    if q is not None:
                        pe.wait_ge(a_q, q + 1)

                def attn_prep(t, p, i):
                    n = l * (NT + 1) + t
                    pe.wait_ge(tile_in[p], loaded(l, p, i, 4))
                    for k in range(6):
                        last = pe.transpose(PSUM[:, k * P:(k + 1) * P], ain[p][:, k], ident)
                    last.then_inc(transposed, 1)
                    stack(n, l * NT + t)
                tiles(pe, attn_prep)
                stack(l * (NT + 1) + NT, None)
                barrier(pe, l, 11)

                def scores(t, u, h):
                    g, s = h // 4, h % 2
                    if h == 0:
                        pe.wait_ge(q_set, l * NT + t + 1)
                    sample = not (isinstance(t, int) and t == NS)
                    spans = ((0, 512, 0), (512, 512, 512), (NT * P, P, 1024)) if sample else ((SAMPLE, P, 0),)
                    for col, width, at in spans:
                        dst = PSUM[:, 1536 * s + at:1536 * s + at + width]
                        pe.matmul(dst, q_now[u][:, h], k_hi[:, g, col:col + width], start=True, stop=False)
                        last = pe.matmul(dst, q_now[u][:, h], k_lo[:, g, col:col + width], start=False, stop=True)
                    last.then_inc(at_s, 1)

                def values(t, h, key_tiles):
                    n, g, s = l * NT + t, h // 4, h % 2
                    pe.wait_ge(at_c[0], n * AH + h + 1)
                    if len(key_tiles) > 4:
                        pe.wait_ge(at_c[1], (l * NS + t) * AH + h + 1)
                    for j, kt in enumerate(key_tiles):
                        last = pe.matmul(bank(7, AD, h * AD), prob_t[s][:, j], v_all[:, kt, g * AD:(g + 1) * AD],
                                         start=(j == 0), stop=(j == len(key_tiles) - 1))
                    last.then_inc(at_v, 1)

                def attn(t, u, key_tiles, first=False):
                    n, nk = l * NT + t, len(key_tiles)
                    for h in range(AH):
                        s = h % 2
                        if nk > 4 and h:
                            pe.wait_ge(at_c[1], (l * NS + t) * AH + h)
                        if h + 1 < AH:
                            scores(t, u, h + 1)
                        elif nk > 4:
                            scores(t + 1, 1 - u, 0)
                        pe.wait_ge(at_e, n * AH + h + 1)
                        if h:
                            pe.wait_ge(at_c[0], n * AH + h)
                        elif not first:
                            pe.wait_ge(gated, nth(l, t, 2, 3))
                        for j in range(nk):
                            dst = bank(6, P, j * P) if j < 4 else PSUM[:, 1536 * s + j * P:1536 * s + (j + 1) * P]
                            last = pe.transpose(dst, prob[s][:, j * P:(j + 1) * P], ident)
                            if j == min(3, nk - 1):
                                last.then_inc(at_t[0], 1)
                        if nk > 4:
                            last.then_inc(at_t[1], 1)
                        if h:
                            values(t, h - 1, key_tiles)
                    values(t, AH - 1, key_tiles)
                    pe.wait_ge(o_norm, n + 1)
                    for k in range(4):
                        last = pe.transpose(bank(6, P, k * P), o_att[:, 2 * k:2 * k + 2].rearrange("p h d -> p (h d)"), ident)
                    last.then_inc(o_tr, 1)
                sample_keys = [0, 1, 2, 3, 4, 5, 6, 7, NT]
                scores(0, 0, 0)
                attn(0, 0, sample_keys, first=True)
                attn(1, 1, sample_keys)
                with pe.Fori(0, 2) as i:
                    for u in range(2):
                        attn(i * 2 + (u + 2), u, sample_keys)
                attn(6, 0, sample_keys)
                attn(7, 1, sample_keys)
                attn(NS, 0, [NS])
                barrier(pe, l, 12)
                groups(pe, G_ATT, 4, lambda n, p, m, j: multiply_group(pe, l, n, p, m, 4, b_hi, b_lo))
                barrier(pe, l, 13)

                pe.wait_ge(m_lo, l * KT + KT)
                pe.sem_inc(waits_held, 1)
                groups(pe, G_OUT, 4, lambda n, p, m, j: multiply_group(pe, l, n, p, m, 8, b_hi, b_lo))
                barrier(pe, l, 14)

            for t in range(NT):
                pe.wait_ge(tok_in[t % 2], 16 * ((5 - t % 2) + t // 2 + 1))
                if t >= 2:
                    pe.wait_ge(f_y, t - 1)
                for k in range(KT):
                    last = pe.transpose(bank(2 * (t % 2), P, k * P), x_blk[t % 2][:, k], ident)
                last.then_inc(f_tr, 1)

        @block.scalar
        def _(act):
            act.wait_ge(cond_t, 1)
            act.activation(stat[:, 0:24], bank(7, 24), ACT.Tanh, scale=0.5).then_inc(cond_th, 1)
            for t in range(NT):
                act.wait_ge(first_t, t + 1)
                if t >= 2:
                    act.wait_ge(first_out[t % 2], 16 * (t // 2))
                act.activation(x_blk[t % 2][:], PSUM[:, 1024 * (t % 2):1024 * (t % 2) + 1024].rearrange("p (k t) -> p k t", t=P), ACT.Copy).then_inc(first_c, 1)
            first_barrier(act)

            with act.Fori(0, DEPTH) as l:
                for at, name in ((V_NORM, "norm_w"), (V_BMOD, "b_mod"), (V_SBIAS, "ssm_conv_b"),
                                 (V_SNORM, "ssm_norm_w"), (V_GNORM, "gdn_norm_w")):
                    src = A[name][l].rearrange("(k p) -> k p", p=P)
                    act.dma_start(vec_in[at:at + src.shape[0]], src).then_inc(vec_loaded, 16)
                for at, name in ((V_GCONV, "gdn_conv_w"), (V_SCONV, "ssm_conv_w")):
                    act.dma_start(vec_in[at:at + 36], A[name][l].rearrange("w (k p) -> (w k) p", p=P)).then_inc(vec_loaded, 16)
                for at, name in ((0, "gdn_a_log"), (8, "ssm_a_log"), (40, "gdn_dt_bias"), (48, "ssm_dt_bias")):
                    src = A[name][l].rearrange("d h -> (d h)")
                    act.dma_start(rows[:, at:at + src.shape[0]], src.partition_broadcast(P)).then_inc(vec_loaded, 16)
                act.dma_start(rows[:, 80:96], A["ssm_d"][l].partition_broadcast(P)).then_inc(vec_loaded, 16)
                for at, name, heads in ((0, "attn_q_norm", AH), (AH, "attn_k_norm", KVH)):
                    for h in range(heads):
                        act.dma_start(qk_gain[:, at + h], A[name][l].partition_broadcast(P)).then_inc(vec_loaded, 16)
                act.wait_ge(x_in_sb, l * 128 + 128)
                for k in range(KT):
                    if k >= 3:
                        act.wait_ge(n_add, l * (KT - 1) + k - 2)
                    act.activation(wide[k % 2][:] if k else tmp[:], x_sb[:, k], ACT.Square).then_inc(n_sq, 1)
                for g in range(6):
                    act.wait_ge(mod_used, l * 6 + g + 1)
                    act.activation(mod_rows[0:2, g * 512:(g + 1) * 512], bank(6 + g % 2)[0:2], ACT.Copy).then_inc(mod_row, 1)

                def rows_out(u):
                    act.wait_ge(n_bc, u + 1)
                    act.activation(thirds(row_bc[:]), acc(1), ACT.Copy).then_inc(n_row, 1)
                rows_out(l * 2)
                for k in range(KT):
                    act.wait_ge(n_t, l * KT + k + 1)
                    for c, (lo, hi) in enumerate(((0, SAMPLE), (SAMPLE, T))):
                        last = act.activation(h_hi[:, k, lo:hi], wide[k % 2][:, lo:hi], ACT.Identity, bias=mod[:, k, c:c + 1])
                    last.then_inc(n_h, 1)
                act.wait_ge(vec_loaded, l * (22 * 16) + 22 * 16)
                act.activation(coef[:, :, 0:4], rows[:, 0:8].rearrange("p (d h) -> p d h", d=2), ACT.Exp)
                act.activation(coef[:, :, 4:20], rows[:, 8:40].rearrange("p (d h) -> p d h", d=2), ACT.Exp).then_inc(coef_e, 1)
                barrier(act, l, 0)

                base, stored, conv, th = G_PROJ, 0, 0, 0
                for kind, pairs, col, _ in PROJ_RUNS:
                    def body(n, p, m, j, kind=kind, st=stored, cv=conv, tq=th):
                        for b in range(2):
                            act.wait_ge(acc_ready[b], acc_done(l, n, b))
                            if kind.startswith("conv"):
                                act.activation(thirds(conv_in[b][:, 1:1 + 2 * THIRD]), acc(b)[:, 0:2], ACT.Copy)
                                act.activation(conv_in[b][:, 1 + 2 * THIRD:1 + SAMPLE], acc(b)[:, 2, 0:THIRD - PROMPT], ACT.Copy)
                                act.activation(conv_in[b][:, SAMPLE + 2:T + 2], acc(b)[:, 2, THIRD - PROMPT:THIRD], ACT.Copy).then_inc(acc_free[b], 1)
                                act.wait_ge(conv_mid[b], l * 12 + j + (cv + 1))
                                act.wait_ge(leave_free[b], l * 35 + j + (st + 1))
                                act.activation(leave[b][:, 0:T + 1], conv_out[b][:, 0:T + 1], ACT.Tanh).then_inc(th_ready[b], 1)
                            elif kind == "kv_small" and j == 1:
                                act.activation(thirds(wide[b][0:32]), acc(b)[0:32], ACT.Copy).then_inc(acc_free[b], 1)
                            else:
                                act.wait_ge(leave_free[b], l * 35 + j + (st + 1))
                                if kind == "silu":
                                    act.activation(thirds(leave[b][:, 0:T]), acc(b), ACT.Tanh, scale=0.5).then_inc(th_ready[b], 1)
                                else:
                                    f, sc = (ACT.Tanh, 0.5) if kind == "tanh" else (ACT.Copy, 1.0)
                                    act.activation(thirds(leave[b][:, 0:T]), acc(b), f, scale=sc).then_inc(leave_ready[b], 1)
                                    act.drain().then_inc(acc_free[b], 1)
                    if kind == "kv_small":
                        body(base, 0, base // 2, 0)
                        body(base + 1, 1, base // 2, 1)
                    else:
                        groups(act, base, 2 * pairs, body)
                    stored += 1 if kind == "kv_small" else 2 * pairs
                    conv += 2 * pairs if kind.startswith("conv") else 0
                    th += 2 * pairs if kind.startswith("conv") or kind == "silu" else 0
                    base += 2 * pairs
                barrier(act, l, 1)

                act.wait_ge(decay_term, l * 3 + 1)
                act.activation(dec["e_abs"][:], dec["neg"][:], ACT.Exp)
                act.activation(dec["e_low"][:], dec["low"][:], ACT.Exp).then_inc(decay_exp, 1)
                act.wait_ge(decay_term, l * 3 + 3)
                act.activation(e_cum[:], cum[:], ACT.Exp)
                act.activation(e_tot[:], tot[:], ACT.Exp)
                act.activation(e_rest[:], rest[:], ACT.Exp).then_inc(decay_exp, 1)
                barrier(act, l, 2)

                def ssm_prep(t, p, i):
                    n = l * NT + t
                    for half in range(2):
                        act.wait_ge(sp_prod, n * 2 + 1 + half)
                        hs = slice(8 * half, 8 * half + 8)
                        act.activation(e_ssm[:, hs], PSUM[:, 1536 + 1024 * half:2560 + 1024 * half].rearrange("p (h l) -> p h l", l=P), ACT.Exp).then_inc(sp_e, 1)
                    act.wait_ge(transposed, nth(l, t, 0, 5) + 1)
                    if not (isinstance(t, int) and t < 2):
                        act.wait_ge(tile_stored, nth(l, t, 0, 2) * 16 - 16)
                    act.activation(xt[p][:], PSUM[:, 0:1280], ACT.Copy).then_inc(out_ready, 1)
                ssm_prep(0, 0, 0)
                ssm_prep(1, 1, 0)
                with act.Fori(0, 3) as i:
                    for p in range(2):
                        ssm_prep(i * 2 + (p + 2), p, i + 1)
                ssm_prep(NT - 1, 0, 4)
                barrier(act, l, 3)

                for d in range(2):
                    act.wait_ge(ssm_s_t[d], l * 2 + 1)
                    act.activation(s_ssm[d][:], PSUM[:, d * 2048:d * 2048 + 1024], ACT.Copy).then_inc(state[d], 1)
                for d in range(2):
                    act.wait_ge(ssm_s_t[d], l * 2 + 2)
                    act.activation(s_io[d][:], PSUM[:, d * 2048:d * 2048 + 1024].rearrange("p (b n) -> p b n", n=P), ACT.Copy).then_inc(ssm_s_out[d], 1)
                barrier(act, l, 4)

                def ssm_post(t, p, i):
                    n = l * NT + t
                    act.activation(y_st[p][:], y_acc[:, t], ACT.Copy).then_inc(y_copied, 1)
                    act.wait_ge(gated, nth(l, t, 0, 3) + 1)
                    act.activation(y_sq[:], yz[:], ACT.Square).then_inc(squared, 1)
                    act.wait_ge(scaled, nth(l, t, 0, 4) + 1)
                    act.activation(b_hi[:, :, cols(t)], yzw[:], ACT.Copy).then_inc(hi_made, 1)
                    act.wait_ge(lo_made, nth(l, t, 0, 3) + 1)
                tiles(act, ssm_post)
                rows_out(l * 2 + 1)
                barrier(act, l, 5)
                barrier(act, l, 6)

                def gdn_prep(t, p, i):
                    n = l * NT + t
                    act.wait_ge(transposed, nth(l, t, 2, 5) + 1)
                    act.activation(g_sq[:], PSUM[:, 0:1024].rearrange("p (h d) -> p h d", d=GD), ACT.Square).then_inc(squared, 1)
                    act.activation(g_out[p][:, 3], bank(2), ACT.Copy)
                    act.wait_ge(gp_tt, n + 1)
                    act.activation(g_out[p][:, 1], bank(3), ACT.Copy)
                    act.activation(g_out[p][:, 0], bank(4), ACT.Copy).then_inc(gp_c, 1)
                    act.wait_ge(gp_k, n + 1)
                    act.activation(g_out[p][:, 4], bank(5), ACT.Copy)
                    act.activation(g_out[p][:, 5], bank(6), ACT.Copy).then_inc(out_ready, 1)
                tiles(act, gdn_prep)
                barrier(act, l, 7)

                def flat(x):
                    return x[:].rearrange("p h t -> p (h t)")

                def gdn_step(t, p, i):
                    n = l * NT + t
                    for d in range(2):
                        act.wait_ge(g_term[d], n * 4 + 2)
                        act.activation(gd[d]["E"][:], gd[d]["E"][:], ACT.Exp).then_inc(g_e[d], 1)
                    for lev in range(1, 7):
                        for d in range(2):
                            act.wait_ge(g_level[d], n * 12 + 2 * lev)
                            if lev < 6:
                                act.activation(flat(gd[d]["X"]), bank(4 * d + 1), ACT.Copy)
                            act.activation(flat(gd[d]["Y"]), bank(4 * d + 2), ACT.Copy).then_inc(g_x[d], 1)
                    for d in range(2):
                        act.wait_ge(g_v[d], n + 1)
                        act.activation(flat(gd[d]["V"]), bank(4 * d + 1), ACT.Copy).then_inc(g_vc[d], 1)
                tiles(act, gdn_step)
                barrier(act, l, 8)

                def gdn_post(t, p, i):
                    n = l * NT + t
                    act.activation(o_sq[:], o_acc[:, t].rearrange("p (h d) -> p h d", d=GD), ACT.Square).then_inc(squared, 1)
                    act.wait_ge(gated, nth(l, t, 1, 3) + 1)
                    act.activation(b_hi[:, 0:4, cols(t)], o_z[:], ACT.Copy).then_inc(hi_made, 1)
                    act.wait_ge(lo_made, nth(l, t, 1, 3) + 1)
                tiles(act, gdn_post)
                barrier(act, l, 9)
                barrier(act, l, 10)

                def attn_prep(t, p, i):
                    n, n1 = l * NT + t, l * (NT + 1) + t
                    act.wait_ge(transposed, nth(l, t, 4, 5) + 1)
                    act.activation(a_sq[:], PSUM[:, 0:640].rearrange("p (h d) -> p h d", d=AD), ACT.Square).then_inc(squared, 1)
                    act.activation(v_all[:, t], PSUM[:, 640:768], ACT.Copy).then_inc(a_v, 1)
                    act.wait_ge(a_st, n1 + 1)
                    act.activation(q_stack[:, t], PSUM[:, 1024:2048].rearrange("p (h t) -> p h t", t=P), ACT.Copy).then_inc(a_q, 1)
                tiles(act, attn_prep)
                barrier(act, l, 11)

                def attn(t, u, nk):
                    n, ns = l * NT + t, l * NS + t
                    width = nk * P
                    for h in range(AH):
                        s = h % 2
                        if nk == 1 and h:
                            act.wait_ge(at_t[0], n * AH + h)
                        act.wait_ge(at_m, n * AH + h + 1)
                        act.activation(prob[s][:, 0:width], PSUM[:, 1536 * s:1536 * s + width], ACT.Exp, bias=row_max[:, u, h:h + 1],
                                       accum_out=row_sum[:, u, h:h + 1]).then_inc(at_e, 1)
                        if nk > 1:
                            act.wait_ge(at_t[1], ns * AH + h + 1)
                            act.activation(prob_t[s][:, 4:9], PSUM[:, 1536 * s + 512:1536 * s + T].rearrange("p (j t) -> p j t", t=P), ACT.Copy).then_inc(at_c[1], 1)
                    act.wait_ge(gated, nth(l, t, 2, 3) + 1)
                    act.activation(b_hi[:, 0:4, cols(t)], o_bz[:], ACT.Copy).then_inc(hi_made, 1)
                with act.Fori(0, NS // 2) as i:
                    for u in range(2):
                        attn(i * 2 + u, u, 9)
                attn(NS, 0, 1)
                barrier(act, l, 12)
                barrier(act, l, 13)

                for k in range(KT):
                    act.activation(b_hi[:, k], merged[:, k], ACT.Copy).then_inc(m_hi, 1)
                barrier(act, l, 14)

            for t in range(NT):
                act.wait_ge(f_tr, t + 1)
                if t >= 2:
                    act.wait_ge(f_y, t - 1)
                if t:
                    act.wait_ge(f_sq, t)
                act.activation(rows_wide[:], PSUM[:, 1024 * (t % 2):1024 * (t % 2) + 1024], ACT.Square,
                               accum_out=stat[:, 16 + t:17 + t]).then_inc(f_sq, 1)

        @block.gpsimd
        def _(pool):
            for b in range(2):
                pool.sem_inc(leave_free[b], 1)
                pool.sem_inc(wide_free[b], 1)
            pool.memset(minus_half[:], -0.5)
            for t in range(NT):
                pool.wait_ge(first_c, t + 1)
                pool.sem_inc(waits_held, 1)
                pool.dma_start(x_d[:, :, cols(t)].rearrange("k p t -> p k t"), x_blk[t % 2][:]).then_inc(first_out[t % 2], 16)
            pool.wait_ge(first_out[0], 80)
            pool.wait_ge(first_out[1], 64)
            first_barrier(pool)

            with pool.Fori(0, DEPTH) as l:
                pool.wait_ge(n_ms, l * 2 + 1)
                pool.tensor_tensor(r_tok[:], stat[:, 0:NT], minus_half[:, 0:NT], ALU.pow).then_inc(n_r, 1)
                barrier(pool, l, 0)

                base, stored = G_PROJ, 0
                for kind, pairs, col, blk in PROJ_RUNS:
                    at = SAMPLE + 1 if kind.startswith("conv") else SAMPLE

                    def body(n, p, m, j, at=at, blk=blk, st=stored):
                        for b in range(2):
                            pool.wait_ge(leave_ready[b], l * 35 + j + (st + 1))
                            pool.sem_inc(waits_held, 1)
                            pool.dma_start(proj_d[j * 2 + (blk + b), :, 0:SAMPLE], leave[b][:, 0:SAMPLE]).then_inc(leave_out[b], 16)
                            pool.dma_start(proj_d[j * 2 + (blk + b), :, SAMPLE:T], leave[b][:, at:at + PROMPT]).then_inc(leave_out[b], 16)
                            pool.wait_ge(leave_out[b], (l * 35 + j + (st + 1)) * 32)
                            pool.sem_inc(leave_free[b], 1)
                    if kind == "kv_small":
                        body(base, 0, base // 2, 0)
                    else:
                        groups(pool, base, 2 * pairs, body)
                    stored += 1 if kind == "kv_small" else 2 * pairs
                    base += 2 * pairs
                barrier(pool, l, 1)
                barrier(pool, l, 2)

                def build_before(t):
                    for half in range(2):
                        hs = slice(8 * half, 8 * half + 8)
                        pool.tensor_tensor(before[:, hs], again(cst[:, C_STRICT + 1], 8), over(logd[:, t, 1, 4 + 8 * half:12 + 8 * half], P), ALU.mult).then_inc(sp_bwd, 1)

                def ssm_prep(t, p, i):
                    n = l * NT + t
                    last_tile = isinstance(t, int) and t == NT - 1
                    pool.wait_ge(sp_prod, n * 2 + 2)
                    pool.wait_ge(out_ready, nth(l, t, 0, 2) + 1)
                    if not (isinstance(t, int) and t == 0):
                        pool.wait_ge(sp_yd, n)
                    xh = xt[p][:, 0:D_MODEL].rearrange("p (h q) -> p h q", q=SP_)
                    pool.tensor_tensor(x_dt[1][:], xh, over(dt_[:, t, 1], SP_), ALU.mult)
                    pool.wait_ge(sp_fwd, n * 6 + 4)
                    for g in range(SG):
                        pool.tensor_tensor(w_b[:, 8 * g:8 * g + 8], e_ssm[:, 8 * g:8 * g + 8], again(cb[1][:, g], 8), ALU.mult).then_inc(sp_bwd, 1)
                    if not last_tile:
                        build_before(t + 1)
                    pool.tensor_tensor(d_x[:], xh, over(rows[:, 80:96], SP_), ALU.mult).then_inc(sp_dx, 1)
                build_before(0)
                ssm_prep(0, 0, 0)
                ssm_prep(1, 1, 0)
                with pool.Fori(0, 3) as i:
                    for p in range(2):
                        ssm_prep(i * 2 + (p + 2), p, i + 1)
                ssm_prep(NT - 1, 0, 4)
                barrier(pool, l, 3)

                def ssm_step(t, p, i):
                    for d in range(2):
                        tt = t if isinstance(t, int) or d == 0 else (NS - 1) - t
                        pool.wait_ge(scan_in[d][p], scan_loaded(l, p, 2 * i + 2))
                        pool.sem_inc(waits_held, 1)
                        pool.wait_ge(state[d], l * 22 + (10 if isinstance(t, int) else t + 1))
                        pool.sem_inc(waits_held, 1)
                        pool.tensor_tensor(x_in[d][:], xs[d][p][:, 0:D_MODEL].rearrange("p (h q) -> p h q", q=SP_), over(dt_rest[:, d, tt], SP_), ALU.mult).then_inc(ssm_side[d], 1)
                        pool.tensor_tensor(s_kept[d][:].rearrange("p (h q) -> p h q", q=SP_), s_ssm[d][:].rearrange("p (h q) -> p h q", q=SP_), over(e_tot[:, d, tt, 4:20], SP_), ALU.mult).then_inc(ssm_side[d], 1)
                tiles(pool, ssm_step)
                barrier(pool, l, 4)

                def ssm_post(t, p, i):
                    n = l * NT + t
                    pool.wait_ge(gated, nth(l, t, 0, 3) + 1)
                    pool.tensor_tensor(yzw[:], yz[:], over(vec[:, V_SNORM:V_SNORM + 8], P), ALU.mult).then_inc(scaled, 1)
                    pool.wait_ge(lo_made, nth(l, t, 0, 3) + 1)
                tiles(pool, ssm_post)
                pool.wait_ge(n_ms, l * 2 + 2)
                pool.tensor_tensor(r_tok[:], stat[:, 0:NT], minus_half[:, 0:NT], ALU.pow).then_inc(n_r, 1)
                barrier(pool, l, 5)
                barrier(pool, l, 6)

                def gdn_prep(t, p, i):
                    pool.wait_ge(sums_made, nth(l, t, 1, 4) + 1)
                    pool.tensor_tensor(stat[:, 8:16], stat[:, 0:8], minus_half[:, 0:8], ALU.pow).then_inc(inv_rms, 1)
                tiles(pool, gdn_prep)
                barrier(pool, l, 7)

                pool.memset(o_acc[:], 0.0).then_inc(o_zero, 1)

                def gdn_step(t, p, i):
                    n = l * NT + t
                    for d in range(2):
                        tt = t if isinstance(t, int) or d == 0 else (NS - 1) - t
                        g = gd[d]
                        pool.wait_ge(scan_in[d][p], scan_loaded(l, p, 2 * (5 - p) + i + 1))
                        pool.sem_inc(waits_held, 1)
                        kind = lambda c: g_t[d][p][:, c].rearrange("p (h t) -> p h t", t=P)
                        pool.wait_ge(state[d], l * 22 + 11 + (10 if isinstance(t, int) else t + 1))
                        pool.sem_inc(waits_held, 1)
                        pool.tensor_tensor(g["VB"][:], kind(3), over(beta[:, tt, d], P), ALU.mult).then_inc(g_side[d], 1)
                        pool.tensor_tensor(g["KD"][:], kind(2), over(e_rest[:, d, tt, 0:4], P), ALU.mult).then_inc(g_side[d], 1)
                        pool.tensor_tensor(g["SK"][:], g["S"][:], over(e_tot[:, d, tt, 0:4], P), ALU.mult).then_inc(g_side[d], 1)
                    for d in range(2):
                        g = gd[d]
                        kind = lambda c: g_t[d][p][:, c].rearrange("p (h t) -> p h t", t=P)
                        pool.wait_ge(g_e[d], n + 1)
                        pool.tensor_tensor(g["A0"][:], kind(4), g["E"][:], ALU.mult).then_inc(g_side[d], 1)
                        pool.tensor_tensor(g["Q0"][:], kind(5), g["E"][:], ALU.mult)
                        pool.drain()
                        pool.tensor_tensor(g["Q"][:], g["Q0"][:], again(cst[:, C_TRI + d], GH), ALU.mult).then_inc(g_side[d], 1)
                tiles(pool, gdn_step)
                barrier(pool, l, 8)

                def gdn_post(t, p, i):
                    pool.wait_ge(sums_made, nth(l, t, 2, 4) + 1)
                    pool.tensor_tensor(stat[:, 8:12], stat[:, 0:4], minus_half[:, 0:4], ALU.pow).then_inc(inv_rms, 1)
                tiles(pool, gdn_post)
                barrier(pool, l, 9)
                barrier(pool, l, 10)

                def attn_prep(t, p, i):
                    n = l * NT + t
                    pool.wait_ge(sums_made, nth(l, t, 3, 4) + 1)
                    pool.tensor_tensor(stat[:, 16:26], stat[:, 0:10], minus_half[:, 0:10], ALU.pow).then_inc(inv_rms, 1)
                    pool.wait_ge(scaled, nth(l, t, 3, 4) + 1)
                    qk5 = qk[:].rearrange("p h (a s f) -> p h a s f", a=2, s=2)
                    t5 = a_sq[:].rearrange("p h (a s f) -> p h a s f", a=2, s=2)
                    for s in range(2):
                        sin = rope[:, t, 1].rearrange("p (a s f) -> p a s f", a=2, s=2)[:, :, s]
                        last = pool.tensor_tensor(t5[:, :, :, s], qk5[:, :, :, 1 - s], sin.unsqueeze(1).broadcast_to([P, 10, 2, 16]), ALU.mult)
                    last.then_inc(a_sin, 1)
                tiles(pool, attn_prep)
                barrier(pool, l, 11)

                def set_queries(t, u, wait=True):
                    if wait:
                        pool.wait_ge(at_s, (l * NT + t - 1) * AH)
                        pool.sem_inc(waits_held, 1)
                    pool.tensor_copy(q_now[u][:], q_stack[:, t]).then_inc(q_set, 1)
                set_queries(0, 0, False)
                set_queries(1, 1, False)
                with pool.Fori(0, 3) as i:
                    for u in range(2):
                        set_queries(i * 2 + (u + 2), u)
                set_queries(NS, 0)
                barrier(pool, l, 12)
                barrier(pool, l, 13)

                for blk in range(KT):
                    b = blk % 2
                    pool.wait_ge(x_new, l * KT + blk + 1)
                    pool.sem_inc(waits_held, 1)
                    pool.dma_start(x_d[blk], wide[b][:]).then_inc(x_out[b], 16)
                    pool.wait_ge(x_out[b], l * 64 + 16 * (blk // 2) + 16)
                    pool.sem_inc(wide_free[b], 1)
                barrier(pool, l, 14)

            for t in range(NT):
                pool.wait_ge(f_ms, t + 1)
                pool.tensor_tensor(r_tok[:, t:t + 1], stat[:, 25:26], minus_half[:, 0:1], ALU.pow).then_inc(f_r, 1)

        @block.vector
        def _(dve):
            for b in range(2):
                dve.sem_inc(w_ready[b], 1)
                dve.sem_inc(acc_free[b], 1)
            dve.wait_ge(cond_th, 1)
            dve.scalar_tensor_tensor(cond[:], stat[:, 0:24], 1.0, bank(7, 24), ALU.add, ALU.mult)
            dve.drain()
            dve.tensor_scalar(cond[:], cond[:], 0.5, None, ALU.mult)
            first_barrier(dve)

            def diagonals(u):
                dve.wait_ge(n_r, u + 1)
                for t in range(NT):
                    last = dve.tensor_scalar(r_diag[:, t], ident, r_tok[:, t:t + 1], None, ALU.mult)
                last.then_inc(n_diag, 1)

            with dve.Fori(0, DEPTH) as l:
                for k in range(1, KT):
                    dve.drain()
                    dve.wait_ge(n_sq, l * KT + k + 1)
                    dve.tensor_tensor(tmp[:], tmp[:], wide[k % 2][:], ALU.add).then_inc(n_add, 1)
                dve.wait_ge(n_mm, l + 1)
                dve.tensor_scalar(stat[:, 0:NT], bank(2, NT), 1.0 / D_MODEL, EPS, ALU.mult, ALU.add).then_inc(n_ms, 1)
                dve.wait_ge(vec_t, l + 1)
                dve.tensor_copy(vec[:], bank(0, NV))
                dve.tensor_scalar(half_vec[:], bank(0, NV), 0.5, None, ALU.mult)
                dve.tensor_scalar(qk_gain[:, 0:AH], qk_gain[:, 0:AH], AD ** -0.5, None, ALU.mult)
                diagonals(l * 2)
                dve.wait_ge(mod_col, l + 1)
                dve.tensor_tensor(mod[:], bank(1, 48).rearrange("p (k c) -> p k c", c=2), over(vec[:, V_BMOD:V_BMOD + 24], 2), ALU.add)
                dve.drain()
                dve.scalar_tensor_tensor(gain[:], mod[:, 8:16], 1.0, over(vec[:, 0:KT], 2), ALU.add, ALU.mult)
                dve.tensor_scalar(half_gate[:], mod[:, 16:24], 0.5, None, ALU.mult)
                dve.drain()
                dve.wait_ge(n_row, l * 2 + 1)

                def scale_block(k):
                    for c, (lo, hi) in enumerate(((0, SAMPLE), (SAMPLE, T))):
                        last = dve.scalar_tensor_tensor(wide[k % 2][:, lo:hi], x_sb[:, k, lo:hi], gain[:, k, c:c + 1], row_bc[:, lo:hi], ALU.mult, ALU.mult)
                    last.then_inc(n_t, 1)
                scale_block(0)
                for k in range(KT):
                    dve.drain()
                    if k + 1 < KT:
                        scale_block(k + 1)
                    dve.wait_ge(n_h, l * KT + k + 1)
                    for c, (lo, hi) in enumerate(((0, SAMPLE), (SAMPLE, T))):
                        dve.scalar_tensor_tensor(h_lo[:, k, lo:hi], wide[k % 2][:, lo:hi], mod[:, k, c:c + 1], h_hi[:, k, lo:hi].bitcast(F32), ALU.add, ALU.subtract)
                dve.wait_ge(coef_e, l + 1)
                dve.tensor_scalar(coef[:], coef[:], -1.0, None, ALU.mult)
                barrier(dve, l, 0)

                for b in range(2):
                    for c in (0, SAMPLE + 1, T + 2):
                        dve.memset(conv_in[b][:, c:c + 1], 0.0)
                split_group(dve, l, 0, 0, 0, KT)
                split_group(dve, l, 1, 1, 0, KT)
                base, stored, conv, th = G_PROJ, 0, 0, 0
                for kind, pairs, col, blk0 in PROJ_RUNS:
                    def body(n, p, m, j, kind=kind, st=stored, cv=conv, tq=th):
                        for b in range(2):
                            if kind.startswith("conv"):
                                v0 = V_GCONV if kind == "conv_gdn" else V_SCONV
                                tap = lambda w: half_vec[:, one(j * 2 + (v0 + 12 * w + b))]
                                bias = half_vec[:, one(j * 2 + (V_SBIAS + b))] if kind == "conv_ssm" else 0.0
                                dve.wait_ge(acc_free[b], l * NG + n + 2)
                                out = conv_out[b][:, 0:T + 1]
                                dve.tensor_scalar(out, conv_in[b][:, 1:T + 2], tap(1), bias, ALU.mult, ALU.add)
                                dve.drain()
                                dve.scalar_tensor_tensor(out, conv_in[b][:, 0:T + 1], tap(0), out, ALU.mult, ALU.add)
                                dve.drain()
                                dve.scalar_tensor_tensor(out, conv_in[b][:, 2:T + 3], tap(2), out, ALU.mult, ALU.add).then_inc(conv_mid[b], 1)
                                dve.wait_ge(th_ready[b], l * 20 + j + (tq + 1))
                                dve.scalar_tensor_tensor(leave[b][:, 0:T + 1], leave[b][:, 0:T + 1], 1.0, out, ALU.add, ALU.mult).then_inc(leave_ready[b], 1)
                            elif kind == "silu":
                                dve.wait_ge(th_ready[b], l * 20 + j + (tq + 1))
                                dve.scalar_tensor_tensor(thirds(leave[b][:, 0:T]), thirds(leave[b][:, 0:T]), 1.0, acc(b), ALU.add, ALU.mult).then_inc(leave_ready[b], 1)
                                dve.drain().then_inc(acc_free[b], 1)
                        if isinstance(n, int) and n + 2 == 11:
                            dve.wait_ge(dt_loaded, l * 16 + 16)
                        if not (isinstance(n, int) and n + 2 >= G_SSM):
                            split_group(dve, l, n + 2, p, m + 1, KT)
                    if pairs == 1:
                        for j in range(2):
                            body(base + j, j, base // 2, j)
                    elif kind == "tanh":
                        groups(dve, base, 2 * pairs - 2, body)
                        for j in range(2):
                            body(base + 2 * pairs - 2 + j, j, base // 2 + pairs - 1, 2 * pairs - 2 + j)
                    else:
                        groups(dve, base, 2 * pairs, body)
                    stored += 1 if kind == "kv_small" else 2 * pairs
                    conv += 2 * pairs if kind.startswith("conv") else 0
                    th += 2 * pairs if kind.startswith("conv") or kind == "silu" else 0
                    base += 2 * pairs
                barrier(dve, l, 1)

                dve.wait_ge(decay_prod, l * 2 + 1)
                D = {k: v[:] for k, v in dec.items()}
                pre_ps = bank(0, 432).rearrange("p (t c) -> p t c", c=48)
                dve.tensor_copy(D["pre"][:, :, 0:8], pre_ps[:, :, 0:8])
                dve.tensor_tensor(D["pre"][:, :, 8:48], pre_ps[:, :, 8:48], again(rows[:, 40:80], NT), ALU.add)
                dve.drain()
                dve.tensor_scalar(D["neg"], D["pre"], -1.0, None, ALU.mult)
                dve.tensor_scalar(D["low"], D["pre"], 0.0, None, ALU.min)
                dve.drain()
                dve.tensor_tensor(D["neg"], D["neg"], D["pre"], ALU.min).then_inc(decay_term, 1)
                dve.wait_ge(decay_exp, l * 2 + 1)
                dve.tensor_scalar(D["u"], D["e_abs"], 2.0, None, ALU.add)
                dve.drain()
                dve.reciprocal(D["u"], D["u"])
                dve.drain()
                dve.tensor_tensor(D["s"], D["u"], D["e_abs"], ALU.mult)
                dve.drain()
                dve.tensor_tensor(D["s2"], D["s"], D["s"], ALU.mult)
                dve.drain()
                dve.tensor_scalar(D["poly"], D["s2"], 1.0 / 17.0, None, ALU.mult)
                for c in (15, 13, 11, 9, 7, 5, 3):
                    dve.drain()
                    dve.scalar_tensor_tensor(D["poly"], D["poly"], 1.0 / c, D["s2"], ALU.add, ALU.mult)
                dve.drain()
                dve.scalar_tensor_tensor(D["poly"], D["poly"], 1.0, D["s"], ALU.add, ALU.mult)
                dve.tensor_scalar(D["u"], D["pre"], 0.0, None, ALU.max)
                dve.drain()
                dve.scalar_tensor_tensor(D["soft"], D["poly"], 2.0, D["u"], ALU.mult, ALU.add)
                dve.tensor_scalar(D["s"], D["e_abs"], 1.0, None, ALU.add)
                dve.drain()
                dve.reciprocal(D["s"], D["s"])
                dve.drain()
                dve.tensor_tensor(beta[:].rearrange("p t d h -> p t (d h)"), D["e_low"][:, :, 0:8], D["s"][:, :, 0:8], ALU.mult)
                dve.tensor_copy(dt_[:].rearrange("p t d h -> p t (d h)"), D["soft"][:, :, 16:48])
                for d in range(2):
                    dve.tensor_tensor(logd[:, :, d, 0:4], D["soft"][:, :, 8 + 4 * d:12 + 4 * d], again(coef[:, d, 0:4], NT), ALU.mult)
                    last = dve.tensor_tensor(logd[:, :, d, 4:20], D["soft"][:, :, 16 + 16 * d:32 + 16 * d], again(coef[:, d, 4:20], NT), ALU.mult)
                last.then_inc(decay_term, 1)
                dve.wait_ge(decay_prod, l * 2 + 2)
                for d in range(2):
                    dve.tensor_copy(cum[:, d].rearrange("p t h -> p (t h)"), bank(1 + d, 180))
                    dve.tensor_copy(tot[:, d].rearrange("p t h -> p (t h)"), bank(3 + d, 180))
                dve.drain()
                dve.tensor_tensor(rest[:], tot[:], cum[:], ALU.subtract).then_inc(decay_term, 1)
                dve.wait_ge(decay_exp, l * 2 + 2)
                for d in range(2):
                    dve.scalar_tensor_tensor(neg_be[:, d], beta[:, :, d], -1.0, e_cum[:, d, :, 0:4], ALU.mult, ALU.mult)
                    dve.tensor_tensor(dt_rest[:, d], dt_[:, :, d], e_rest[:, d, :, 4:20], ALU.mult)
                barrier(dve, l, 2)

                def build_after(t):
                    for half in range(2):
                        hs = slice(8 * half, 8 * half + 8)
                        dve.tensor_tensor(after[:, hs], again(cst[:, C_STRICT], 8), over(logd[:, t, 0, 4 + 8 * half:12 + 8 * half], P), ALU.mult).then_inc(sp_fwd, 1)

                def ssm_prep(t, p, i):
                    n = l * NT + t
                    last_tile = isinstance(t, int) and t == NT - 1
                    dve.wait_ge(transposed, nth(l, t, 0, 5) + 1)
                    if not (isinstance(t, int) and t == 0):
                        dve.wait_ge(sp_bwd, n * 4)
                    for d in range(2):
                        dve.tensor_tensor(cb[d][:], bank(7, 256).rearrange("p (g l) -> p g l", l=P), again(cst[:, C_TRI + d], SG), ALU.mult).then_inc(sp_fwd, 1)
                    dve.wait_ge(out_ready, nth(l, t, 0, 2) + 1)
                    dve.tensor_tensor(x_dt[0][:], xt[p][:, 0:D_MODEL].rearrange("p (h q) -> p h q", q=SP_), over(dt_[:, t, 0], SP_), ALU.mult)
                    dve.drain()
                    for g in range(SG):
                        dve.wait_ge(sp_e, n * 2 + 1 + g)
                        dve.tensor_tensor(w_f[:, 8 * g:8 * g + 8], e_ssm[:, 8 * g:8 * g + 8], again(cb[0][:, g], 8), ALU.mult).then_inc(sp_fwd, 1)
                    if not last_tile:
                        build_after(t + 1)
                    dve.wait_ge(sp_y, n + 1)
                    dve.wait_ge(sp_dx, n + 1)
                    dve.tensor_tensor(y_acc[:, t], PSUM[:, 0:D_MODEL], d_x[:].rearrange("p h q -> p (h q)"), ALU.add).then_inc(sp_yd, 1)
                build_after(0)
                ssm_prep(0, 0, 0)
                ssm_prep(1, 1, 0)
                with dve.Fori(0, 3) as i:
                    for p in range(2):
                        ssm_prep(i * 2 + (p + 2), p, i + 1)
                ssm_prep(NT - 1, 0, 4)
                barrier(dve, l, 3)

                def ssm_step(t, p, i):
                    n = l * NT + t
                    if isinstance(t, int):
                        for d in range(2):
                            dve.memset(s_ssm[d][:], 0.0).then_inc(state[d], 1)
                    for d in range(2):
                        tt = t if isinstance(t, int) or d == 0 else (NS - 1) - t
                        dve.wait_ge(ssm_prod[d], n * 2 + 1)
                        dve.sem_inc(waits_held, 1)
                        dve.tensor_tensor(y_tmp[d][:].rearrange("p (h q) -> p h q", q=SP_), PSUM[:, 2048 * d:2048 * d + 1024].rearrange("p (h q) -> p h q", q=SP_),
                                          over(e_cum[:, d, tt, 4:20], SP_), ALU.mult)
                        dve.wait_ge(ssm_prod[d], n * 2 + 2)
                        dve.sem_inc(waits_held, 1)
                        dve.wait_ge(ssm_side[d], n * 2 + 2)
                        dve.tensor_tensor(s_ssm[d][:], s_kept[d][:], PSUM[:, 2048 * d + 1024:2048 * d + 2048], ALU.add).then_inc(state[d], 1)
                        dve.drain()
                        dve.tensor_tensor(y_acc[:, tt], y_acc[:, tt], y_tmp[d][:], ALU.add)
                tiles(dve, ssm_step)
                barrier(dve, l, 4)

                def ssm_post(t, p, i):
                    n = l * NT + t
                    dve.wait_ge(tile_in[p], loaded(l, p, i, 1))
                    dve.wait_ge(transposed, nth(l, t, 1, 5) + 1)
                    dve.tensor_tensor(yz[:], PSUM[:, 0:1024].rearrange("p (k t) -> p k t", t=P), z_c[p][:], ALU.mult).then_inc(gated, 1)
                    dve.wait_ge(sums_made, nth(l, t, 0, 4) + 1)
                    dve.tensor_copy(stat[:, one(t)], bank(2, 1)).then_inc(y_ss_read, 1)
                    dve.wait_ge(hi_made, nth(l, t, 0, 3) + 1)
                    dve.tensor_tensor(b_lo[:, :, cols(t)], yzw[:], b_hi[:, :, cols(t)].bitcast(F32), ALU.subtract).then_inc(lo_made, 1)
                tiles(dve, ssm_post)
                dve.drain()
                dve.tensor_scalar(stat[:, 0:NT], stat[:, 0:NT], 1.0 / D_MODEL, 4 * EPS, ALU.mult, ALU.add).then_inc(n_ms, 1)
                diagonals(l * 2 + 1)
                barrier(dve, l, 5)

                def branch(base, kt, merge):
                    for j in range(2):
                        split_group(dve, l, base + j, j, base // 2, kt)
                    for j in range(4):
                        n, p = base + j, j % 2
                        for b in range(2):
                            dve.drain()
                            dve.wait_ge(acc_ready[b], acc_done(l, n, b))
                            dve.wait_ge(wide_in[b], l * 256 + 16 * (n - G_SSM) + 16)
                            merge(2 * j + b, b)
                        if j < 2:
                            split_group(dve, l, n + 2, p, base // 2 + 1, kt)

                def merge_first(blk, b):
                    dve.tensor_tensor(thirds(tmp[:]), acc(b), thirds(row_bc[:]), ALU.mult)
                    dve.drain().then_inc(acc_free[b], 1)
                    dve.scalar_tensor_tensor(merged[:, blk], wide[b][:], 1.0, tmp[:], ALU.add, ALU.mult).then_inc(wide_free[b], 1)

                def merge_more(blk, b):
                    dve.scalar_tensor_tensor(thirds(tmp[:]), thirds(wide[b][:]), 1.0, acc(b), ALU.add, ALU.mult)
                    dve.drain().then_inc(acc_free[b], 1)
                    dve.tensor_tensor(merged[:, blk], merged[:, blk], tmp[:], ALU.add).then_inc(wide_free[b], 1)

                def merge_out(blk, b):
                    w = thirds(wide[b][:])
                    dve.scalar_tensor_tensor(w[:, 0:2], acc(b)[:, 0:2], half_gate[:, blk, 0:1], w[:, 0:2], ALU.mult, ALU.add)
                    for c, (lo, hi) in enumerate(((0, THIRD - PROMPT), (THIRD - PROMPT, THIRD))):
                        last = dve.scalar_tensor_tensor(w[:, 2, lo:hi], acc(b)[:, 2, lo:hi], half_gate[:, blk, c:c + 1], w[:, 2, lo:hi], ALU.mult, ALU.add)
                    last.then_inc(x_new, 1)
                    dve.drain().then_inc(acc_free[b], 1)
                branch(G_SSM, 8, merge_first)
                barrier(dve, l, 6)

                def gdn_prep(t, p, i):
                    n = l * NT + t
                    dve.wait_ge(squared, nth(l, t, 1, 4) + 1)
                    dve.tensor_reduce(stat[:, 0:8], g_sq[:], AX_X, ALU.add)
                    dve.drain()
                    dve.tensor_scalar(stat[:, 0:4], stat[:, 0:4], EPS, float(GD), ALU.add, ALU.mult)
                    dve.tensor_scalar(stat[:, 4:8], stat[:, 4:8], EPS, None, ALU.add).then_inc(sums_made, 1)
                    dve.wait_ge(inv_rms, nth(l, t, 0, 3) + 1)
                    dve.tensor_tensor(q_n[:], bank(0).rearrange("p (h d) -> p h d", d=GD), over(stat[:, 8:12], GD), ALU.mult)
                    dve.tensor_tensor(g_out[p][:, 2].rearrange("p (h d) -> p h d", d=GD), bank(1).rearrange("p (h d) -> p h d", d=GD), over(stat[:, 12:16], GD), ALU.mult).then_inc(scaled, 1)
                tiles(dve, gdn_prep)
                barrier(dve, l, 7)

                for d in range(2):
                    dve.wait_ge(state_in[d], l * 32 + 32)
                    dve.sem_inc(waits_held, 1)
                    dve.drain().then_inc(state[d], 1)
                dve.wait_ge(o_zero, l + 1)
                dve.sem_inc(waits_held, 1)

                def heads(x):
                    return x.rearrange("p (h t) -> p h t", t=P)

                def gdn_step(t, p, i):
                    n = l * NT + t
                    tile_of = lambda d: t if isinstance(t, int) or d == 0 else (NS - 1) - t
                    if isinstance(t, int):
                        for d in range(2):
                            dve.memset(gd[d]["S"][:], 0.0).then_inc(state[d], 1)
                    for d in range(2):
                        tt = tile_of(d)
                        dve.tensor_copy(gd[d]["col"][:, 0:4], over(logd[:, tt, d, 0:4], P))
                        dve.tensor_copy(gd[d]["col"][:, 4:8], over(beta[:, tt, d], P)).then_inc(g_term[d], 1)
                    for d in range(2):
                        tt = tile_of(d)
                        dve.wait_ge(g_row[d], n * 2 + 1)
                        for h in range(GH):
                            last = dve.tensor_scalar(gd[d]["E"][:, h], bank(4 * d + 3, P, h * P), cum[:, d, tt, h:h + 1], 0.0, ALU.subtract, ALU.min)
                        last.then_inc(g_term[d], 1)
                    for d in range(2):
                        dve.wait_ge(g_side[d], n * 5 + 4)
                        dve.tensor_tensor(gd[d]["A"][:], gd[d]["A0"][:], heads(bank(4 * d)), ALU.mult).then_inc(g_term[d], 1)
                    for d in range(2):
                        g = gd[d]
                        dve.drain()
                        dve.tensor_tensor(g["Y"][:], g["A"][:], again(cst[:, C_LV + 7 * (1 - d)], GH), ALU.mult)
                        dve.wait_ge(g_row[d], n * 2 + 2)
                        dve.tensor_tensor(g["X"][:], heads(bank(4 * d + 3)), again(cst[:, C_LV + 7 * d], GH), ALU.mult)
                        dve.drain()
                        dve.tensor_tensor(g["Y"][:], g["Y"][:], again(ident, GH), ALU.add)
                        dve.tensor_tensor(g["X"][:], g["X"][:], again(ident, GH), ALU.add).then_inc(g_x[d], 1)
                    for lev in range(1, 7):
                        for d in range(2):
                            dve.wait_ge(g_level[d], n * 12 + 2 * lev - 1)
                            dve.tensor_tensor(gd[d]["T"][:], heads(bank(4 * d)), again(cst[:, C_LV + 7 * d + lev], GH), ALU.mult).then_inc(g_tm[d], 1)
                    for d in range(2):
                        g, tt = gd[d], tile_of(d)
                        dve.wait_ge(g_from_s[d], n * 2 + 1)
                        dve.tensor_tensor(g["R0"][:], heads(bank(4 * d)), over(neg_be[:, d, tt], P), ALU.mult)
                        dve.drain()
                        dve.wait_ge(g_side[d], n * 5 + 1)
                        dve.tensor_tensor(g["R"][:], g["R0"][:], g["VB"][:], ALU.add).then_inc(g_term[d], 1)
                    for d in range(2):
                        g, tt = gd[d], tile_of(d)
                        dve.wait_ge(g_from_s[d], n * 2 + 2)
                        dve.tensor_tensor(g["O"][:], heads(bank(4 * d + 3)), over(e_cum[:, d, tt, 0:4], P), ALU.mult)
                        dve.drain()
                        dve.tensor_tensor(o_acc[:, tt], o_acc[:, tt], g["O"][:].rearrange("p h t -> p (h t)"), ALU.add)
                    for d in range(2):
                        g, tt = gd[d], tile_of(d)
                        dve.wait_ge(g_from_v[d], n * 2 + 1)
                        dve.wait_ge(g_side[d], n * 5 + 3)
                        dve.tensor_tensor(g["S"][:], g["SK"][:], heads(bank(4 * d)), ALU.add).then_inc(state[d], 1)
                        dve.drain()
                        dve.wait_ge(g_from_v[d], n * 2 + 2)
                        dve.tensor_tensor(o_acc[:, tt], o_acc[:, tt], bank(4 * d + 2), ALU.add).then_inc(g_step[d], 1)
                tiles(dve, gdn_step)
                barrier(dve, l, 8)

                def gdn_post(t, p, i):
                    n = l * NT + t
                    dve.wait_ge(squared, nth(l, t, 2, 4) + 1)
                    dve.tensor_reduce(stat[:, 0:4], o_sq[:], AX_X, ALU.add)
                    dve.drain()
                    dve.tensor_scalar(stat[:, 0:4], stat[:, 0:4], 1.0 / GD, EPS, ALU.mult, ALU.add).then_inc(sums_made, 1)
                    dve.wait_ge(inv_rms, nth(l, t, 1, 3) + 1)
                    dve.tensor_tensor(o_st[p][:], o_acc[:, t].rearrange("p (h d) -> p h d", d=GD), over(stat[:, 8:12], GD), ALU.mult).then_inc(scaled, 1)
                    dve.wait_ge(tile_in[p], loaded(l, p, i, 3))
                    dve.wait_ge(transposed, nth(l, t, 3, 5) + 1)
                    dve.scalar_tensor_tensor(o_z[:], heads(bank(p)), half_vec[:, V_GNORM:V_GNORM + 1], z_a[p][:], ALU.mult, ALU.mult).then_inc(gated, 1)
                    dve.wait_ge(hi_made, nth(l, t, 1, 3) + 1)
                    dve.tensor_tensor(b_lo[:, 0:4, cols(t)], o_z[:], b_hi[:, 0:4, cols(t)].bitcast(F32), ALU.subtract).then_inc(lo_made, 1)
                tiles(dve, gdn_post)
                barrier(dve, l, 9)
                branch(G_GDN, 4, merge_more)
                barrier(dve, l, 10)

                def split_k(src):
                    dve.tensor_copy(k_hh[:, :, 0:AD], src)
                    dve.tensor_copy(k_hh[:, :, AD:P], src)
                    dve.drain()
                    dve.tensor_tensor(k_ll[:, :, 0:AD], src, k_hh[:, :, 0:AD].bitcast(F32), ALU.subtract)
                    return dve.tensor_tensor(k_ll[:, :, AD:P], src, k_hh[:, :, 0:AD].bitcast(F32), ALU.subtract)

                def place_k(n, t):
                    dve.wait_ge(a_st, n + 1)
                    dve.tensor_copy(k_hi[:, :, cols(t)], bank(4)[:, 0:256].rearrange("p (g t) -> p g t", t=P))
                    dve.tensor_copy(k_lo[:, :, cols(t)], bank(4)[:, 256:512].rearrange("p (g t) -> p g t", t=P)).then_inc(a_k, 1)

                def attn_prep(t, p, i):
                    n, n1 = l * NT + t, l * (NT + 1) + t
                    ps = PSUM[:, 0:640].rearrange("p (h d) -> p h d", d=AD)
                    dve.wait_ge(squared, nth(l, t, 3, 4) + 1)
                    dve.tensor_reduce(stat[:, 0:10], a_sq[:], AX_X, ALU.add)
                    dve.drain()
                    dve.tensor_scalar(stat[:, 0:10], stat[:, 0:10], 1.0 / AD, EPS, ALU.mult, ALU.add).then_inc(sums_made, 1)
                    dve.wait_ge(inv_rms, nth(l, t, 2, 3) + 1)
                    dve.wait_ge(a_v, n + 1)
                    dve.tensor_tensor(qk[:], ps, over(stat[:, 16:26], AD), ALU.mult)
                    dve.drain()
                    dve.tensor_tensor(qk[:], qk[:], qk_gain[:], ALU.mult).then_inc(scaled, 1)
                    dve.drain()
                    dve.tensor_tensor(qk_c[:], qk[:], again(rope[:, t, 0], 10), ALU.mult)
                    dve.drain()
                    dve.wait_ge(a_sin, n + 1)
                    dve.tensor_tensor(qk[:], qk_c[:], a_sq[:], ALU.add).then_inc(qk_done, 1)
                    dve.drain()
                    dve.tensor_copy(q_hl[:, :, 0:AD], qk[:, 0:AH])
                    dve.drain()
                    dve.tensor_tensor(q_hl[:, :, AD:P], qk[:, 0:AH], q_hl[:, :, 0:AD].bitcast(F32), ALU.subtract)
                    split_k(qk[:, AH:10]).then_inc(a_split, 1)
                    place_k(n1, t)
                tiles(dve, attn_prep)
                dve.wait_ge(past_in, l * 32 + 32)
                split_k(ain[1][:, 0].rearrange("p (g d) -> p g d", d=AD)).then_inc(a_split, 1)
                place_k(l * (NT + 1) + NT, NT)
                barrier(dve, l, 11)

                def head_max(t, u, h):
                    nk = 1 if isinstance(t, int) and t == NS else 9
                    dve.wait_ge(at_s, (l * NT + t) * AH + h + 1)
                    dve.tensor_reduce(row_max[:, u, h:h + 1], PSUM[:, 1536 * (h % 2):1536 * (h % 2) + nk * P], AX_X, ALU.max, negate=True).then_inc(at_m, 1)

                def attn(t, u, nk):
                    n = l * NT + t
                    for h in range(AH):
                        if h + 1 < AH:
                            head_max(t, u, h + 1)
                        elif nk > 1:
                            head_max(t + 1, 1 - u, 0)
                        dve.wait_ge(at_t[0], n * AH + h + 1)
                        w = min(nk, 4)
                        dve.tensor_copy(prob_t[h % 2][:, 0:w], bank(6, w * P).rearrange("p (j t) -> p j t", t=P)).then_inc(at_c[0], 1)
                    dve.reciprocal(inv_sum[:], row_sum[:, u])
                    dve.drain()
                    dve.tensor_scalar(inv_sum[:], inv_sum[:], 0.5, None, ALU.mult)
                    dve.drain()
                    dve.wait_ge(at_v, n * AH + AH)
                    dve.tensor_tensor(o_att[:], bank(7).rearrange("p (h d) -> p h d", d=AD), over(inv_sum[:], AD), ALU.mult).then_inc(o_norm, 1)
                    dve.wait_ge(zb_in, n * 16 + 16)
                    dve.wait_ge(o_tr, n + 1)
                    dve.tensor_tensor(o_bz[:], heads(bank(6)), z_b[:], ALU.mult).then_inc(gated, 1)
                    dve.wait_ge(hi_made, nth(l, t, 2, 3) + 1)
                    dve.tensor_tensor(b_lo[:, 0:4, cols(t)], o_bz[:], b_hi[:, 0:4, cols(t)].bitcast(F32), ALU.subtract).then_inc(lo_made, 1)
                head_max(0, 0, 0)
                with dve.Fori(0, 3) as i:
                    for u in range(2):
                        attn(i * 2 + u, u, 9)
                attn(6, 0, 9)
                attn(7, 1, 9)
                attn(NS, 0, 1)
                barrier(dve, l, 12)
                branch(G_ATT, 4, merge_more)
                barrier(dve, l, 13)

                for k in range(KT):
                    dve.wait_ge(m_hi, l * KT + k + 1)
                    dve.tensor_tensor(b_lo[:, k], merged[:, k], b_hi[:, k].bitcast(F32), ALU.subtract).then_inc(m_lo, 1)
                branch(G_OUT, 8, merge_out)
                barrier(dve, l, 14)

            dve.wait_ge(f_in, 16)
            for t in range(NT):
                dve.wait_ge(f_sq, t + 1)
                dve.tensor_scalar(stat[:, 25:26], stat[:, 16 + t:17 + t], 1.0 / D_MODEL, EPS, ALU.mult, ALU.add).then_inc(f_ms, 1)
                dve.wait_ge(f_r, t + 1)
                if t >= 2:
                    dve.wait_ge(f_out[t % 2], 16 * (t // 2))
                dve.scalar_tensor_tensor(x_tok[t % 2][:], PSUM[:, 1024 * (t % 2):1024 * (t % 2) + 1024], r_tok[:, t:t + 1], f_gain[:], ALU.mult, ALU.mult).then_inc(f_y, 1)


_INS = ["x_prompt", "x_sample", "cache_k", "cache_v", "state_gdn", "state_ssm", "c", "c_ctx", "norm_w", "w_mod",
        "b_mod", "w_in", "gdn_conv_w", "gdn_a_log", "gdn_dt_bias", "gdn_norm_w", "attn_q_norm", "attn_k_norm",
        "ssm_conv_w", "ssm_conv_b", "ssm_a_log", "ssm_dt_bias", "ssm_d", "ssm_norm_w", "w_branch_a", "w_branch_b",
        "w_branch_c", "w_out", "final_norm_w"]
_OUTS = [("y_prompt", (1, PROMPT, D_MODEL)), ("y_sample", (1, SAMPLE, D_MODEL)),
         ("cache_k", (1, DEPTH, PROMPT, KVH, AD)), ("cache_v", (1, DEPTH, PROMPT, KVH, AD)),
         ("state_gdn", (1, DEPTH, 2, GH, GD, GD)), ("state_ssm", (1, DEPTH, 2, SH, SP_, SN))]


def kernel(**inputs):
    import numpy as _np
    import concourse.bacc as _bacc
    from concourse.bass_utils import run_bass_kernel_spmd as _run

    nc = _bacc.Bacc("TRN2", target_bir_lowering=False, num_devices=1)
    arrays, ins, outs = {}, {}, {}
    for name in _INS:
        arrays[f"in_{name}"] = _np.ascontiguousarray(inputs[name])
        ins[name] = nc.dram_tensor(f"in_{name}", arrays[f"in_{name}"].shape, F32, kind="ExternalInput").ap()
    tables = []
    for name, a in zip(("table", "rope_table"), constants()):
        arrays[name] = a
        tables.append(nc.dram_tensor(name, a.shape, F32, kind="ExternalInput").ap())
    for name, shape in _OUTS:
        outs[name] = nc.dram_tensor(f"out_{name}", shape, F32, kind="ExternalOutput").ap()
    backbone_kernel(nc, ins, outs, *tables)
    r = _run(nc, [arrays], core_ids=[0])
    return tuple(r.results[0][f"out_{name}"] for name, _ in _OUTS)
```

```python
from contextlib import ExitStack

import numpy as np

import concourse.bass as bass
from concourse import mybir

ALU = mybir.AluOpType
ACT = mybir.ActivationFunctionType
F32 = mybir.dt.float32
F32R = mybir.dt.float32r
AX_X = mybir.AxisListType.X

P = 128
DEPTH = 2
D_MODEL = 1024
KT = D_MODEL // P
SAMPLE = 1024
PROMPT = 128
T = SAMPLE + PROMPT
NT = T // P
NS = SAMPLE // P
EPS = 1e-6
GH, GD = 4, 128
AH, KVH, AD = 8, 2, 64
SH, SP_, SG, SN = 16, 64, 2, 128
PAST = 128
IN_WIDTH = 9008
GW = 256
THIRD = T // 3

PROJ_RUNS = (
    ("conv_gdn", 3, 0, 0),
    ("silu", 1, 1536, 12),
    ("plain", 1, 2064, 16),
    ("kv_small", 1, 2576, 20),
    ("silu", 1, 2832, 22),
    ("conv_ssm", 3, 3344, 26),
    ("silu", 2, 4880, 38),
    ("tanh", 6, 5936, 46),
)
BETA_COL, DT_COL = 2048, 5904
NB_PROJ = 70
B_GDN, B_ZA, B_ATT, B_ZB, B_XBC, B_ZC, B_GATE = 0, 12, 16, 22, 26, 38, 46
G_PROJ, G_SSM, G_GDN, G_ATT, G_OUT, NG = 0, 36, 40, 44, 48, 52

V_NORM, V_BMOD, V_GCONV, V_SCONV, V_SBIAS, V_SNORM, V_GNORM, NV = 0, 8, 32, 68, 104, 116, 124, 125

K_KT, K_QT, K_K, K_V, K_KQ = 1, 2, 3, 4, 5
K_KK = (0, 6)

LEVELS = (1, 2, 4, 8, 16, 32, 64)
C_ID, C_TRI, C_STRICT, C_ONE, C_LV = 0, 1, 3, 5, 6
NC_ = 6 + 2 * len(LEVELS)
NPH = 15


def constants():
    i = np.arange(P)
    t = np.zeros((P, NC_, P), np.float32)
    t[:, C_ID] = np.eye(P)
    t[:, C_TRI] = i[:, None] <= i[None, :]
    t[:, C_TRI + 1] = i[:, None] >= i[None, :]
    t[:, C_STRICT] = i[:, None] > i[None, :]
    t[:, C_STRICT + 1] = i[:, None] < i[None, :]
    t[:, C_ONE] = 1.0
    for n, b in enumerate(LEVELS):
        r, c = i[:, None] // b, i[None, :] // b
        t[:, C_LV + n] = -1.0 * ((r % 2 == 1) & (c == r - 1))
        t[:, C_LV + len(LEVELS) + n] = t[:, C_LV + n].T
    rot = AD // 2
    freqs = 10000.0 ** (-np.arange(rot // 2, dtype=np.float32) / (rot // 2))
    pos = np.arange(SAMPLE)
    cs = np.zeros((T, 2, 2, 2, rot // 2), np.float32)
    cs[:, 0] = 1.0
    for axis, x in enumerate((pos // 64, pos % 64)):
        ang = x.astype(np.float32)[:, None] * freqs.astype(np.float32)
        cs[:SAMPLE, 0, axis, 0] = cs[:SAMPLE, 0, axis, 1] = np.cos(ang)
        cs[:SAMPLE, 1, axis, 0] = -np.sin(ang)
        cs[:SAMPLE, 1, axis, 1] = np.sin(ang)
    cs = cs.reshape(NT, P, 2 * AD).transpose(1, 0, 2)
    return t.reshape(P, NC_ * P), np.ascontiguousarray(cs).reshape(P, NT * 2 * AD)


def over(ap, n):
    return ap.unsqueeze(2).broadcast_to([ap.shape[0], ap.shape[1], n])


def again(ap, n):
    return ap.unsqueeze(1).broadcast_to([ap.shape[0], n, ap.shape[1]])


def backbone_kernel(nc, A, O, table, rope_table):
    with ExitStack() as ctx:
        sem_of = {}

        def sem(name):
            if name not in sem_of:
                sem_of[name] = ctx.enter_context(nc.semaphore(name))
            return sem_of[name]

        def dram(name, shape):
            return nc.dram_tensor(name, shape, F32, kind="Internal").ap()

        x_d = dram("x_d", [KT, P, T])
        proj_d = dram("proj_d", [NB_PROJ, P, T])
        ssm_tok_d = dram("ssm_tok_d", [NT, P, 1280])
        gdn_tile_d = dram("gdn_tile_d", [NT, P, 7, 512])

        base = 16512
        top = [base]

        def fixed(name, shape, dt=F32):
            size = int(np.prod(shape[1:])) * 4
            t = nc.alloc_sbuf_tensor_at(name, shape, dt, offset=top[0])
            top[0] += (size + 31) // 32 * 32
            return t

        def region(size):
            start = top[0]
            top[0] += size
            return [start, start, start + size]

        def place(r, name, shape, dt=F32):
            size = (int(np.prod(shape[1:])) * 4 + 31) // 32 * 32
            assert r[1] + size <= r[2], (name, r, size)
            t = nc.alloc_sbuf_tensor_at(name, shape, dt, offset=r[1])
            r[1] += size
            return t

        def fresh(r):
            return [r[0], r[0], r[2]]

        cst = fixed("cst", [P, NC_, P])
        rope = fixed("rope", [P, NT, 2, AD])
        cond = fixed("cond", [P, 24])
        vec = fixed("vec", [P, NV])
        half_vec = fixed("half_vec", [P, NV])
        mod = fixed("mod", [P, 24, 2])
        gain = fixed("gain", [P, KT, 2])
        half_gate = fixed("half_gate", [P, KT, 2])
        rows = fixed("rows", [P, 96])
        coef = fixed("coef", [P, 2, 20])
        qk_gain = fixed("qk_gain", [P, 10, AD])
        beta = fixed("beta", [P, NT, 2, GH])
        dt_ = fixed("dt_", [P, NT, 2, SH])
        logd = fixed("logd", [P, NT, 2, 20])
        cum = fixed("cum", [P, 2, NT, 20])
        tot = fixed("tot", [P, 2, NT, 20])
        e_cum = fixed("e_cum", [P, 2, NT, 20])
        e_tot = fixed("e_tot", [P, 2, NT, 20])
        e_rest = fixed("e_rest", [P, 2, NT, 20])
        neg_e = fixed("neg_e", [P, 2, NT, GH])
        dt_rest = fixed("dt_rest", [P, 2, NT, SH])
        stat = fixed("stat", [P, 32])
        minus_half = fixed("minus_half", [P, 16])
        r_tok = fixed("r_tok", [P, NT])

        ACTV = region(2 * KT * T * 4)
        MRG = region(KT * T * 4)
        WT = region(6 * KT * GW * 4)
        EV = region(229344 - top[0])
        a = fresh(ACTV)
        h_hi = place(a, "h_hi", [P, KT, T], F32R)
        h_lo = place(a, "h_lo", [P, KT, T], F32R)
        a = fresh(ACTV)
        b_hi = place(a, "b_hi", [P, KT, T], F32R)
        b_lo = place(a, "b_lo", [P, KT, T], F32R)
        a = fresh(WT)
        w_raw = [place(a, f"w_raw{n}", [P, KT, GW]) for n in range(2)]
        w_hi = [place(a, f"w_hi{n}", [P, KT, GW], F32R) for n in range(2)]
        w_lo = [place(a, f"w_lo{n}", [P, KT, GW], F32R) for n in range(2)]
        a = fresh(MRG)
        merged = place(a, "merged", [P, KT, T])
        a = fresh(MRG)
        x_sb = place(a, "x_sb", [P, KT, T])
        a = fresh(MRG)
        CW = T + 4
        conv_in = [place(a, f"conv_in{n}", [P, CW]) for n in range(2)]
        conv_out = [place(a, f"conv_out{n}", [P, CW]) for n in range(2)]
        leave = [place(a, f"leave{n}", [P, CW]) for n in range(2)]
        a = fresh(EV)
        row_bc = place(a, "row_bc", [P, T])
        wide = [place(a, f"wide{n}", [P, T]) for n in range(2)]
        at_tmp = list(a)
        tmp = place(a, "tmp", [P, T])
        vec_in = place(a, "vec_in", [P, P])

        a = fresh(ACTV)
        xin = [place(a, f"xin{n}", [P, 12, P]) for n in range(2)]
        xt = [place(a, f"xt{n}", [P, 1280]) for n in range(2)]
        after = place(a, "after", [P, SH, P])
        before = place(a, "before", [P, SH, P])
        e_ssm = place(a, "e_ssm", [P, SH, P])
        w_f = place(a, "w_f", [P, SH, P])
        a2 = fresh(WT)
        w_b = place(a2, "w_b", [P, SH, P])
        x_dt = [place(a2, f"x_dt{n}", [P, SH, SP_]) for n in range(2)]
        d_x = place(a2, "d_x", [P, SH, SP_])
        cb = [place(a2, f"cb{n}", [P, 2, SG, P]) for n in range(2)]
        a = fresh(MRG)
        y_acc = place(a, "y_acc", [P, NT, D_MODEL])
        a = fresh(ACTV)
        xs = [[place(a, f"xs{d}{n}", [P, 1280]) for n in range(2)] for d in range(2)]
        c_t = [[place(a, f"c_t{d}{n}", [P, SG, P]) for n in range(2)] for d in range(2)]
        s_ssm = [place(a, f"s_ssm{d}", [P, D_MODEL]) for d in range(2)]
        s_kept = [place(a, f"s_kept{d}", [P, D_MODEL]) for d in range(2)]
        x_in = [place(a, f"x_in{d}", [P, SH, SP_]) for d in range(2)]
        y_tmp = [place(a, f"y_tmp{d}", [P, D_MODEL]) for d in range(2)]
        s_io = [place(a, f"s_io{d}", [P, 8, P]) for d in range(2)]
        a = fresh(WT)
        y_st = [place(a, f"y_st{n}", [P, D_MODEL]) for n in range(2)]
        z_c = [place(a, f"z_c{n}", [P, KT, P]) for n in range(2)]
        yz = [place(a, f"yz{n}", [P, KT, P]) for n in range(2)]
        yzw = [place(a, f"yzw{n}", [P, KT, P]) for n in range(2)]
        y_sq = place(a, "y_sq", [P, KT, P])
        a = fresh(ACTV)
        gin = [place(a, f"gin{n}", [P, 12, P]) for n in range(2)]
        g_sq = place(a, "g_sq", [P, 8, GD])
        q_n = place(a, "q_n", [P, GH, GD])
        g_out = [place(a, f"g_out{n}", [P, 7, 512]) for n in range(2)]
        a = fresh(WT)
        g_t = [[place(a, f"g_t{d}{n}", [P, 6, 512]) for n in range(2)] for d in range(2)]
        a = fresh(ACTV)
        gd = []
        for d in range(2):
            g = {}
            for n in ("col", "E", "Q0", "T", "R0", "R", "V", "KD", "SK", "S"):
                g[n] = place(a, f"g_{n}{d}", [P, GH, GD])
            for n in ("Q", "A", "X", "Y"):
                g[n] = [place(a, f"g_{n}{d}{m}", [P, GH, GD]) for m in range(2)]
            gd.append(g)
        a = fresh(EV)
        o_acc = place(a, "o_acc", [P, NT, 512])
        a = fresh(WT)
        o_st = [place(a, f"o_st{n}", [P, GH, GD]) for n in range(2)]
        z_a = [place(a, f"z_a{n}", [P, GH, P]) for n in range(2)]
        o_sq = place(a, "o_sq", [P, GH, GD])
        o_z = place(a, "o_z", [P, GH, P])
        a = fresh(WT)
        q_stack = place(a, "q_stack", [P, NT, AH, P], F32R)
        q_now = [place(a, f"q_now{n}", [P, AH, P], F32R) for n in range(2)]
        o_att = place(a, "o_att", [P, AH, AD])
        half = ACTV[0] + 4 * T * 4
        a = [half, half, half + 4 * T * 4]
        k_hi = place(a, "k_hi", [P, KVH, 10 * P], F32R)
        v_all = place(a, "v_all", [P, 10, P])
        qk_s = place(a, "qk_s", [P, 10, AD])
        half = ACTV[0] + 12 * T * 4
        a = [half, half, half + 4 * T * 4]
        k_lo = place(a, "k_lo", [P, KVH, 10 * P], F32R)
        z_b = place(a, "z_b", [P, 4, P])
        o_bz = place(a, "o_bz", [P, 4, P])
        row_max = place(a, "row_max", [P, 2, AH])
        row_sum = place(a, "row_sum", [P, 2, AH])
        inv_sum = place(a, "inv_sum", [P, AH])
        a = fresh(EV)
        ain = [place(a, f"ain{n}", [P, 6, P]) for n in range(2)]
        a_sq = place(a, "a_sq", [P, 10, AD])
        qk = place(a, "qk", [P, 10, AD])
        qk_c = place(a, "qk_c", [P, 10, AD])
        q_hl = place(a, "q_hl", [P, AH, P], F32R)
        k_hh = place(a, "k_hh", [P, KVH, P], F32R)
        k_ll = place(a, "k_ll", [P, KVH, P], F32R)
        a = fresh(EV)
        prob = [place(a, f"prob{n}", [P, T]) for n in range(2)]
        prob_t = [place(a, f"prob_t{n}", [P, 9, P]) for n in range(2)]
        a = fresh([ACTV[2] - 12288, 0, ACTV[2]])
        mod_rows = place(a, "mod_rows", [P, 3 * D_MODEL])
        a = fresh(WT)
        w_mod = [place(a, f"w_mod{n}", [P, KT, 2 * GW]) for n in range(3)]
        a = fresh(WT)
        x_tok = [place(a, f"x_tok{n}", [P, D_MODEL]) for n in range(2)]
        x_blk = [place(a, f"x_blk{n}", [P, KT, P]) for n in range(2)]
        f_gain = place(a, "f_gain", [P, D_MODEL])
        rows_wide = place(a, "rows_wide", [P, D_MODEL])
        rows_in = place(a, "rows_in", [P, P])
        dec = {}
        a = fresh(ACTV)
        for n in ("pre", "neg", "low", "e_abs", "e_low", "u", "s", "s2", "poly", "soft"):
            dec[n] = place(a, f"dec_{n}", [P, NT, 48])
        r_diag = place(at_tmp, "r_diag", [P, NT, P])
        rest = place(a, "rest", [P, 2, NT, 20])

        PSUM = ctx.enter_context(nc.psum_tensor("PSUM", [P, 4096], F32))

        def bank(n, width=512, at=0):
            return PSUM[:, 512 * n + at:512 * n + at + width]

        def acc(b):
            return PSUM[:, 1536 * b:1536 * b + 1536].rearrange("p (c n) -> p c n", n=512)[:, :, 0:THIRD]

        def thirds(x):
            return x.rearrange("p (c n) -> p c n", n=THIRD)

        ident = cst[:, C_ID]
        ones = cst[:, C_ONE]
        block = ctx.enter_context(nc.Block())
        phase_done = sem("phase_done")

        waits_held = sem("waits_held")

        cst_in = sem("cst_in")
        ssm_s_out = sem("ssm_s_out")
        tok_turned = sem("tok_turned")
        first_c = sem("first_c")
        cond_t = sem("cond_t")
        cond_th = sem("cond_th")
        vec_loaded = sem("vec_loaded")
        vec_t = sem("vec_t")
        coef_e = sem("coef_e")
        mod_used = sem("mod_used")
        mod_row = sem("mod_row")
        mod_col = sem("mod_col")
        n_add = sem("n_add")
        x_in_sb = sem("x_in_sb")
        n_sq = sem("n_sq")
        n_mm = sem("n_mm")
        n_ms = sem("n_ms")
        n_r = sem("n_r")
        n_diag = sem("n_diag")
        n_bc = sem("n_bc")
        n_row = sem("n_row")
        n_t = sem("n_t")
        n_h = sem("n_h")
        dt_loaded = sem("dt_loaded")
        decay_prod = sem("decay_prod")
        decay_term = sem("decay_term")
        decay_exp = sem("decay_exp")
        sp_prod = sem("sp_prod")
        sp_fwd = sem("sp_fwd")
        sp_bwd = sem("sp_bwd")
        sp_e = sem("sp_e")
        sp_yd = sem("sp_yd")
        sp_y = sem("sp_y")
        states_out = sem("states_out")
        y_copied = sem("y_copied")
        y_ss_read = sem("y_ss_read")
        transposed = sem("transposed")
        squared = sem("squared")
        sums_made = sem("sums_made")
        inv_rms = sem("inv_rms")
        scaled = sem("scaled")
        gated = sem("gated")
        hi_made = sem("hi_made")
        lo_made = sem("lo_made")
        out_ready = sem("out_ready")
        tile_stored = sem("tile_stored")
        gp_c = sem("gp_c")
        gp_k = sem("gp_k")
        gp_tt = sem("gp_tt")
        gp_v = sem("gp_v")
        gp_kk = sem("gp_kk")
        o_zero = sem("o_zero")
        a_v = sem("a_v")
        a_split = sem("a_split")
        a_st = sem("a_st")
        a_k = sem("a_k")
        a_q = sem("a_q")
        a_sin = sem("a_sin")
        qk_done = sem("qk_done")
        past_in = sem("past_in")
        kv_out = sem("kv_out")
        q_set = sem("q_set")
        at_s = sem("at_s")
        at_m = sem("at_m")
        at_e = sem("at_e")
        at_v = sem("at_v")
        o_norm = sem("o_norm")
        o_tr = sem("o_tr")
        zb_in = sem("zb_in")
        m_hi = sem("m_hi")
        m_lo = sem("m_lo")
        x_new = sem("x_new")
        f_in = sem("f_in")
        f_sq = sem("f_sq")
        f_ms = sem("f_ms")
        f_r = sem("f_r")
        f_y = sem("f_y")
        tok_in = [sem(f"tok_in{i}") for i in range(2)]
        f_out = [sem(f"f_out{i}") for i in range(2)]
        w_loaded = [sem(f"w_loaded{i}") for i in range(2)]
        w_ready = [sem(f"w_ready{i}") for i in range(2)]
        acc_ready = [sem(f"acc_ready{i}") for i in range(2)]
        acc_free = [sem(f"acc_free{i}") for i in range(2)]
        conv_mid = [sem(f"conv_mid{i}") for i in range(2)]
        th_ready = [sem(f"th_ready{i}") for i in range(2)]
        leave_free = [sem(f"leave_free{i}") for i in range(2)]
        leave_ready = [sem(f"leave_ready{i}") for i in range(2)]
        leave_out = [sem(f"leave_out{i}") for i in range(2)]
        wide_free = [sem(f"wide_free{i}") for i in range(2)]
        wide_in = [sem(f"wide_in{i}") for i in range(2)]
        x_out = [sem(f"x_out{i}") for i in range(2)]
        tile_in = [sem(f"tile_in{i}") for i in range(2)]
        state_in = [sem(f"state_in{i}") for i in range(2)]
        state = [sem(f"state{i}") for i in range(2)]
        ssm_prod = [sem(f"ssm_prod{i}") for i in range(2)]
        ssm_side = [sem(f"ssm_side{i}") for i in range(2)]
        g_pre = [sem(f"g_pre{i}") for i in range(2)]
        g_used = [sem(f"g_used{i}") for i in range(2)]
        g_a = [sem(f"g_a{i}") for i in range(2)]
        g_row = [sem(f"g_row{i}") for i in range(2)]
        g_e = [sem(f"g_e{i}") for i in range(2)]
        g_x = [sem(f"g_x{i}") for i in range(2)]
        g_level = [sem(f"g_level{i}") for i in range(2)]
        g_tm = [sem(f"g_tm{i}") for i in range(2)]
        g_from_s = [sem(f"g_from_s{i}") for i in range(2)]
        g_side = [sem(f"g_side{i}") for i in range(2)]
        g_from_v = [sem(f"g_from_v{i}") for i in range(2)]
        g_v = [sem(f"g_v{i}") for i in range(2)]
        g_vc = [sem(f"g_vc{i}") for i in range(2)]
        g_step = [sem(f"g_step{i}") for i in range(2)]
        at_t = [sem(f"at_t{i}") for i in range(2)]
        at_c = [sem(f"at_c{i}") for i in range(2)]
        mod_in = [sem(f"mod_in{i}") for i in range(3)]
        scan_in = [[sem(f"scan_in{d}{i}") for i in range(2)] for d in range(2)]

        def barrier(e, l, k):
            e.sem_inc(waits_held, 1)
            e.drain().then_inc(phase_done, 1)
            e.wait_ge(phase_done, l * 5 * NPH + 5 * (k + 2))
            e.sem_inc(waits_held, 1)

        def arrive(e, l, k):
            e.sem_inc(waits_held, 1)
            e.drain().then_inc(phase_done, 1)

        def first_barrier(e):
            e.drain().then_inc(phase_done, 1)
            e.wait_ge(phase_done, 5)

        def tiles(e, body):
            with e.Fori(0, NT // 2) as i:
                for p in range(2):
                    body(i * 2 + p, p, i)
            body(NT - 1, 0, NT // 2)

        def overlapped(e, body):
            body(0, 0, 0)
            with e.Fori(0, NT // 2 - 1) as i:
                body(i * 2 + 1, 1, i)
                body(i * 2 + 2, 0, i + 1)
            body(NT - 2, 1, NT // 2 - 1)
            body(NT - 1, 0, NT // 2)

        def next_tile(t, p, i):
            return t + 1, 1 - p, i + p

        def scan_tile(t, d):
            return NS if is_tile(t, NS) else t if d == 0 else (NS - 1) - t

        def states_before(l, t):
            return l * 22 + 11 + (NS + 2 if is_tile(t, NS) else t + 1)

        def is_tile(t, u):
            return isinstance(t, int) and t == u

        def cols(t):
            return slice(t * P, t * P + P) if isinstance(t, int) else bass.ds(t * P, P)

        def one(c):
            return slice(c, c + 1) if isinstance(c, int) else bass.ds(c, 1)

        def nth(l, t, k, of):
            return (l * of + k) * NT + t

        def loaded(l, p, i, k):
            return ((l * 5 + k) * (5 - p) + i + 1) * 16

        def scan_loaded(l, p, count):
            return (l * 3 * (5 - p) + count) * 16

        def split_count(l, m):
            return l * (NG // 2) + m

        def load_group(sp, l, p, m, src):
            sp.wait_ge(w_ready[p], split_count(l, m) + 1)
            sp.dma_start(w_raw[p][:, 0:src.shape[1], 0:src.shape[2]], src).then_inc(w_loaded[p], 16)

        def split_group(dve, l, n, p, m, kt):
            dve.wait_ge(w_loaded[p], 16 * split_count(l, m) + 16)
            dve.wait_ge(acc_ready[1], l * NG + n + 1)
            dve.tensor_copy(w_hi[p][:, 0:kt], w_raw[p][:, 0:kt])
            dve.drain()
            dve.tensor_tensor(w_lo[p][:, 0:kt], w_raw[p][:, 0:kt], w_hi[p][:, 0:kt].bitcast(F32),
                              ALU.subtract).then_inc(w_ready[p], 1)

        def multiply_group(pe, l, n, p, m, kt, x_hi, x_lo):
            pe.wait_ge(w_ready[p], split_count(l, m) + 2)
            for b in range(2):
                pe.wait_ge(acc_free[b], l * NG + n + 1)
                for c in range(3):
                    lo, hi = c * THIRD, (c + 1) * THIRD
                    dst = bank(3 * b + c, THIRD)
                    for k in range(kt):
                        wh = w_hi[p][:, k, b * P:b * P + P]
                        wl = w_lo[p][:, k, b * P:b * P + P]
                        pe.matmul(dst, wh, x_hi[:, k, lo:hi], start=(k == 0), stop=False)
                        pe.matmul(dst, wh, x_lo[:, k, lo:hi], start=False, stop=False)
                        last = pe.matmul(dst, wl, x_hi[:, k, lo:hi], start=False, stop=(k == kt - 1))
                last.then_inc(acc_ready[b], 1)

        def acc_done(l, n, b):
            return l * NG + n + 1 + (2 if b else 0)

        def groups(e, base, count, body):
            with e.Fori(0, count // 2) as i:
                for p in range(2):
                    body(i * 2 + (base + p), p, i + base // 2, i * 2 + p)

        @block.sync
        def _(sp):
            sp.dma_start(cst[:], table.rearrange("p (c n) -> p c n", n=P)).then_inc(cst_in, 16)
            sp.dma_start(rope[:], rope_table.rearrange("p (t a d) -> p t a d", t=NT, a=2)).then_inc(cst_in, 16)
            sp.dma_start(rows_in[0:8], A["c"].rearrange("b (k p) -> (b k) p", p=P)).then_inc(cst_in, 16)
            sp.dma_start(rows_in[8:16], A["c_ctx"].rearrange("(k p) -> k p", p=P)).then_inc(cst_in, 16)
            sp.dma_start(rows_in[16:24], A["final_norm_w"].rearrange("(k p) -> k p", p=P)).then_inc(cst_in, 16)
            xsm = A["x_sample"].rearrange("b t d -> (b t) d")
            for t in range(NT):
                if t >= 2:
                    sp.wait_ge(tok_turned, t - 1)
                src = xsm[t * P:(t + 1) * P] if t < NS else A["x_prompt"].rearrange("b t d -> (b t) d")
                sp.dma_start(x_tok[t % 2][:], src).then_inc(tok_in[t % 2], 16)
            first_barrier(sp)

            with sp.Fori(0, DEPTH) as l:
                for k in range(KT):
                    sp.dma_start(x_sb[:, k], x_d[k]).then_inc(x_in_sb, 16)
                wm = A["w_mod"][l].rearrange("(k p) n -> p k n", p=P)
                for g in range(6):
                    if g >= 3:
                        sp.wait_ge(mod_used, l * 6 + g - 2)
                    sp.dma_start(w_mod[g % 3][:], wm[:, :, g * 2 * GW:(g + 1) * 2 * GW]).then_inc(mod_in[g % 3], 16)
                barrier(sp, l, 0)

                win = A["w_in"][l].rearrange("(k p) n -> p k n", p=P)
                base = G_PROJ
                for kind, pairs, col, _ in PROJ_RUNS:
                    if kind == "kv_small":
                        load_group(sp, l, 0, base // 2, win[:, :, col:col + GW])
                        load_group(sp, l, 1, base // 2, win[:, :, BETA_COL:BETA_COL + 16])
                        sp.dma_start(w_raw[1][:, :, P:P + 32], win[:, :, DT_COL:DT_COL + 32]).then_inc(dt_loaded, 16)
                    else:
                        groups(sp, base, 2 * pairs, lambda n, p, m, j: load_group(
                            sp, l, p, m, win[:, :, bass.ds(j * GW + col, GW)]))
                    base += 2 * pairs
                barrier(sp, l, 1)
                barrier(sp, l, 2)

                def xin_load(t, p):
                    sp.dma_start(xin[p][:], proj_d[B_XBC:B_XBC + 12, :, cols(t)].rearrange("k p t -> p k t")).then_inc(tile_in[p], 16)

                def xt_store(t, p):
                    sp.wait_ge(out_ready, nth(l, t, 0, 2) + 1)
                    sp.dma_start(ssm_tok_d[t], xt[p][:]).then_inc(tile_stored, 16)
                    sp.wait_ge(tile_stored, nth(l, t, 0, 2) * 16 + 16)
                    sp.sem_inc(waits_held, 1)
                xin_load(0, 0)
                xin_load(1, 1)
                with sp.Fori(0, 3) as i:
                    for p in range(2):
                        xt_store(i * 2 + p, p)
                        xin_load(i * 2 + (p + 2), p)
                xt_store(6, 0)
                xin_load(8, 0)
                xt_store(7, 1)
                xt_store(8, 0)
                barrier(sp, l, 3)

                def ssm_loads(i, p):
                    for d in range(2):
                        t = scan_tile(i, d)
                        sp.dma_start(xs[d][p][:], ssm_tok_d[t]).then_inc(scan_in[d][p], 16)
                        sp.dma_start(c_t[d][p][:], proj_d[B_XBC + 10:B_XBC + 12, :, cols(t)].rearrange("k p t -> p k t")).then_inc(scan_in[d][p], 16)
                for d in range(2):
                    sp.dma_start(s_io[d][:], A["state_ssm"][0, l, d].rearrange("(b h) p n -> (h p) b n", h=2)).then_inc(state_in[d], 16)
                ssm_loads(0, 0)
                ssm_loads(1, 1)
                with sp.Fori(0, 3) as i:
                    for p in range(2):
                        for d in range(2):
                            sp.wait_ge(state[d], i * 2 + (l * 22 + p + 2))
                        ssm_loads(i * 2 + (p + 2), p)
                for d in range(2):
                    sp.wait_ge(state[d], l * 22 + 8)
                ssm_loads(NS, 0)
                for d in range(2):
                    sp.wait_ge(ssm_s_out, l * 2 + d + 1)
                    sp.dma_start(O["state_ssm"][0, l, d].rearrange("(b h) p n -> (h p) b n", h=2), s_io[d][:]).then_inc(states_out, 16)
                sp.wait_ge(states_out, l * 64 + 32)
                barrier(sp, l, 4)

                def z_loads(buf, blk, n_blk, k):
                    def load(t, p):
                        sp.dma_start(buf[p][:], proj_d[blk:blk + n_blk, :, cols(t)].rearrange("k p t -> p k t")).then_inc(tile_in[p], 16)
                    load(0, 0)
                    load(1, 1)
                    with sp.Fori(0, 3) as i:
                        for p in range(2):
                            sp.wait_ge(gated, nth(l, i * 2, k, 3) + (p + 1))
                            load(i * 2 + (p + 2), p)
                    sp.wait_ge(gated, nth(l, 7, k, 3))
                    load(8, 0)
                z_loads(z_c, B_ZC, KT, 0)
                barrier(sp, l, 5)

                def branch(base, name, kt, gate):
                    w = A[name][l].rearrange("(k p) n -> p k n", p=P)

                    def body(n, p, m, j):
                        load_group(sp, l, p, m, w[:, :, bass.ds(j * GW, GW)])
                        for b in range(2):
                            sp.wait_ge(wide_free[b], l * 16 + (j + (base - G_SSM + 1)))
                            sp.dma_start(wide[b][:], proj_d[j * 2 + (gate + b)] if gate is not None else x_d[j * 2 + b]).then_inc(wide_in[b], 16)
                    groups(sp, base, 4, body)
                branch(G_SSM, "w_branch_c", 8, B_GATE + 16)
                barrier(sp, l, 6)

                def gin_load(t, p):
                    sp.dma_start(gin[p][:], proj_d[B_GDN:B_GDN + 12, :, cols(t)].rearrange("k p t -> p k t")).then_inc(tile_in[p], 16)

                def g_store(t, p):
                    sp.wait_ge(tile_stored, nth(l, t, 1, 2) * 16)
                    sp.sem_inc(waits_held, 1)
                    sp.wait_ge(gp_kk, l * NT + t + 1)
                    sp.sem_inc(waits_held, 1)
                    sp.wait_ge(out_ready, nth(l, t, 1, 2) + 1)
                    sp.dma_start(gdn_tile_d[t], g_out[p][:]).then_inc(tile_stored, 16)

                def g_next(t, p):
                    sp.wait_ge(transposed, nth(l, t, 2, 5) + 1)
                    sp.sem_inc(waits_held, 1)
                    gin_load(t + 2, p)
                    g_store(t, p)
                gin_load(0, 0)
                gin_load(1, 1)
                with sp.Fori(0, 3) as i:
                    for p in range(2):
                        g_next(i * 2 + p, p)
                g_next(6, 0)
                g_store(7, 1)
                g_store(8, 0)
                sp.wait_ge(tile_stored, nth(l, NT, 1, 2) * 16)
                barrier(sp, l, 7)

                def gdn_loads(i, p):
                    for d in range(2):
                        sp.dma_start(g_t[d][p][:], gdn_tile_d[scan_tile(i, d), :, d:d + 6]).then_inc(scan_in[d][p], 16)
                for d in range(2):
                    sp.dma_start(gd[d]["S"][:], A["state_gdn"][0, l, d].rearrange("h k v -> k h v")).then_inc(state_in[d], 16)
                gdn_loads(0, 0)
                gdn_loads(1, 1)
                with sp.Fori(0, 3) as i:
                    for p in range(2):
                        for d in range(2):
                            sp.wait_ge(g_step[d], i * 2 + (l * NT + p + 1))
                        gdn_loads(i * 2 + (p + 2), p)
                for d in range(2):
                    sp.wait_ge(g_step[d], l * NT + 7)
                gdn_loads(NS, 0)
                for d in range(2):
                    sp.wait_ge(g_step[d], l * NT + 9)
                    sp.dma_start(O["state_gdn"][0, l, d].rearrange("h k v -> k h v"), gd[d]["S"][:]).then_inc(states_out, 16)
                sp.wait_ge(states_out, l * 64 + 64)
                barrier(sp, l, 8)

                z_loads(z_a, B_ZA, 4, 1)
                barrier(sp, l, 9)
                branch(G_GDN, "w_branch_a", 4, B_GATE)
                barrier(sp, l, 10)

                def ain_load(t, p):
                    sp.dma_start(ain[p][:], proj_d[B_ATT:B_ATT + 6, :, cols(t)].rearrange("k p t -> p k t")).then_inc(tile_in[p], 16)
                ain_load(0, 0)
                ain_load(1, 1)
                with sp.Fori(0, 3) as i:
                    for p in range(2):
                        sp.wait_ge(transposed, nth(l, i * 2, 4, 5) + (p + 1))
                        ain_load(i * 2 + (p + 2), p)
                sp.wait_ge(transposed, nth(l, 7, 4, 5))
                ain_load(8, 0)
                sp.wait_ge(transposed, nth(l, 8, 4, 5))
                sp.dma_start(ain[1][:, 0], A["cache_k"][0, l].rearrange("t g d -> t (g d)")).then_inc(past_in, 16)
                sp.dma_start(v_all[:, NT], A["cache_v"][0, l].rearrange("t g d -> t (g d)")).then_inc(past_in, 16)
                sp.wait_ge(qk_done, l * NT + 9)
                sp.dma_start(O["cache_k"][0, l].rearrange("t g d -> t (g d)"), qk[:, AH:10].rearrange("p h d -> p (h d)")).then_inc(kv_out, 16)
                sp.dma_start(O["cache_v"][0, l].rearrange("t g d -> t (g d)"), v_all[:, NS]).then_inc(kv_out, 16)
                sp.wait_ge(kv_out, l * 32 + 32)
                barrier(sp, l, 11)

                def zb_load(t):
                    sp.dma_start(z_b[:], proj_d[B_ZB:B_ZB + 4, :, cols(t)].rearrange("k p t -> p k t")).then_inc(zb_in, 16)
                zb_load(0)
                with sp.Fori(0, NS) as t:
                    sp.wait_ge(lo_made, nth(l, t, 2, 3) + 1)
                    zb_load(t + 1)
                barrier(sp, l, 12)
                branch(G_ATT, "w_branch_b", 4, B_GATE + 8)
                arrive(sp, l, 13)
                branch(G_OUT, "w_out", 8, None)
                barrier(sp, l, 14)

            sp.dma_start(f_gain[:], A["final_norm_w"].partition_broadcast(P)).then_inc(f_in, 16)
            for t in range(NT + 2):
                if t < NT:
                    if t >= 2:
                        sp.wait_ge(tok_turned, NT + t - 1)
                    sp.dma_start(x_blk[t % 2][:], x_d[:, :, cols(t)].rearrange("k p t -> p k t")).then_inc(tok_in[t % 2], 16)
                if t >= 2:
                    sp.wait_ge(f_y, t - 1)
                    u = t - 2
                    dst = O["y_sample"].rearrange("b t d -> (b t) d")[u * P:(u + 1) * P] if u < NS else O["y_prompt"].rearrange("b t d -> (b t) d")
                    sp.dma_start(dst, x_tok[u % 2][:]).then_inc(f_out[u % 2], 16)
            sp.wait_ge(f_out[0], 80)
            sp.wait_ge(f_out[1], 64)

        @block.tensor
        def _(pe):
            pe.sem_inc(acc_ready[1], 2)

            pe.wait_ge(cst_in, 80)
            pe.transpose(bank(7, 24), rows_in[0:24], ident[0:24, 0:24]).then_inc(cond_t, 1)
            for t in range(NT):
                pe.wait_ge(tok_in[t % 2], 16 * (t // 2) + 16)
                if t >= 2:
                    pe.wait_ge(first_c, t - 1)
                for k in range(KT):
                    last = pe.transpose(bank(2 * (t % 2), P, k * P), x_tok[t % 2][:, k * P:(k + 1) * P], ident)
                last.then_inc(tok_turned, 1)
            first_barrier(pe)

            def sums_to_rows(u):
                pe.wait_ge(n_diag, u + 1)
                for t in range(NT):
                    last = pe.matmul(bank(3 + t // 3, P, (t % 3) * P), ones, r_diag[:, t], start=True, stop=True)
                last.then_inc(n_bc, 1)

            with pe.Fori(0, DEPTH) as l:
                def mod_columns(first, count, dst):
                    pe.wait_ge(mod_row, l * 6 + (first + count) // 4)
                    pe.sem_inc(waits_held, 1)
                    for b in range(count):
                        last = pe.transpose(bank(dst, 2, 32 + 2 * b), mod_rows[0:2, (first + b) * P:(first + b + 1) * P], ident[0:2, 0:2])
                    last.then_inc(mod_col, 1)
                for g in range(6):
                    pe.wait_ge(mod_in[g % 3], l * 32 + 16 * (g // 3) + 16)
                    if g >= 2:
                        pe.wait_ge(mod_row, l * 6 + g - 1)
                    for k in range(KT):
                        last = pe.matmul(bank(6 + g % 2)[0:2], cond[:, k:16:8], w_mod[g % 3][:, k],
                                         start=(k == 0), stop=(k == KT - 1))
                    last.then_inc(mod_used, 1)
                    if g == 1:
                        pe.wait_ge(n_add, l * (KT - 1) + KT - 1)
                        for t in range(NT):
                            last = pe.matmul(bank(2, 1, t), tmp[:, t * P:(t + 1) * P], ones[:, 0:1], start=True, stop=True)
                        last.then_inc(n_mm, 1)
                        pe.wait_ge(vec_loaded, l * (22 * 16) + 22 * 16)
                        pe.transpose(bank(0, NV), vec_in[0:NV], ident[0:NV, 0:NV]).then_inc(vec_t, 1)
                    if g == 2:
                        sums_to_rows(l * 2)
                    if g == 3:
                        mod_columns(0, 16, 1)
                mod_columns(16, 8, 2)
                barrier(pe, l, 0)

                base = G_PROJ
                for kind, pairs, col, _ in PROJ_RUNS:
                    groups(pe, base, 2 * pairs, lambda n, p, m, j: multiply_group(pe, l, n, p, m, KT, h_hi, h_lo))
                    base += 2 * pairs
                barrier(pe, l, 1)

                for t in range(NT):
                    pe.transpose(bank(0, 16, t * 48), wide[0][0:16, t * P:(t + 1) * P], ident[0:16, 0:16])
                    last = pe.transpose(bank(0, 32, t * 48 + 16), wide[1][0:32, t * P:(t + 1) * P], ident[0:32, 0:32])
                last.then_inc(decay_prod, 1)
                pe.wait_ge(decay_term, l * 3 + 2)
                for d in range(2):
                    pe.matmul(bank(1 + d, 180), cst[:, C_TRI + d], logd[:, :, d], start=True, stop=True)
                    last = pe.matmul(bank(3 + d, 180), ones, logd[:, :, d], start=True, stop=True)
                last.then_inc(decay_prod, 1)
                barrier(pe, l, 2)

                def y_products(n, late):
                    for half in range(2):
                        pe.wait_ge(sp_fwd, n * 6 + (5 + late + half))
                        pe.wait_ge(sp_bwd, n * 4 + (3 + late + half))
                        for h in range(8 * half, 8 * half + 8):
                            dst = PSUM[:, h * SP_:(h + 1) * SP_]
                            pe.matmul(dst, w_f[:, h], x_dt[0][:, h], start=True, stop=False)
                            last = pe.matmul(dst, w_b[:, h], x_dt[1][:, h], start=False, stop=True)
                    last.then_inc(sp_y, 1)

                def ssm_prep(t, p, i):
                    n = l * NT + t
                    first = isinstance(t, int) and t == 0
                    pe.wait_ge(tile_in[p], loaded(l, p, i, 0))
                    if not first:
                        pe.wait_ge(sp_fwd, n * 6 - 2)
                    if not (isinstance(t, int) and t < 2):
                        pe.wait_ge(sp_yd, n - 1)
                    for k in range(10):
                        pe.transpose(PSUM[:, k * P:(k + 1) * P], xin[p][:, k], ident)
                    for g in range(SG):
                        last = pe.matmul(bank(7, P, g * P), xin[p][:, 8 + g], xin[p][:, 10 + g], start=True, stop=True)
                    last.then_inc(transposed, 1)
                    for half in range(2):
                        if not first:
                            pe.wait_ge(sp_e, n * 2 + (half - 1))
                        pe.wait_ge(sp_fwd, n * 6 + (1 if first else -1) + half)
                        pe.wait_ge(sp_bwd, n * 4 + (1 if first else -1) + half)
                        for h in range(8 * half, 8 * half + 8):
                            dst = PSUM[:, 1536 + h * P:1536 + (h + 1) * P]
                            pe.matmul(dst, after[:, h], cst[:, C_TRI], start=True, stop=False)
                            last = pe.matmul(dst, before[:, h], cst[:, C_TRI + 1], start=False, stop=True)
                        last.then_inc(sp_prod, 1)
                    pe.wait_ge(out_ready, nth(l, t, 0, 2) + 1)
                    if not first:
                        y_products(n - 1, 2)
                ssm_prep(0, 0, 0)
                ssm_prep(1, 1, 0)
                with pe.Fori(0, 3) as i:
                    for p in range(2):
                        ssm_prep(i * 2 + (p + 2), p, i + 1)
                ssm_prep(NT - 1, 0, 4)
                pe.wait_ge(sp_yd, l * NT + NT - 1)
                y_products(l * NT + NT - 1, 0)
                barrier(pe, l, 3)

                for d in range(2):
                    pe.wait_ge(state_in[d], l * 32 + 16)
                    for b in range(8):
                        last = pe.transpose(PSUM[:, d * 2048 + b * P:d * 2048 + (b + 1) * P], s_io[d][:, b], ident)
                    last.then_inc(ssm_prod[d], 1)

                def ssm_step(t, p, i):
                    for d in range(2):
                        before_ = l * 22 + (10 if isinstance(t, int) else t + 1)
                        pe.wait_ge(scan_in[d][p], scan_loaded(l, p, 2 * i + 2))
                        pe.wait_ge(state[d], before_)
                        for g in range(SG):
                            last = pe.matmul(bank(4 * d + g), c_t[d][p][:, g], s_ssm[d][:, g * 512:(g + 1) * 512], start=True, stop=True)
                        last.then_inc(ssm_prod[d], 1)
                        pe.wait_ge(ssm_side[d], (l * NT + t) * 2 + 1)
                        for g in range(SG):
                            last = pe.matmul(bank(4 * d + 2 + g), xs[d][p][:, 1024 + g * P:1024 + (g + 1) * P],
                                             x_in[d][:, 8 * g:8 * g + 8].rearrange("p h q -> p (h q)"), start=True, stop=True)
                        last.then_inc(ssm_prod[d], 1)
                tiles(pe, ssm_step)
                for d in range(2):
                    pe.wait_ge(state[d], l * 22 + 11)
                    for b in range(8):
                        last = pe.transpose(PSUM[:, d * 2048 + b * P:d * 2048 + (b + 1) * P], s_ssm[d][:, b * P:(b + 1) * P], ident)
                    last.then_inc(ssm_prod[d], 1)
                barrier(pe, l, 4)

                def y_turn(t, p, i):
                    pe.wait_ge(y_copied, l * NT + t + 1)
                    for k in range(KT):
                        last = pe.transpose(bank(4 * p, P, k * P), y_st[p][:, k * P:(k + 1) * P], ident)
                    last.then_inc(transposed, 1)

                def ssm_post(t, p, i):
                    n = l * NT + t
                    if not is_tile(t, 0) and not is_tile(t, NT - 1):
                        pe.wait_ge(gated, nth(l, t, 0, 3))
                    if not is_tile(t, NT - 1):
                        y_turn(*next_tile(t, p, i))
                    if not is_tile(t, 0):
                        pe.wait_ge(y_ss_read, n)
                    pe.wait_ge(squared, nth(l, t, 0, 4) + 1)
                    for k in range(KT):
                        last = pe.matmul(bank(2, 1), y_sq[:, k], ones[:, 0:1], start=(k == 0), stop=(k == KT - 1))
                    last.then_inc(sums_made, 1)
                y_turn(0, 0, 0)
                overlapped(pe, ssm_post)
                pe.sem_inc(waits_held, 1)
                sums_to_rows(l * 2 + 1)
                barrier(pe, l, 5)
                groups(pe, G_SSM, 4, lambda n, p, m, j: multiply_group(pe, l, n, p, m, 8, b_hi, b_lo))
                barrier(pe, l, 6)

                def tile_in_turn(t, p, i):
                    pe.wait_ge(tile_in[p], loaded(l, p, i, 2))
                    for k in range(12):
                        last = pe.transpose(PSUM[:, k * P:(k + 1) * P], gin[p][:, k], ident)
                    last.then_inc(transposed, 1)

                def gdn_prep(t, p, i):
                    n = l * NT + t
                    pe.wait_ge(scaled, nth(l, t, 1, 4) + 1)
                    pe.wait_ge(gp_v, n + 1)
                    if not is_tile(t, NT - 1):
                        tile_in_turn(*next_tile(t, p, i))
                    for h in range(GH):
                        pe.transpose(bank(3, P, h * P), q_n[:, h], ident)
                        last = pe.transpose(bank(4, P, h * P), g_out[p][:, K_K, h * P:(h + 1) * P], ident)
                    last.then_inc(gp_tt, 1)
                    if not is_tile(t, 0):
                        pe.wait_ge(out_ready, nth(l, t, 1, 2))
                        pe.wait_ge(gp_kk, n)
                    pe.wait_ge(gp_c, n + 1)
                    for h in range(GH):
                        hh = slice(h * P, (h + 1) * P)
                        pe.matmul(bank(5)[:, hh], g_out[p][:, K_KT, hh], g_out[p][:, K_KT, hh], start=True, stop=True)
                        last = pe.matmul(bank(6)[:, hh], g_out[p][:, K_KT, hh], g_out[p][:, K_QT, hh], start=True, stop=True)
                    last.then_inc(gp_k, 1)
                tile_in_turn(0, 0, 0)
                overlapped(pe, gdn_prep)
                barrier(pe, l, 7)

                def decay_rows(t):
                    for d in range(2):
                        pe.wait_ge(g_pre[d], (l * NT + t) * 3 + 1)
                        for h in range(GH):
                            last = pe.matmul(bank(4 * d + 3, P, h * P), gd[d]["col"][:, h], cst[:, C_TRI + d], start=True, stop=True)
                        last.then_inc(g_row[d], 1)

                def transpose_a(t, p):
                    for d in range(2):
                        pe.wait_ge(g_a[d], (l * NT + t) * 2 + 1)
                        for h in range(GH):
                            last = pe.transpose(bank(4 * d + 3, P, h * P), gd[d]["A"][p][:, h], ident)
                        last.then_inc(g_row[d], 1)

                def gdn_step(t, p, i):
                    n = l * NT + t
                    more = not is_tile(t, NT - 1)
                    for d in range(2):
                        g, b0 = gd[d], 4 * d
                        if not is_tile(t, 0):
                            pe.wait_ge(g_step[d], n)
                        pe.wait_ge(g_pre[d], n * 3 + 3)
                        pe.matmul(bank(b0 + 1), ident, g["X"][p][:].rearrange("p h t -> p (h t)"), start=True, stop=False, skip_group_check=True)
                        pe.matmul(bank(b0 + 2), ident, g["Y"][p][:].rearrange("p h t -> p (h t)"), start=True, stop=False, skip_group_check=True)
                    for lev in range(1, 7):
                        for d in range(2):
                            g, b0 = gd[d], 4 * d
                            if lev > 1:
                                pe.wait_ge(g_x[d], n * 6 + lev - 1)
                            for h in range(GH):
                                last = pe.matmul(bank(b0, P, h * P), g["A"][p][:, h], g["X"][p][:, h], start=True, stop=True)
                            last.then_inc(g_level[d], 1)
                        if lev == 1:
                            for d in range(2):
                                pe.wait_ge(state[d], states_before(l, t))
                                for h in range(GH):
                                    last = pe.matmul(bank(4 * d + 3, P, h * P), g_t[d][p][:, K_KT - d, h * P:(h + 1) * P], gd[d]["S"][:, h], start=True, stop=True)
                                last.then_inc(g_from_s[d], 1)
                        elif lev == 2:
                            for d in range(2):
                                pe.wait_ge(g_used[d], n * 2 + 1)
                                for h in range(GH):
                                    last = pe.matmul(bank(4 * d + 3, P, h * P), g_t[d][p][:, K_QT - d, h * P:(h + 1) * P], gd[d]["S"][:, h], start=True, stop=True)
                                last.then_inc(g_from_s[d], 1)
                        elif lev == 3 and more:
                            for d in range(2):
                                pe.wait_ge(g_used[d], n * 2 + 2)
                            decay_rows(t + 1)
                        elif lev == 5 and more:
                            transpose_a(t + 1, 1 - p)
                        for d in range(2):
                            g, b0 = gd[d], 4 * d
                            pe.wait_ge(g_tm[d], n * 6 + lev)
                            for h in range(GH):
                                if lev < 6:
                                    pe.matmul(bank(b0 + 1, P, h * P), g["Y"][p][:, h], g["T"][:, h], start=False, stop=False, skip_group_check=True)
                                last = pe.matmul(bank(b0 + 2, P, h * P), g["T"][:, h], g["Y"][p][:, h], start=False, stop=(lev == 6 and h == 3), skip_group_check=True)
                            last.then_inc(g_level[d], 1)
                    for d in range(2):
                        g, b0 = gd[d], 4 * d
                        pe.wait_ge(g_x[d], n * 6 + 6)
                        for h in range(GH):
                            last = pe.matmul(bank(b0 + 1, P, h * P), g["Y"][p][:, h], g["R"][:, h], start=True, stop=True)
                        last.then_inc(g_v[d], 1)
                    for d in range(2):
                        g, b0 = gd[d], 4 * d
                        pe.wait_ge(g_side[d], n * 2 + 1)
                        pe.wait_ge(g_vc[d], n + 1)
                        for h in range(GH):
                            last = pe.matmul(bank(b0, P, h * P), g["KD"][:, h], g["V"][:, h], start=True, stop=True)
                        last.then_inc(g_from_v[d], 1)
                    for d in range(2):
                        g, b0 = gd[d], 4 * d
                        pe.wait_ge(g_a[d], n * 2 + 2)
                        for h in range(GH):
                            last = pe.matmul(bank(b0 + 2, P, h * P), g["Q"][p][:, h], g["V"][:, h], start=True, stop=True)
                        last.then_inc(g_from_v[d], 1)
                decay_rows(0)
                transpose_a(0, 0)
                overlapped(pe, gdn_step)
                barrier(pe, l, 8)

                def gdn_post(t, p, i):
                    n = l * NT + t
                    pe.wait_ge(scaled, nth(l, t, 2, 4) + 1)
                    for h in range(GH):
                        last = pe.transpose(bank(p, P, h * P), o_st[p][:, h], ident)
                    last.then_inc(transposed, 1)
                tiles(pe, gdn_post)
                barrier(pe, l, 9)
                groups(pe, G_GDN, 4, lambda n, p, m, j: multiply_group(pe, l, n, p, m, 4, b_hi, b_lo))
                barrier(pe, l, 10)

                def stack(n, q):
                    if q is None or not is_tile(q[1], 0):
                        pe.wait_ge(a_k, n)
                    pe.wait_ge(a_split, n + 1)
                    if q is not None:
                        if not is_tile(q[1], 0):
                            pe.wait_ge(a_q, q[0])
                        for h in range(AH):
                            pe.transpose(bank(2, P, h * P), q_hl[:, h].bitcast(F32), ident)
                    for g in range(KVH):
                        pe.transpose(bank(4, P, g * P), k_hh[:, g].bitcast(F32), ident)
                        last = pe.transpose(bank(4, P, 256 + g * P), k_ll[:, g].bitcast(F32), ident)
                    last.then_inc(a_st, 1)

                def ain_turn(t, p, i):
                    pe.wait_ge(tile_in[p], loaded(l, p, i, 4))
                    for k in range(6):
                        last = pe.transpose(PSUM[:, k * P:(k + 1) * P], ain[p][:, k], ident)
                    last.then_inc(transposed, 1)

                def attn_prep(t, p, i):
                    if not is_tile(t, NT - 1):
                        pe.wait_ge(scaled, nth(l, t, 3, 4) + 1)
                        ain_turn(*next_tile(t, p, i))
                    stack(l * (NT + 1) + t, (l * NT + t, t))
                ain_turn(0, 0, 0)
                overlapped(pe, attn_prep)
                stack(l * (NT + 1) + NT, None)
                barrier(pe, l, 11)

                def scores(t, u, h):
                    g, s = h // 4, h % 2
                    if h == 0:
                        pe.wait_ge(q_set, l * NT + t + 1)
                    sample = not (isinstance(t, int) and t == NS)
                    spans = ((0, 512, 0), (512, 512, 512), (NT * P, P, 1024)) if sample else ((SAMPLE, P, 0),)
                    for col, width, at in spans:
                        dst = PSUM[:, 1536 * s + at:1536 * s + at + width]
                        pe.matmul(dst, q_now[u][:, h], k_hi[:, g, col:col + width], start=True, stop=False)
                        last = pe.matmul(dst, q_now[u][:, h], k_lo[:, g, col:col + width], start=False, stop=True)
                    last.then_inc(at_s, 1)

                def values(t, h, key_tiles):
                    n, g, s = l * NT + t, h // 4, h % 2
                    pe.wait_ge(at_c[0], n * AH + h + 1)
                    if len(key_tiles) > 4:
                        pe.wait_ge(at_c[1], (l * NS + t) * AH + h + 1)
                    for j, kt in enumerate(key_tiles):
                        last = pe.matmul(bank(7, AD, h * AD), prob_t[s][:, j], v_all[:, kt, g * AD:(g + 1) * AD],
                                         start=(j == 0), stop=(j == len(key_tiles) - 1))
                    last.then_inc(at_v, 1)

                def attn(t, u, key_tiles, first=False):
                    n, nk = l * NT + t, len(key_tiles)
                    for h in range(AH):
                        s = h % 2
                        if nk > 4 and h:
                            pe.wait_ge(at_c[1], (l * NS + t) * AH + h)
                        if h + 1 < AH:
                            scores(t, u, h + 1)
                        elif nk > 4:
                            scores(t + 1, 1 - u, 0)
                        pe.wait_ge(at_e, n * AH + h + 1)
                        if h:
                            pe.wait_ge(at_c[0], n * AH + h)
                        elif not first:
                            pe.wait_ge(gated, nth(l, t, 2, 3))
                        for j in range(nk):
                            dst = bank(6, P, j * P) if j < 4 else PSUM[:, 1536 * s + j * P:1536 * s + (j + 1) * P]
                            last = pe.transpose(dst, prob[s][:, j * P:(j + 1) * P], ident)
                            if j == min(3, nk - 1):
                                last.then_inc(at_t[0], 1)
                        if nk > 4:
                            last.then_inc(at_t[1], 1)
                        if h:
                            values(t, h - 1, key_tiles)
                    values(t, AH - 1, key_tiles)
                    pe.wait_ge(o_norm, n + 1)
                    for k in range(4):
                        last = pe.transpose(bank(6, P, k * P), o_att[:, 2 * k:2 * k + 2].rearrange("p h d -> p (h d)"), ident)
                    last.then_inc(o_tr, 1)
                sample_keys = [0, 1, 2, 3, 4, 5, 6, 7, NT]
                scores(0, 0, 0)
                attn(0, 0, sample_keys, first=True)
                attn(1, 1, sample_keys)
                with pe.Fori(0, 2) as i:
                    for u in range(2):
                        attn(i * 2 + (u + 2), u, sample_keys)
                attn(6, 0, sample_keys)
                attn(7, 1, sample_keys)
                attn(NS, 0, [NS])
                barrier(pe, l, 12)
                groups(pe, G_ATT, 4, lambda n, p, m, j: multiply_group(pe, l, n, p, m, 4, b_hi, b_lo))
                barrier(pe, l, 13)

                pe.wait_ge(m_lo, l * KT + KT)
                pe.sem_inc(waits_held, 1)
                groups(pe, G_OUT, 4, lambda n, p, m, j: multiply_group(pe, l, n, p, m, 8, b_hi, b_lo))
                barrier(pe, l, 14)

            for t in range(NT):
                pe.wait_ge(tok_in[t % 2], 16 * ((5 - t % 2) + t // 2 + 1))
                if t >= 2:
                    pe.wait_ge(f_y, t - 1)
                for k in range(KT):
                    last = pe.transpose(bank(2 * (t % 2), P, k * P), x_blk[t % 2][:, k], ident)
                last.then_inc(tok_turned, 1)

        @block.scalar
        def _(act):
            act.wait_ge(cond_t, 1)
            act.activation(stat[:, 0:24], bank(7, 24), ACT.Tanh, scale=0.5).then_inc(cond_th, 1)
            for t in range(NT):
                act.wait_ge(tok_turned, t + 1)
                if t >= 2:
                    act.wait_ge(x_out[t % 2], 16 * (t // 2))
                act.activation(x_blk[t % 2][:], PSUM[:, 1024 * (t % 2):1024 * (t % 2) + 1024].rearrange("p (k t) -> p k t", t=P), ACT.Copy).then_inc(first_c, 1)
            first_barrier(act)

            with act.Fori(0, DEPTH) as l:
                for at, name in ((V_NORM, "norm_w"), (V_BMOD, "b_mod"), (V_SBIAS, "ssm_conv_b"),
                                 (V_SNORM, "ssm_norm_w"), (V_GNORM, "gdn_norm_w")):
                    src = A[name][l].rearrange("(k p) -> k p", p=P)
                    act.dma_start(vec_in[at:at + src.shape[0]], src).then_inc(vec_loaded, 16)
                for at, name in ((V_GCONV, "gdn_conv_w"), (V_SCONV, "ssm_conv_w")):
                    act.dma_start(vec_in[at:at + 36], A[name][l].rearrange("w (k p) -> (w k) p", p=P)).then_inc(vec_loaded, 16)
                for at, name in ((0, "gdn_a_log"), (8, "ssm_a_log"), (40, "gdn_dt_bias"), (48, "ssm_dt_bias")):
                    src = A[name][l].rearrange("d h -> (d h)")
                    act.dma_start(rows[:, at:at + src.shape[0]], src.partition_broadcast(P)).then_inc(vec_loaded, 16)
                act.dma_start(rows[:, 80:96], A["ssm_d"][l].partition_broadcast(P)).then_inc(vec_loaded, 16)
                for at, name, heads in ((0, "attn_q_norm", AH), (AH, "attn_k_norm", KVH)):
                    for h in range(heads):
                        act.dma_start(qk_gain[:, at + h], A[name][l].partition_broadcast(P)).then_inc(vec_loaded, 16)
                act.wait_ge(x_in_sb, l * 128 + 128)
                for k in range(KT):
                    if k >= 3:
                        act.wait_ge(n_add, l * (KT - 1) + k - 2)
                    act.activation(wide[k % 2][:] if k else tmp[:], x_sb[:, k], ACT.Square).then_inc(n_sq, 1)
                def mod_out(g):
                    act.wait_ge(mod_used, l * 6 + g + 1)
                    act.activation(mod_rows[0:2, g * 512:(g + 1) * 512], bank(6 + g % 2)[0:2], ACT.Copy).then_inc(mod_row, 1)
                for g in range(3):
                    mod_out(g)

                def rows_out(u):
                    act.wait_ge(n_bc, u + 1)
                    act.activation(thirds(row_bc[:]), acc(1), ACT.Copy).then_inc(n_row, 1)
                rows_out(l * 2)
                mod_out(3)
                for k in range(KT):
                    if k in (2, 4):
                        mod_out(3 + k // 2)
                    act.wait_ge(n_t, l * KT + k + 1)
                    for c, (lo, hi) in enumerate(((0, SAMPLE), (SAMPLE, T))):
                        last = act.activation(h_hi[:, k, lo:hi], wide[k % 2][:, lo:hi], ACT.Identity, bias=mod[:, k, c:c + 1])
                    last.then_inc(n_h, 1)
                act.wait_ge(vec_loaded, l * (22 * 16) + 22 * 16)
                act.activation(coef[:, :, 0:4], rows[:, 0:8].rearrange("p (d h) -> p d h", d=2), ACT.Exp)
                act.activation(coef[:, :, 4:20], rows[:, 8:40].rearrange("p (d h) -> p d h", d=2), ACT.Exp).then_inc(coef_e, 1)
                barrier(act, l, 0)

                base, stored, conv, th = G_PROJ, 0, 0, 0
                for kind, pairs, col, _ in PROJ_RUNS:
                    def body(n, p, m, j, kind=kind, st=stored, cv=conv, tq=th):
                        for b in range(2):
                            act.wait_ge(acc_ready[b], acc_done(l, n, b))
                            if kind.startswith("conv"):
                                act.activation(thirds(conv_in[b][:, 1:1 + 2 * THIRD]), acc(b)[:, 0:2], ACT.Copy)
                                act.activation(conv_in[b][:, 1 + 2 * THIRD:1 + SAMPLE], acc(b)[:, 2, 0:THIRD - PROMPT], ACT.Copy)
                                act.activation(conv_in[b][:, SAMPLE + 2:T + 2], acc(b)[:, 2, THIRD - PROMPT:THIRD], ACT.Copy).then_inc(acc_free[b], 1)
                                act.wait_ge(conv_mid[b], l * 12 + j + (cv + 1))
                                act.wait_ge(leave_free[b], l * 35 + j + (st + 1))
                                act.activation(leave[b][:, 0:T + 1], conv_out[b][:, 0:T + 1], ACT.Tanh).then_inc(th_ready[b], 1)
                            elif kind == "kv_small" and j == 1:
                                act.activation(thirds(wide[b][0:32]), acc(b)[0:32], ACT.Copy).then_inc(acc_free[b], 1)
                            else:
                                act.wait_ge(leave_free[b], l * 35 + j + (st + 1))
                                if kind == "silu":
                                    act.activation(thirds(leave[b][:, 0:T]), acc(b), ACT.Tanh, scale=0.5).then_inc(th_ready[b], 1)
                                else:
                                    f, sc = (ACT.Tanh, 0.5) if kind == "tanh" else (ACT.Copy, 1.0)
                                    act.activation(thirds(leave[b][:, 0:T]), acc(b), f, scale=sc).then_inc(leave_ready[b], 1)
                                    act.drain().then_inc(acc_free[b], 1)
                    if kind == "kv_small":
                        body(base, 0, base // 2, 0)
                        body(base + 1, 1, base // 2, 1)
                    else:
                        groups(act, base, 2 * pairs, body)
                    stored += 1 if kind == "kv_small" else 2 * pairs
                    conv += 2 * pairs if kind.startswith("conv") else 0
                    th += 2 * pairs if kind.startswith("conv") or kind == "silu" else 0
                    base += 2 * pairs
                barrier(act, l, 1)

                act.wait_ge(decay_term, l * 3 + 1)
                act.activation(dec["e_abs"][:], dec["neg"][:], ACT.Exp)
                act.activation(dec["e_low"][:], dec["low"][:], ACT.Exp).then_inc(decay_exp, 1)
                act.wait_ge(decay_term, l * 3 + 3)
                act.activation(e_cum[:], cum[:], ACT.Exp)
                act.activation(e_tot[:], tot[:], ACT.Exp)
                act.activation(e_rest[:], rest[:], ACT.Exp).then_inc(decay_exp, 1)
                barrier(act, l, 2)

                def ssm_prep(t, p, i):
                    n = l * NT + t
                    act.wait_ge(transposed, nth(l, t, 0, 5) + 1)
                    if not (isinstance(t, int) and t < 2):
                        act.wait_ge(tile_stored, nth(l, t, 0, 2) * 16 - 16)
                    act.activation(xt[p][:], PSUM[:, 0:1280], ACT.Copy).then_inc(out_ready, 1)
                    for half in range(2):
                        if not (isinstance(t, int) and t == 0):
                            act.wait_ge(sp_fwd, n * 6 + (1 + half))
                            act.wait_ge(sp_bwd, n * 4 + (1 + half))
                        act.wait_ge(sp_prod, n * 2 + 1 + half)
                        hs = slice(8 * half, 8 * half + 8)
                        act.activation(e_ssm[:, hs], PSUM[:, 1536 + 1024 * half:2560 + 1024 * half].rearrange("p (h l) -> p h l", l=P), ACT.Exp).then_inc(sp_e, 1)
                ssm_prep(0, 0, 0)
                ssm_prep(1, 1, 0)
                with act.Fori(0, 3) as i:
                    for p in range(2):
                        ssm_prep(i * 2 + (p + 2), p, i + 1)
                ssm_prep(NT - 1, 0, 4)
                barrier(act, l, 3)

                for d in range(2):
                    act.wait_ge(ssm_prod[d], l * 20 + 1)
                    act.activation(s_ssm[d][:], PSUM[:, d * 2048:d * 2048 + 1024], ACT.Copy).then_inc(state[d], 1)
                for d in range(2):
                    act.wait_ge(ssm_prod[d], l * 20 + 20)
                    act.activation(s_io[d][:], PSUM[:, d * 2048:d * 2048 + 1024].rearrange("p (b n) -> p b n", n=P), ACT.Copy).then_inc(ssm_s_out, 1)
                barrier(act, l, 4)

                def y_copy(t, p, i):
                    act.activation(y_st[p][:], y_acc[:, t], ACT.Copy).then_inc(y_copied, 1)

                def ssm_post(t, p, i):
                    act.wait_ge(gated, nth(l, t, 0, 3) + 1)
                    if not is_tile(t, 0):
                        act.wait_ge(sums_made, nth(l, t, 0, 4))
                    act.activation(y_sq[:], yz[p][:], ACT.Square).then_inc(squared, 1)
                    if not is_tile(t, NT - 2) and not is_tile(t, NT - 1):
                        act.activation(y_st[p][:], y_acc[:, t + 2], ACT.Copy).then_inc(y_copied, 1)
                    act.wait_ge(scaled, nth(l, t, 0, 4) + 1)
                    act.activation(b_hi[:, :, cols(t)], yzw[p][:], ACT.Copy).then_inc(hi_made, 1)
                y_copy(0, 0, 0)
                y_copy(1, 1, 0)
                overlapped(act, ssm_post)
                rows_out(l * 2 + 1)
                barrier(act, l, 5)
                barrier(act, l, 6)

                def square_next(t):
                    act.wait_ge(transposed, nth(l, t, 2, 5) + 1)
                    act.activation(g_sq[:], PSUM[:, 0:1024].rearrange("p (h d) -> p h d", d=GD), ACT.Square).then_inc(squared, 1)

                def values_out(t, p, i):
                    act.wait_ge(tile_stored, nth(l, t, 1, 2) * 16 - 16)
                    act.activation(g_out[p][:, K_V], bank(2), ACT.Copy).then_inc(gp_v, 1)

                def gdn_prep(t, p, i):
                    n = l * NT + t
                    if not is_tile(t, NT - 1):
                        square_next(t + 1)
                    act.wait_ge(gp_tt, n + 1)
                    act.activation(g_out[p][:, K_QT], bank(3), ACT.Copy)
                    act.activation(g_out[p][:, K_KT], bank(4), ACT.Copy).then_inc(gp_c, 1)
                    act.wait_ge(gp_k, n + 1)
                    act.activation(g_out[p][:, K_KQ], bank(6), ACT.Copy).then_inc(out_ready, 1)
                    if not is_tile(t, NT - 1):
                        values_out(*next_tile(t, p, i))
                square_next(0)
                values_out(0, 0, 0)
                overlapped(act, gdn_prep)
                barrier(act, l, 7)

                def flat(x):
                    return x[:].rearrange("p h t -> p (h t)")

                def decays_exp(t):
                    for d in range(2):
                        act.wait_ge(g_pre[d], (l * NT + t) * 3 + 2)
                        act.activation(gd[d]["E"][:], gd[d]["E"][:], ACT.Exp).then_inc(g_e[d], 1)

                def gdn_step(t, p, i):
                    n = l * NT + t
                    for lev in range(1, 7):
                        for d in range(2):
                            act.wait_ge(g_level[d], n * 12 + 2 * lev)
                            if lev < 6:
                                act.activation(flat(gd[d]["X"][p]), bank(4 * d + 1), ACT.Copy)
                            act.activation(flat(gd[d]["Y"][p]), bank(4 * d + 2), ACT.Copy).then_inc(g_x[d], 1)
                        if lev == 3 and not is_tile(t, NT - 1):
                            decays_exp(t + 1)
                decays_exp(0)
                overlapped(act, gdn_step)
                barrier(act, l, 8)

                def square_o(t):
                    act.activation(o_sq[:], o_acc[:, t].rearrange("p (h d) -> p h d", d=GD), ACT.Square).then_inc(squared, 1)

                def gdn_post(t, p, i):
                    if not is_tile(t, NT - 1):
                        act.wait_ge(sums_made, nth(l, t, 2, 4) + 1)
                        square_o(t + 1)
                    act.wait_ge(gated, nth(l, t, 1, 3) + 1)
                    act.activation(b_hi[:, 0:4, cols(t)], o_z[:], ACT.Copy).then_inc(hi_made, 1)
                square_o(0)
                overlapped(act, gdn_post)
                barrier(act, l, 9)
                barrier(act, l, 10)

                def square_head(t, p, i):
                    act.wait_ge(transposed, nth(l, t, 4, 5) + 1)
                    act.activation(a_sq[:], PSUM[:, 0:640].rearrange("p (h d) -> p h d", d=AD), ACT.Square).then_inc(squared, 1)
                    act.activation(v_all[:, t], PSUM[:, 640:768], ACT.Copy).then_inc(a_v, 1)

                def attn_prep(t, p, i):
                    if not is_tile(t, NT - 1):
                        square_head(*next_tile(t, p, i))
                    act.wait_ge(a_st, l * (NT + 1) + t + 1)
                    act.activation(q_stack[:, t], PSUM[:, 1024:2048].rearrange("p (h t) -> p h t", t=P), ACT.Copy).then_inc(a_q, 1)
                square_head(0, 0, 0)
                overlapped(act, attn_prep)
                barrier(act, l, 11)

                def attn(t, u, nk):
                    n, ns = l * NT + t, l * NS + t
                    width = nk * P
                    for h in range(AH):
                        s = h % 2
                        if nk == 1 and h:
                            act.wait_ge(at_t[0], n * AH + h)
                        act.wait_ge(at_m, n * AH + h + 1)
                        act.activation(prob[s][:, 0:width], PSUM[:, 1536 * s:1536 * s + width], ACT.Exp, bias=row_max[:, u, h:h + 1],
                                       accum_out=row_sum[:, u, h:h + 1]).then_inc(at_e, 1)
                        if nk > 1:
                            act.wait_ge(at_t[1], ns * AH + h + 1)
                            act.activation(prob_t[s][:, 4:9], PSUM[:, 1536 * s + 512:1536 * s + T].rearrange("p (j t) -> p j t", t=P), ACT.Copy).then_inc(at_c[1], 1)
                    act.wait_ge(gated, nth(l, t, 2, 3) + 1)
                    act.activation(b_hi[:, 0:4, cols(t)], o_bz[:], ACT.Copy).then_inc(hi_made, 1)
                with act.Fori(0, NS // 2) as i:
                    for u in range(2):
                        attn(i * 2 + u, u, 9)
                attn(NS, 0, 1)
                barrier(act, l, 12)
                barrier(act, l, 13)

                for k in range(KT):
                    act.activation(b_hi[:, k], merged[:, k], ACT.Copy).then_inc(m_hi, 1)
                barrier(act, l, 14)

            for t in range(NT):
                act.wait_ge(tok_turned, NT + t + 1)
                if t >= 2:
                    act.wait_ge(f_y, t - 1)
                if t:
                    act.wait_ge(f_sq, t)
                act.activation(rows_wide[:], PSUM[:, 1024 * (t % 2):1024 * (t % 2) + 1024], ACT.Square,
                               accum_out=stat[:, 16 + t:17 + t]).then_inc(f_sq, 1)

        @block.gpsimd
        def _(pool):
            for b in range(2):
                pool.sem_inc(leave_free[b], 1)
                pool.sem_inc(wide_free[b], 1)
            pool.memset(minus_half[:], -0.5)
            for t in range(NT):
                pool.wait_ge(first_c, t + 1)
                pool.sem_inc(waits_held, 1)
                pool.dma_start(x_d[:, :, cols(t)].rearrange("k p t -> p k t"), x_blk[t % 2][:]).then_inc(x_out[t % 2], 16)
            pool.wait_ge(x_out[0], 80)
            pool.wait_ge(x_out[1], 64)
            first_barrier(pool)

            with pool.Fori(0, DEPTH) as l:
                pool.wait_ge(n_ms, l * 2 + 1)
                pool.tensor_tensor(r_tok[:], stat[:, 0:NT], minus_half[:, 0:NT], ALU.pow).then_inc(n_r, 1)
                barrier(pool, l, 0)

                base, stored = G_PROJ, 0
                for kind, pairs, col, blk in PROJ_RUNS:
                    at = SAMPLE + 1 if kind.startswith("conv") else SAMPLE

                    def body(n, p, m, j, at=at, blk=blk, st=stored):
                        for b in range(2):
                            pool.wait_ge(leave_ready[b], l * 35 + j + (st + 1))
                            pool.sem_inc(waits_held, 1)
                            pool.dma_start(proj_d[j * 2 + (blk + b), :, 0:SAMPLE], leave[b][:, 0:SAMPLE]).then_inc(leave_out[b], 16)
                            pool.dma_start(proj_d[j * 2 + (blk + b), :, SAMPLE:T], leave[b][:, at:at + PROMPT]).then_inc(leave_out[b], 16)
                            pool.wait_ge(leave_out[b], (l * 35 + j + (st + 1)) * 32)
                            pool.sem_inc(leave_free[b], 1)
                    if kind == "kv_small":
                        body(base, 0, base // 2, 0)
                    else:
                        groups(pool, base, 2 * pairs, body)
                    stored += 1 if kind == "kv_small" else 2 * pairs
                    base += 2 * pairs
                barrier(pool, l, 1)
                barrier(pool, l, 2)

                def build_before(t):
                    for half in range(2):
                        hs = slice(8 * half, 8 * half + 8)
                        pool.tensor_tensor(before[:, hs], again(cst[:, C_STRICT + 1], 8), over(logd[:, t, 1, 4 + 8 * half:12 + 8 * half], P), ALU.mult).then_inc(sp_bwd, 1)

                def ssm_prep(t, p, i):
                    n = l * NT + t
                    last_tile = isinstance(t, int) and t == NT - 1
                    if not last_tile:
                        pool.wait_ge(sp_prod, n * 2 + 2)
                        build_before(t + 1)
                    pool.wait_ge(out_ready, nth(l, t, 0, 2) + 1)
                    if not (isinstance(t, int) and t == 0):
                        pool.wait_ge(sp_y, n)
                    xh = xt[p][:, 0:D_MODEL].rearrange("p (h q) -> p h q", q=SP_)
                    pool.tensor_tensor(x_dt[1][:], xh, over(dt_[:, t, 1], SP_), ALU.mult)
                    for g in range(SG):
                        pool.wait_ge(sp_e, n * 2 + 1 + g)
                        pool.wait_ge(sp_fwd, n * 6 + 4)
                        pool.tensor_tensor(w_b[:, 8 * g:8 * g + 8], e_ssm[:, 8 * g:8 * g + 8], again(cb[p][:, 1, g], 8), ALU.mult).then_inc(sp_bwd, 1)
                build_before(0)
                ssm_prep(0, 0, 0)
                ssm_prep(1, 1, 0)
                with pool.Fori(0, 3) as i:
                    for p in range(2):
                        ssm_prep(i * 2 + (p + 2), p, i + 1)
                ssm_prep(NT - 1, 0, 4)
                barrier(pool, l, 3)

                def ssm_step(t, p, i):
                    for d in range(2):
                        tt = t if isinstance(t, int) or d == 0 else (NS - 1) - t
                        pool.wait_ge(scan_in[d][p], scan_loaded(l, p, 2 * i + 2))
                        pool.sem_inc(waits_held, 1)
                        pool.wait_ge(state[d], l * 22 + (10 if isinstance(t, int) else t + 1))
                        pool.sem_inc(waits_held, 1)
                        pool.tensor_tensor(x_in[d][:], xs[d][p][:, 0:D_MODEL].rearrange("p (h q) -> p h q", q=SP_), over(dt_rest[:, d, tt], SP_), ALU.mult).then_inc(ssm_side[d], 1)
                        pool.tensor_tensor(s_kept[d][:].rearrange("p (h q) -> p h q", q=SP_), s_ssm[d][:].rearrange("p (h q) -> p h q", q=SP_), over(e_tot[:, d, tt, 4:20], SP_), ALU.mult).then_inc(ssm_side[d], 1)
                tiles(pool, ssm_step)
                barrier(pool, l, 4)

                def ssm_post(t, p, i):
                    pool.wait_ge(gated, nth(l, t, 0, 3) + 1)
                    if not is_tile(t, 0):
                        pool.wait_ge(lo_made, nth(l, t, 0, 3))
                    pool.tensor_tensor(yzw[p][:], yz[p][:], over(vec[:, V_SNORM:V_SNORM + 8], P), ALU.mult).then_inc(scaled, 1)
                overlapped(pool, ssm_post)
                pool.wait_ge(n_ms, l * 2 + 2)
                pool.tensor_tensor(r_tok[:], stat[:, 0:NT], minus_half[:, 0:NT], ALU.pow).then_inc(n_r, 1)
                barrier(pool, l, 5)
                barrier(pool, l, 6)

                def gdn_prep(t, p, i):
                    pool.wait_ge(sums_made, nth(l, t, 1, 4) + 1)
                    pool.tensor_tensor(stat[:, 8:16], stat[:, 0:8], minus_half[:, 0:8], ALU.pow).then_inc(inv_rms, 1)
                tiles(pool, gdn_prep)
                barrier(pool, l, 7)

                pool.memset(o_acc[:], 0.0).then_inc(o_zero, 1)

                def kinds(d, p, c):
                    return g_t[d][p][:, c - d].rearrange("p (h t) -> p h t", t=P)

                def decayed(t, p, i):
                    for d in range(2):
                        pool.wait_ge(scan_in[d][p], scan_loaded(l, p, 2 * (5 - p) + i + 1))
                        pool.sem_inc(waits_held, 1)
                        pool.wait_ge(g_e[d], l * NT + t + 1)
                        pool.tensor_tensor(gd[d]["A"][p][:], kinds(d, p, K_KK[d]), gd[d]["E"][:], ALU.mult).then_inc(g_a[d], 1)
                    for d in range(2):
                        pool.drain()
                        pool.tensor_tensor(gd[d]["Q0"][:], kinds(d, p, K_KQ), gd[d]["E"][:], ALU.mult)
                        pool.drain()
                        pool.tensor_tensor(gd[d]["Q"][p][:], gd[d]["Q0"][:], again(cst[:, C_TRI + d], GH), ALU.mult).then_inc(g_a[d], 1)

                def gdn_step(t, p, i):
                    for d in range(2):
                        tt, g = scan_tile(t, d), gd[d]
                        pool.wait_ge(state[d], states_before(l, t))
                        pool.sem_inc(waits_held, 1)
                        pool.tensor_tensor(g["KD"][:], kinds(d, p, K_K), over(e_rest[:, d, tt, 0:4], P), ALU.mult).then_inc(g_side[d], 1)
                        pool.tensor_tensor(g["SK"][:], g["S"][:], over(e_tot[:, d, tt, 0:4], P), ALU.mult).then_inc(g_side[d], 1)
                        if not is_tile(t, 0):
                            pool.wait_ge(g_step[d], l * NT + t)
                            pool.sem_inc(waits_held, 1)
                    if not is_tile(t, NT - 1):
                        decayed(*next_tile(t, p, i))
                decayed(0, 0, 0)
                overlapped(pool, gdn_step)
                barrier(pool, l, 8)

                def gdn_post(t, p, i):
                    pool.wait_ge(sums_made, nth(l, t, 2, 4) + 1)
                    pool.tensor_tensor(stat[:, 8:12], stat[:, 0:4], minus_half[:, 0:4], ALU.pow).then_inc(inv_rms, 1)
                tiles(pool, gdn_post)
                barrier(pool, l, 9)
                barrier(pool, l, 10)

                def inverse_rms(t):
                    pool.wait_ge(sums_made, nth(l, t, 3, 4) + 1)
                    pool.tensor_tensor(stat[:, 16:26], stat[:, 0:10], minus_half[:, 0:10], ALU.pow).then_inc(inv_rms, 1)

                def attn_prep(t, p, i):
                    pool.wait_ge(scaled, nth(l, t, 3, 4) + 1)
                    qk5 = qk[:].rearrange("p h (a s f) -> p h a s f", a=2, s=2)
                    t5 = qk_s[:].rearrange("p h (a s f) -> p h a s f", a=2, s=2)
                    for s in range(2):
                        sin = rope[:, t, 1].rearrange("p (a s f) -> p a s f", a=2, s=2)[:, :, s]
                        last = pool.tensor_tensor(t5[:, :, :, s], qk5[:, :, :, 1 - s], sin.unsqueeze(1).broadcast_to([P, 10, 2, 16]), ALU.mult)
                    last.then_inc(a_sin, 1)
                    if not is_tile(t, NT - 1):
                        inverse_rms(t + 1)
                inverse_rms(0)
                overlapped(pool, attn_prep)
                barrier(pool, l, 11)

                def set_queries(t, u, wait=True):
                    if wait:
                        pool.wait_ge(at_s, (l * NT + t - 1) * AH)
                        pool.sem_inc(waits_held, 1)
                    pool.tensor_copy(q_now[u][:], q_stack[:, t]).then_inc(q_set, 1)
                set_queries(0, 0, False)
                set_queries(1, 1, False)
                with pool.Fori(0, 3) as i:
                    for u in range(2):
                        set_queries(i * 2 + (u + 2), u)
                set_queries(NS, 0)
                barrier(pool, l, 12)
                barrier(pool, l, 13)

                for blk in range(KT):
                    b = blk % 2
                    pool.wait_ge(x_new, l * KT + blk + 1)
                    pool.sem_inc(waits_held, 1)
                    pool.dma_start(x_d[blk], wide[b][:]).then_inc(x_out[b], 16)
                    pool.wait_ge(x_out[b], 16 * (5 - b) + l * 64 + 16 * (blk // 2) + 16)
                    pool.sem_inc(wide_free[b], 1)
                barrier(pool, l, 14)

            for t in range(NT):
                pool.wait_ge(f_ms, t + 1)
                pool.tensor_tensor(r_tok[:, t:t + 1], stat[:, 25:26], minus_half[:, 0:1], ALU.pow).then_inc(f_r, 1)

        @block.vector
        def _(dve):
            for b in range(2):
                dve.sem_inc(w_ready[b], 1)
                dve.sem_inc(acc_free[b], 1)
            dve.wait_ge(cond_th, 1)
            dve.scalar_tensor_tensor(cond[:], stat[:, 0:24], 1.0, bank(7, 24), ALU.add, ALU.mult)
            dve.drain()
            dve.tensor_scalar(cond[:], cond[:], 0.5, None, ALU.mult)
            first_barrier(dve)

            def diagonals(u):
                dve.wait_ge(n_r, u + 1)
                for t in range(NT):
                    last = dve.tensor_scalar(r_diag[:, t], ident, r_tok[:, t:t + 1], None, ALU.mult)
                last.then_inc(n_diag, 1)

            with dve.Fori(0, DEPTH) as l:
                for k in range(1, KT):
                    dve.drain()
                    dve.wait_ge(n_sq, l * KT + k + 1)
                    dve.tensor_tensor(tmp[:], tmp[:], wide[k % 2][:], ALU.add).then_inc(n_add, 1)
                dve.wait_ge(n_mm, l + 1)
                dve.tensor_scalar(stat[:, 0:NT], bank(2, NT), 1.0 / D_MODEL, EPS, ALU.mult, ALU.add).then_inc(n_ms, 1)
                dve.wait_ge(vec_t, l + 1)
                dve.tensor_copy(vec[:], bank(0, NV))
                dve.tensor_scalar(half_vec[:], bank(0, NV), 0.5, None, ALU.mult)
                dve.tensor_scalar(qk_gain[:, 0:AH], qk_gain[:, 0:AH], AD ** -0.5, None, ALU.mult)
                diagonals(l * 2)
                def modulation(first, count, src):
                    dve.tensor_tensor(mod[:, first:first + count], bank(src, 2 * count, 32).rearrange("p (k c) -> p k c", c=2),
                                      over(vec[:, V_BMOD + first:V_BMOD + first + count], 2), ALU.add)
                dve.wait_ge(mod_col, l * 2 + 1)
                modulation(0, 16, 1)
                dve.drain()
                dve.scalar_tensor_tensor(gain[:], mod[:, 8:16], 1.0, over(vec[:, 0:KT], 2), ALU.add, ALU.mult)
                dve.drain()
                dve.wait_ge(n_row, l * 2 + 1)

                def scale_block(k):
                    for c, (lo, hi) in enumerate(((0, SAMPLE), (SAMPLE, T))):
                        last = dve.scalar_tensor_tensor(wide[k % 2][:, lo:hi], x_sb[:, k, lo:hi], gain[:, k, c:c + 1], row_bc[:, lo:hi], ALU.mult, ALU.mult)
                    last.then_inc(n_t, 1)
                scale_block(0)
                for k in range(KT):
                    dve.drain()
                    if k + 1 < KT:
                        scale_block(k + 1)
                    if k == 5:
                        dve.wait_ge(mod_col, l * 2 + 2)
                    dve.wait_ge(n_h, l * KT + k + 1)
                    for c, (lo, hi) in enumerate(((0, SAMPLE), (SAMPLE, T))):
                        dve.scalar_tensor_tensor(h_lo[:, k, lo:hi], wide[k % 2][:, lo:hi], mod[:, k, c:c + 1], h_hi[:, k, lo:hi].bitcast(F32), ALU.add, ALU.subtract)
                dve.wait_ge(mod_col, l * 2 + 2)
                modulation(16, 8, 2)
                dve.drain()
                dve.tensor_scalar(half_gate[:], mod[:, 16:24], 0.5, None, ALU.mult)
                dve.wait_ge(coef_e, l + 1)
                dve.tensor_scalar(coef[:], coef[:], -1.0, None, ALU.mult)
                barrier(dve, l, 0)

                for b in range(2):
                    for c in (0, SAMPLE + 1, T + 2):
                        dve.memset(conv_in[b][:, c:c + 1], 0.0)
                split_group(dve, l, 0, 0, 0, KT)
                split_group(dve, l, 1, 1, 0, KT)
                base, stored, conv, th = G_PROJ, 0, 0, 0
                for kind, pairs, col, blk0 in PROJ_RUNS:
                    def body(n, p, m, j, kind=kind, st=stored, cv=conv, tq=th):
                        for b in range(2):
                            if kind.startswith("conv"):
                                v0 = V_GCONV if kind == "conv_gdn" else V_SCONV
                                tap = lambda w: half_vec[:, one(j * 2 + (v0 + 12 * w + b))]
                                bias = half_vec[:, one(j * 2 + (V_SBIAS + b))] if kind == "conv_ssm" else 0.0
                                dve.wait_ge(acc_free[b], l * NG + n + 2)
                                out = conv_out[b][:, 0:T + 1]
                                dve.tensor_scalar(out, conv_in[b][:, 1:T + 2], tap(1), bias, ALU.mult, ALU.add)
                                dve.drain()
                                dve.scalar_tensor_tensor(out, conv_in[b][:, 0:T + 1], tap(0), out, ALU.mult, ALU.add)
                                dve.drain()
                                dve.scalar_tensor_tensor(out, conv_in[b][:, 2:T + 3], tap(2), out, ALU.mult, ALU.add).then_inc(conv_mid[b], 1)
                                dve.wait_ge(th_ready[b], l * 20 + j + (tq + 1))
                                dve.scalar_tensor_tensor(leave[b][:, 0:T + 1], leave[b][:, 0:T + 1], 1.0, out, ALU.add, ALU.mult).then_inc(leave_ready[b], 1)
                            elif kind == "silu":
                                dve.wait_ge(th_ready[b], l * 20 + j + (tq + 1))
                                dve.scalar_tensor_tensor(thirds(leave[b][:, 0:T]), thirds(leave[b][:, 0:T]), 1.0, acc(b), ALU.add, ALU.mult).then_inc(leave_ready[b], 1)
                                dve.drain().then_inc(acc_free[b], 1)
                        if isinstance(n, int) and n + 2 == 11:
                            dve.wait_ge(dt_loaded, l * 16 + 16)
                        if not (isinstance(n, int) and n + 2 >= G_SSM):
                            split_group(dve, l, n + 2, p, m + 1, KT)
                    if pairs == 1:
                        for j in range(2):
                            body(base + j, j, base // 2, j)
                    elif kind == "tanh":
                        groups(dve, base, 2 * pairs - 2, body)
                        for j in range(2):
                            body(base + 2 * pairs - 2 + j, j, base // 2 + pairs - 1, 2 * pairs - 2 + j)
                    else:
                        groups(dve, base, 2 * pairs, body)
                    stored += 1 if kind == "kv_small" else 2 * pairs
                    conv += 2 * pairs if kind.startswith("conv") else 0
                    th += 2 * pairs if kind.startswith("conv") or kind == "silu" else 0
                    base += 2 * pairs
                barrier(dve, l, 1)

                dve.wait_ge(decay_prod, l * 2 + 1)
                D = {k: v[:] for k, v in dec.items()}
                pre_ps = bank(0, 432).rearrange("p (t c) -> p t c", c=48)
                dve.tensor_copy(D["pre"][:, :, 0:8], pre_ps[:, :, 0:8])
                dve.tensor_tensor(D["pre"][:, :, 8:48], pre_ps[:, :, 8:48], again(rows[:, 40:80], NT), ALU.add)
                dve.drain()
                dve.tensor_scalar(D["neg"], D["pre"], -1.0, None, ALU.mult)
                dve.tensor_scalar(D["low"], D["pre"], 0.0, None, ALU.min)
                dve.drain()
                dve.tensor_tensor(D["neg"], D["neg"], D["pre"], ALU.min).then_inc(decay_term, 1)
                dve.wait_ge(decay_exp, l * 2 + 1)
                dve.tensor_scalar(D["u"], D["e_abs"], 2.0, None, ALU.add)
                dve.drain()
                dve.reciprocal(D["u"], D["u"])
                dve.drain()
                dve.tensor_tensor(D["s"], D["u"], D["e_abs"], ALU.mult)
                dve.drain()
                dve.tensor_tensor(D["s2"], D["s"], D["s"], ALU.mult)
                dve.drain()
                dve.tensor_scalar(D["poly"], D["s2"], 1.0 / 17.0, None, ALU.mult)
                for c in (15, 13, 11, 9, 7, 5, 3):
                    dve.drain()
                    dve.scalar_tensor_tensor(D["poly"], D["poly"], 1.0 / c, D["s2"], ALU.add, ALU.mult)
                dve.drain()
                dve.scalar_tensor_tensor(D["poly"], D["poly"], 1.0, D["s"], ALU.add, ALU.mult)
                dve.tensor_scalar(D["u"], D["pre"], 0.0, None, ALU.max)
                dve.drain()
                dve.scalar_tensor_tensor(D["soft"], D["poly"], 2.0, D["u"], ALU.mult, ALU.add)
                dve.tensor_scalar(D["s"], D["e_abs"], 1.0, None, ALU.add)
                dve.drain()
                dve.reciprocal(D["s"], D["s"])
                dve.drain()
                dve.tensor_tensor(beta[:].rearrange("p t d h -> p t (d h)"), D["e_low"][:, :, 0:8], D["s"][:, :, 0:8], ALU.mult)
                dve.tensor_copy(dt_[:].rearrange("p t d h -> p t (d h)"), D["soft"][:, :, 16:48])
                for d in range(2):
                    dve.tensor_tensor(logd[:, :, d, 0:4], D["soft"][:, :, 8 + 4 * d:12 + 4 * d], again(coef[:, d, 0:4], NT), ALU.mult)
                    last = dve.tensor_tensor(logd[:, :, d, 4:20], D["soft"][:, :, 16 + 16 * d:32 + 16 * d], again(coef[:, d, 4:20], NT), ALU.mult)
                last.then_inc(decay_term, 1)
                dve.wait_ge(decay_prod, l * 2 + 2)
                for d in range(2):
                    dve.tensor_copy(cum[:, d].rearrange("p t h -> p (t h)"), bank(1 + d, 180))
                    dve.tensor_copy(tot[:, d].rearrange("p t h -> p (t h)"), bank(3 + d, 180))
                dve.drain()
                dve.tensor_tensor(rest[:], tot[:], cum[:], ALU.subtract).then_inc(decay_term, 1)
                dve.wait_ge(decay_exp, l * 2 + 2)
                for d in range(2):
                    dve.tensor_scalar(neg_e[:, d], e_cum[:, d, :, 0:4], -1.0, None, ALU.mult)
                    dve.tensor_tensor(dt_rest[:, d], dt_[:, :, d], e_rest[:, d, :, 4:20], ALU.mult)
                barrier(dve, l, 2)

                def build_after(t):
                    for half in range(2):
                        hs = slice(8 * half, 8 * half + 8)
                        dve.tensor_tensor(after[:, hs], again(cst[:, C_STRICT], 8), over(logd[:, t, 0, 4 + 8 * half:12 + 8 * half], P), ALU.mult).then_inc(sp_fwd, 1)

                def y_sum(t):
                    dve.wait_ge(sp_y, l * NT + t + 1)
                    dve.tensor_tensor(y_acc[:, t], PSUM[:, 0:D_MODEL], d_x[:].rearrange("p h q -> p (h q)"), ALU.add).then_inc(sp_yd, 1)

                def ssm_prep(t, p, i):
                    n = l * NT + t
                    last_tile = isinstance(t, int) and t == NT - 1
                    dve.wait_ge(transposed, nth(l, t, 0, 5) + 1)
                    for d in range(2):
                        dve.tensor_tensor(cb[p][:, d], bank(7, 256).rearrange("p (g l) -> p g l", l=P), again(cst[:, C_TRI + d], SG), ALU.mult).then_inc(sp_fwd, 1)
                    if not last_tile:
                        dve.wait_ge(sp_prod, n * 2 + 2)
                        build_after(t + 1)
                    if not (isinstance(t, int) and t == 0):
                        y_sum(t - 1)
                    xh = xt[p][:, 0:D_MODEL].rearrange("p (h q) -> p h q", q=SP_)
                    dve.drain()
                    dve.wait_ge(out_ready, nth(l, t, 0, 2) + 1)
                    dve.tensor_tensor(x_dt[0][:], xh, over(dt_[:, t, 0], SP_), ALU.mult)
                    dve.tensor_tensor(d_x[:], xh, over(rows[:, 80:96], SP_), ALU.mult)
                    for g in range(SG):
                        dve.wait_ge(sp_e, n * 2 + 1 + g)
                        dve.tensor_tensor(w_f[:, 8 * g:8 * g + 8], e_ssm[:, 8 * g:8 * g + 8], again(cb[p][:, 0, g], 8), ALU.mult).then_inc(sp_fwd, 1)
                build_after(0)
                ssm_prep(0, 0, 0)
                ssm_prep(1, 1, 0)
                with dve.Fori(0, 3) as i:
                    for p in range(2):
                        ssm_prep(i * 2 + (p + 2), p, i + 1)
                ssm_prep(NT - 1, 0, 4)
                y_sum(NT - 1)
                barrier(dve, l, 3)

                def ssm_step(t, p, i):
                    n = l * NT + t
                    if isinstance(t, int):
                        for d in range(2):
                            dve.memset(s_ssm[d][:], 0.0).then_inc(state[d], 1)
                    for d in range(2):
                        tt = t if isinstance(t, int) or d == 0 else (NS - 1) - t
                        dve.wait_ge(ssm_prod[d], l * 20 + t * 2 + 2)
                        dve.sem_inc(waits_held, 1)
                        dve.tensor_tensor(y_tmp[d][:].rearrange("p (h q) -> p h q", q=SP_), PSUM[:, 2048 * d:2048 * d + 1024].rearrange("p (h q) -> p h q", q=SP_),
                                          over(e_cum[:, d, tt, 4:20], SP_), ALU.mult)
                        dve.wait_ge(ssm_prod[d], l * 20 + t * 2 + 3)
                        dve.sem_inc(waits_held, 1)
                        dve.wait_ge(ssm_side[d], n * 2 + 2)
                        dve.tensor_tensor(s_ssm[d][:], s_kept[d][:], PSUM[:, 2048 * d + 1024:2048 * d + 2048], ALU.add).then_inc(state[d], 1)
                        dve.drain()
                        dve.tensor_tensor(y_acc[:, tt], y_acc[:, tt], y_tmp[d][:], ALU.add)
                tiles(dve, ssm_step)
                barrier(dve, l, 4)

                def gate_y(t, p, i):
                    dve.wait_ge(tile_in[p], loaded(l, p, i, 1))
                    dve.wait_ge(transposed, nth(l, t, 1, 5) + 1)
                    dve.tensor_tensor(yz[p][:], PSUM[:, 2048 * p:2048 * p + 1024].rearrange("p (k t) -> p k t", t=P), z_c[p][:], ALU.mult).then_inc(gated, 1)

                def ssm_post(t, p, i):
                    n = l * NT + t
                    if not is_tile(t, NT - 1):
                        gate_y(*next_tile(t, p, i))
                    dve.wait_ge(sums_made, nth(l, t, 0, 4) + 1)
                    dve.tensor_copy(stat[:, one(t)], bank(2, 1)).then_inc(y_ss_read, 1)
                    dve.wait_ge(hi_made, nth(l, t, 0, 3) + 1)
                    dve.tensor_tensor(b_lo[:, :, cols(t)], yzw[p][:], b_hi[:, :, cols(t)].bitcast(F32), ALU.subtract).then_inc(lo_made, 1)
                gate_y(0, 0, 0)
                overlapped(dve, ssm_post)
                dve.drain()
                dve.tensor_scalar(stat[:, 0:NT], stat[:, 0:NT], 1.0 / D_MODEL, 4 * EPS, ALU.mult, ALU.add).then_inc(n_ms, 1)
                diagonals(l * 2 + 1)
                barrier(dve, l, 5)

                def branch(base, kt, merge, before=None):
                    for j in range(2):
                        split_group(dve, l, base + j, j, base // 2, kt)
                    if before:
                        before()
                    for j in range(4):
                        n, p = base + j, j % 2
                        for b in range(2):
                            dve.drain()
                            dve.wait_ge(acc_ready[b], acc_done(l, n, b))
                            dve.wait_ge(wide_in[b], l * 256 + 16 * (n - G_SSM) + 16)
                            merge(2 * j + b, b)
                        if j < 2:
                            split_group(dve, l, n + 2, p, base // 2 + 1, kt)

                def merge_first(blk, b):
                    dve.tensor_tensor(thirds(tmp[:]), acc(b), thirds(row_bc[:]), ALU.mult)
                    dve.drain().then_inc(acc_free[b], 1)
                    dve.scalar_tensor_tensor(merged[:, blk], wide[b][:], 1.0, tmp[:], ALU.add, ALU.mult).then_inc(wide_free[b], 1)

                def merge_more(blk, b):
                    dve.scalar_tensor_tensor(thirds(tmp[:]), thirds(wide[b][:]), 1.0, acc(b), ALU.add, ALU.mult)
                    dve.drain().then_inc(acc_free[b], 1)
                    dve.tensor_tensor(merged[:, blk], merged[:, blk], tmp[:], ALU.add).then_inc(wide_free[b], 1)

                def merge_out(blk, b):
                    w = thirds(wide[b][:])
                    dve.scalar_tensor_tensor(w[:, 0:2], acc(b)[:, 0:2], half_gate[:, blk, 0:1], w[:, 0:2], ALU.mult, ALU.add)
                    for c, (lo, hi) in enumerate(((0, THIRD - PROMPT), (THIRD - PROMPT, THIRD))):
                        last = dve.scalar_tensor_tensor(w[:, 2, lo:hi], acc(b)[:, 2, lo:hi], half_gate[:, blk, c:c + 1], w[:, 2, lo:hi], ALU.mult, ALU.add)
                    last.then_inc(x_new, 1)
                    dve.drain().then_inc(acc_free[b], 1)
                branch(G_SSM, 8, merge_first)
                barrier(dve, l, 6)

                def by_head(x):
                    return x.rearrange("p (h d) -> p h d", d=GD)

                def sums_next(t):
                    dve.drain()
                    dve.wait_ge(squared, nth(l, t, 1, 4) + 1)
                    dve.tensor_reduce(stat[:, 0:8], g_sq[:], AX_X, ALU.add)
                    dve.drain()
                    dve.tensor_scalar(stat[:, 0:4], stat[:, 0:4], EPS, float(GD), ALU.add, ALU.mult)
                    dve.tensor_scalar(stat[:, 4:8], stat[:, 4:8], EPS, None, ALU.add).then_inc(sums_made, 1)

                def normalise_next(t, p, i):
                    dve.wait_ge(inv_rms, nth(l, t, 0, 3) + 1)
                    if not is_tile(t, 0):
                        dve.wait_ge(gp_tt, l * NT + t)
                    dve.wait_ge(tile_stored, nth(l, t, 1, 2) * 16 - 16)
                    dve.tensor_tensor(q_n[:], by_head(bank(0)), over(stat[:, 8:12], GD), ALU.mult)
                    dve.tensor_tensor(by_head(g_out[p][:, K_K]), by_head(bank(1)), over(stat[:, 12:16], GD), ALU.mult).then_inc(scaled, 1)

                def gdn_prep(t, p, i):
                    if not is_tile(t, NT - 1):
                        sums_next(t + 1)
                    dve.wait_ge(gp_k, l * NT + t + 1)
                    for d in range(2):
                        last = dve.tensor_tensor(by_head(g_out[p][:, K_KK[d]]), by_head(bank(5)), over(beta[:, t, d], GD), ALU.mult)
                    last.then_inc(gp_kk, 1)
                    if not is_tile(t, NT - 1):
                        normalise_next(*next_tile(t, p, i))
                sums_next(0)
                normalise_next(0, 0, 0)
                overlapped(dve, gdn_prep)
                barrier(dve, l, 7)

                for d in range(2):
                    dve.wait_ge(state_in[d], l * 32 + 32)
                    dve.sem_inc(waits_held, 1)
                    dve.drain().then_inc(state[d], 1)
                dve.wait_ge(o_zero, l + 1)
                dve.sem_inc(waits_held, 1)

                def heads(x):
                    return x.rearrange("p (h t) -> p h t", t=P)

                def decay_columns(t):
                    for d in range(2):
                        dve.tensor_copy(gd[d]["col"][:], over(logd[:, scan_tile(t, d), d, 0:4], P)).then_inc(g_pre[d], 1)

                def decay_exponents(t):
                    for d in range(2):
                        tt = scan_tile(t, d)
                        if not is_tile(t, 0):
                            dve.wait_ge(g_a[d], (l * NT + t) * 2)
                        dve.wait_ge(g_row[d], (l * NT + t) * 2 + 1)
                        for h in range(GH):
                            last = dve.tensor_scalar(gd[d]["E"][:, h], bank(4 * d + 3, P, h * P), cum[:, d, tt, h:h + 1], 0.0, ALU.subtract, ALU.min)
                        last.then_inc(g_pre[d], 1)

                def small_inverse(t, p, d):
                    g = gd[d]
                    dve.wait_ge(g_row[d], (l * NT + t) * 2 + 2)
                    dve.tensor_tensor(g["Y"][p][:], g["A"][p][:], again(cst[:, C_LV + 7 * (1 - d)], GH), ALU.mult)
                    dve.tensor_tensor(g["X"][p][:], heads(bank(4 * d + 3)), again(cst[:, C_LV + 7 * d], GH), ALU.mult)
                    dve.drain()
                    dve.tensor_tensor(g["Y"][p][:], g["Y"][p][:], again(ident, GH), ALU.add)
                    dve.tensor_tensor(g["X"][p][:], g["X"][p][:], again(ident, GH), ALU.add).then_inc(g_pre[d], 1)

                def gdn_step(t, p, i):
                    n = l * NT + t
                    more = not is_tile(t, NT - 1)
                    if not more:
                        for d in range(2):
                            dve.memset(gd[d]["S"][:], 0.0).then_inc(state[d], 1)
                    for lev in range(1, 7):
                        for d in range(2):
                            dve.wait_ge(g_level[d], n * 12 + 2 * lev - 1)
                            dve.tensor_tensor(gd[d]["T"][:], heads(bank(4 * d)), again(cst[:, C_LV + 7 * d + lev], GH), ALU.mult).then_inc(g_tm[d], 1)
                        if lev == 1:
                            for d in range(2):
                                dve.wait_ge(g_from_s[d], n * 2 + 1)
                                dve.sem_inc(waits_held, 1)
                                dve.tensor_tensor(gd[d]["R0"][:], heads(bank(4 * d + 3)), over(neg_e[:, d, scan_tile(t, d)], P), ALU.mult)
                            dve.drain()
                            for d in range(2):
                                dve.tensor_tensor(gd[d]["R"][:], gd[d]["R0"][:], heads(g_t[d][p][:, K_V - d]), ALU.add).then_inc(g_used[d], 1)
                            dve.drain()
                        if lev == 2:
                            for d in range(2):
                                dve.wait_ge(g_from_s[d], n * 2 + 2)
                                dve.sem_inc(waits_held, 1)
                                dve.tensor_tensor(gd[d]["R0"][:], heads(bank(4 * d + 3)), over(e_cum[:, d, scan_tile(t, d), 0:4], P), ALU.mult).then_inc(g_used[d], 1)
                            if more:
                                decay_columns(t + 1)
                            for d in range(2):
                                tt = scan_tile(t, d)
                                dve.drain()
                                dve.tensor_tensor(o_acc[:, tt], o_acc[:, tt], gd[d]["R0"][:].rearrange("p h t -> p (h t)"), ALU.add)
                        if lev == 3 and more:
                            decay_exponents(t + 1)
                        if lev >= 5 and more:
                            small_inverse(t + 1, 1 - p, lev - 5)
                    for d in range(2):
                        dve.wait_ge(g_v[d], n + 1)
                        dve.tensor_tensor(gd[d]["V"][:], heads(bank(4 * d + 1)), over(beta[:, scan_tile(t, d), d], P), ALU.mult).then_inc(g_vc[d], 1)
                    for d in range(2):
                        g = gd[d]
                        dve.wait_ge(g_side[d], n * 2 + 2)
                        dve.wait_ge(g_from_v[d], n * 2 + 1)
                        dve.tensor_tensor(g["S"][:], g["SK"][:], heads(bank(4 * d)), ALU.add).then_inc(state[d], 1)
                    for d in range(2):
                        tt = scan_tile(t, d)
                        dve.drain()
                        dve.wait_ge(g_from_v[d], n * 2 + 2)
                        dve.tensor_tensor(o_acc[:, tt], o_acc[:, tt], bank(4 * d + 2), ALU.add).then_inc(g_step[d], 1)
                decay_columns(0)
                decay_exponents(0)
                for d in range(2):
                    small_inverse(0, 0, d)
                overlapped(dve, gdn_step)
                barrier(dve, l, 8)

                def sums_o(t):
                    dve.wait_ge(squared, nth(l, t, 2, 4) + 1)
                    dve.tensor_reduce(stat[:, 0:4], o_sq[:], AX_X, ALU.add)
                    dve.drain()
                    dve.tensor_scalar(stat[:, 0:4], stat[:, 0:4], 1.0 / GD, EPS, ALU.mult, ALU.add).then_inc(sums_made, 1)

                def scale_o(t, p, i):
                    dve.wait_ge(inv_rms, nth(l, t, 1, 3) + 1)
                    dve.tensor_tensor(o_st[p][:], o_acc[:, t].rearrange("p (h d) -> p h d", d=GD), over(stat[:, 8:12], GD), ALU.mult).then_inc(scaled, 1)

                def gdn_post(t, p, i):
                    dve.drain()
                    if not is_tile(t, NT - 1):
                        sums_o(t + 1)
                    dve.wait_ge(tile_in[p], loaded(l, p, i, 3))
                    dve.wait_ge(transposed, nth(l, t, 3, 5) + 1)
                    dve.scalar_tensor_tensor(o_z[:], heads(bank(p)), half_vec[:, V_GNORM:V_GNORM + 1], z_a[p][:], ALU.mult, ALU.mult).then_inc(gated, 1)
                    if not is_tile(t, NT - 1):
                        scale_o(*next_tile(t, p, i))
                    dve.wait_ge(hi_made, nth(l, t, 1, 3) + 1)
                    dve.tensor_tensor(b_lo[:, 0:4, cols(t)], o_z[:], b_hi[:, 0:4, cols(t)].bitcast(F32), ALU.subtract).then_inc(lo_made, 1)
                sums_o(0)
                scale_o(0, 0, 0)
                overlapped(dve, gdn_post)
                barrier(dve, l, 9)
                branch(G_GDN, 4, merge_more)
                barrier(dve, l, 10)

                def split_k(src):
                    dve.tensor_copy(k_hh[:, :, 0:AD], src)
                    dve.tensor_copy(k_hh[:, :, AD:P], src)
                    dve.drain()
                    dve.tensor_tensor(k_ll[:, :, 0:AD], src, k_hh[:, :, 0:AD].bitcast(F32), ALU.subtract)
                    return dve.tensor_tensor(k_ll[:, :, AD:P], src, k_hh[:, :, 0:AD].bitcast(F32), ALU.subtract)

                def place_k(n, t):
                    dve.wait_ge(a_st, n + 1)
                    dve.tensor_copy(k_hi[:, :, cols(t)], bank(4)[:, 0:256].rearrange("p (g t) -> p g t", t=P))
                    dve.tensor_copy(k_lo[:, :, cols(t)], bank(4)[:, 256:512].rearrange("p (g t) -> p g t", t=P)).then_inc(a_k, 1)

                def head_sums(t):
                    dve.wait_ge(squared, nth(l, t, 3, 4) + 1)
                    dve.tensor_reduce(stat[:, 0:10], a_sq[:], AX_X, ALU.add)
                    dve.drain()
                    dve.tensor_scalar(stat[:, 0:10], stat[:, 0:10], 1.0 / AD, EPS, ALU.mult, ALU.add).then_inc(sums_made, 1)

                def attn_prep(t, p, i):
                    n, n1 = l * NT + t, l * (NT + 1) + t
                    ps = PSUM[:, 0:640].rearrange("p (h d) -> p h d", d=AD)
                    dve.drain()
                    dve.wait_ge(inv_rms, nth(l, t, 2, 3) + 1)
                    dve.wait_ge(a_v, n + 1)
                    dve.tensor_tensor(qk[:], ps, over(stat[:, 16:26], AD), ALU.mult)
                    dve.drain()
                    dve.tensor_tensor(qk[:], qk[:], qk_gain[:], ALU.mult).then_inc(scaled, 1)
                    dve.drain()
                    dve.tensor_tensor(qk_c[:], qk[:], again(rope[:, t, 0], 10), ALU.mult)
                    if not is_tile(t, NT - 1):
                        head_sums(t + 1)
                    if not is_tile(t, 0):
                        place_k(n1 - 1, t - 1)
                    dve.drain()
                    dve.wait_ge(a_sin, n + 1)
                    dve.tensor_tensor(qk[:], qk_c[:], qk_s[:], ALU.add).then_inc(qk_done, 1)
                    dve.drain()
                    dve.tensor_copy(q_hl[:, :, 0:AD], qk[:, 0:AH])
                    dve.drain()
                    dve.tensor_tensor(q_hl[:, :, AD:P], qk[:, 0:AH], q_hl[:, :, 0:AD].bitcast(F32), ALU.subtract)
                    split_k(qk[:, AH:10]).then_inc(a_split, 1)
                head_sums(0)
                overlapped(dve, attn_prep)
                place_k(l * (NT + 1) + NT - 1, NT - 1)
                dve.wait_ge(past_in, l * 32 + 32)
                split_k(ain[1][:, 0].rearrange("p (g d) -> p g d", d=AD)).then_inc(a_split, 1)
                place_k(l * (NT + 1) + NT, NT)
                barrier(dve, l, 11)

                def head_max(t, u, h):
                    nk = 1 if isinstance(t, int) and t == NS else 9
                    dve.wait_ge(at_s, (l * NT + t) * AH + h + 1)
                    dve.tensor_reduce(row_max[:, u, h:h + 1], PSUM[:, 1536 * (h % 2):1536 * (h % 2) + nk * P], AX_X, ALU.max, negate=True).then_inc(at_m, 1)

                def attn(t, u, nk):
                    n = l * NT + t
                    for h in range(AH):
                        if h + 1 < AH:
                            head_max(t, u, h + 1)
                        elif nk > 1:
                            head_max(t + 1, 1 - u, 0)
                        dve.wait_ge(at_t[0], n * AH + h + 1)
                        w = min(nk, 4)
                        dve.tensor_copy(prob_t[h % 2][:, 0:w], bank(6, w * P).rearrange("p (j t) -> p j t", t=P)).then_inc(at_c[0], 1)
                    dve.reciprocal(inv_sum[:], row_sum[:, u])
                    dve.drain()
                    dve.tensor_scalar(inv_sum[:], inv_sum[:], 0.5, None, ALU.mult)
                    dve.drain()
                    dve.wait_ge(at_v, n * AH + AH)
                    dve.tensor_tensor(o_att[:], bank(7).rearrange("p (h d) -> p h d", d=AD), over(inv_sum[:], AD), ALU.mult).then_inc(o_norm, 1)
                    dve.wait_ge(zb_in, n * 16 + 16)
                    dve.wait_ge(o_tr, n + 1)
                    dve.tensor_tensor(o_bz[:], heads(bank(6)), z_b[:], ALU.mult).then_inc(gated, 1)
                    dve.wait_ge(hi_made, nth(l, t, 2, 3) + 1)
                    dve.tensor_tensor(b_lo[:, 0:4, cols(t)], o_bz[:], b_hi[:, 0:4, cols(t)].bitcast(F32), ALU.subtract).then_inc(lo_made, 1)
                head_max(0, 0, 0)
                with dve.Fori(0, 3) as i:
                    for u in range(2):
                        attn(i * 2 + u, u, 9)
                attn(6, 0, 9)
                attn(7, 1, 9)
                attn(NS, 0, 1)
                barrier(dve, l, 12)
                branch(G_ATT, 4, merge_more)
                barrier(dve, l, 13)

                def split_merged():
                    for k in range(KT):
                        dve.wait_ge(m_hi, l * KT + k + 1)
                        dve.tensor_tensor(b_lo[:, k], merged[:, k], b_hi[:, k].bitcast(F32), ALU.subtract).then_inc(m_lo, 1)
                branch(G_OUT, 8, merge_out, split_merged)
                barrier(dve, l, 14)

            dve.wait_ge(f_in, 16)
            for t in range(NT):
                dve.wait_ge(f_sq, t + 1)
                dve.tensor_scalar(stat[:, 25:26], stat[:, 16 + t:17 + t], 1.0 / D_MODEL, EPS, ALU.mult, ALU.add).then_inc(f_ms, 1)
                dve.wait_ge(f_r, t + 1)
                if t >= 2:
                    dve.wait_ge(f_out[t % 2], 16 * (t // 2))
                dve.scalar_tensor_tensor(x_tok[t % 2][:], PSUM[:, 1024 * (t % 2):1024 * (t % 2) + 1024], r_tok[:, t:t + 1], f_gain[:], ALU.mult, ALU.mult).then_inc(f_y, 1)


_INS = ["x_prompt", "x_sample", "cache_k", "cache_v", "state_gdn", "state_ssm", "c", "c_ctx", "norm_w", "w_mod",
        "b_mod", "w_in", "gdn_conv_w", "gdn_a_log", "gdn_dt_bias", "gdn_norm_w", "attn_q_norm", "attn_k_norm",
        "ssm_conv_w", "ssm_conv_b", "ssm_a_log", "ssm_dt_bias", "ssm_d", "ssm_norm_w", "w_branch_a", "w_branch_b",
        "w_branch_c", "w_out", "final_norm_w"]
_OUTS = [("y_prompt", (1, PROMPT, D_MODEL)), ("y_sample", (1, SAMPLE, D_MODEL)),
         ("cache_k", (1, DEPTH, PROMPT, KVH, AD)), ("cache_v", (1, DEPTH, PROMPT, KVH, AD)),
         ("state_gdn", (1, DEPTH, 2, GH, GD, GD)), ("state_ssm", (1, DEPTH, 2, SH, SP_, SN))]


def kernel(**inputs):
    import numpy as _np
    import concourse.bacc as _bacc
    from concourse.bass_utils import run_bass_kernel_spmd as _run

    nc = _bacc.Bacc("TRN2", target_bir_lowering=False, num_devices=1)
    arrays, ins, outs = {}, {}, {}
    for name in _INS:
        arrays[f"in_{name}"] = _np.ascontiguousarray(inputs[name])
        ins[name] = nc.dram_tensor(f"in_{name}", arrays[f"in_{name}"].shape, F32, kind="ExternalInput").ap()
    tables = []
    for name, a in zip(("table", "rope_table"), constants()):
        arrays[name] = a
        tables.append(nc.dram_tensor(name, a.shape, F32, kind="ExternalInput").ap())
    for name, shape in _OUTS:
        outs[name] = nc.dram_tensor(f"out_{name}", shape, F32, kind="ExternalOutput").ap()
    backbone_kernel(nc, ins, outs, *tables)
    r = _run(nc, [arrays], core_ids=[0])
    return tuple(r.results[0][f"out_{name}"] for name, _ in _OUTS)
```
